# Optimizing a Trainium2 kernel written in Bass

```python
import jax, jax.numpy as jnp
from jax import lax
import numpy as np

D_MODEL = 1024
BATCH = 1
SEQ = 256
DEPTH = 2
DEC_BATCH = 1
DEC_SEQ = 1024
PAST_LEN = 256

GRID_W = 64
N_HEADS = 8
QK_NOPE = 64
QK_ROPE = 32
QK_DIM = QK_NOPE + QK_ROPE
V_HEAD = 64
Q_LORA = 384
KV_LORA = 256
CONV_CH = 512
CONV_K = 3
FNET_GROUPS = 4
N_EXPERTS = 16
EXPERT_FF = 512
CAPACITY_FACTOR = 2
ROPE_THETA = 10000.0
EPS = 1e-6
Q_BLOCK = 128
IN0_COLS = Q_LORA + KV_LORA + QK_ROPE + 3 * CONV_CH
MIX0_OUT = N_HEADS * V_HEAD + CONV_CH

kernel_name = 'hybrid_mla_shortconv_fnet_ec_diffusion_step'

def rmsnorm(x, g):
    xf = x.astype(jnp.float32)
    y = xf * lax.rsqrt(jnp.mean(xf * xf, axis=-1, keepdims=True) + EPS)
    return (y * g.astype(jnp.float32)).astype(x.dtype)

def modulation(cond, w_mod, b_mod):
    m = jnp.einsum('bd,df->bf', jax.nn.silu(cond), w_mod) + b_mod
    return jnp.split(m[:, None, :], 6, axis=-1)

def axial_rope(n_tokens):
    rows = n_tokens // GRID_W
    row = jnp.repeat(jnp.arange(rows, dtype=jnp.float32), GRID_W)
    col = jnp.tile(jnp.arange(GRID_W, dtype=jnp.float32), rows)
    axis_dim = QK_ROPE // 2
    inv_freq = ROPE_THETA ** (-jnp.arange(0, axis_dim, 2, dtype=jnp.float32) / axis_dim)
    ang = jnp.concatenate([row[:, None] * inv_freq, col[:, None] * inv_freq], axis=-1)
    return jnp.cos(ang), jnp.sin(ang)

def rotate_rope_part(t, cos, sin):
    nope, pe = t[..., :QK_NOPE], t[..., QK_NOPE:]
    pe = pe.reshape(pe.shape[:-1] + (QK_ROPE // 2, 2))
    x1, x2 = pe[..., 0], pe[..., 1]
    c = cos[None, :, None, :].astype(t.dtype)
    s = sin[None, :, None, :].astype(t.dtype)
    pe = jnp.stack([x1 * c - x2 * s, x1 * s + x2 * c], axis=-1).reshape(nope.shape[:-1] + (QK_ROPE,))
    return jnp.concatenate([nope, pe], axis=-1)

def softmax_attention(q, k, v):
    b, nq, h, dk = q.shape
    scale = dk ** -0.5
    q_blocks = q.reshape(b, nq // Q_BLOCK, Q_BLOCK, h, dk).transpose(1, 0, 2, 3, 4)

    def one_block(qb):
        s = jnp.einsum('bqhd,bkhd->bhqk', qb, k, preferred_element_type=jnp.float32) * scale
        p = jax.nn.softmax(s, axis=-1).astype(v.dtype)
        return jnp.einsum('bhqk,bkhd->bqhd', p, v)

    o = lax.map(one_block, q_blocks)
    return o.transpose(1, 0, 2, 3, 4).reshape(b, nq, h * v.shape[-1])

def mla_expand_kv(c_kv, k_rope, w_kv_up, k_norm):
    b, n, _ = c_kv.shape
    kv = jnp.einsum('bnr,rf->bnf', c_kv, w_kv_up).reshape(b, n, N_HEADS, QK_NOPE + V_HEAD)
    k_nope, v = kv[..., :QK_NOPE], kv[..., QK_NOPE:]
    k_pe = jnp.broadcast_to(k_rope[:, :, None, :], (b, n, N_HEADS, QK_ROPE))
    k = rmsnorm(jnp.concatenate([k_nope, k_pe], axis=-1), k_norm)
    return k, v

def short_conv(u, w):
    pad = CONV_K // 2
    return lax.conv_general_dilated(u, w[:, None, :].astype(u.dtype), window_strides=(1,),
                                    padding=((pad, pad),), dimension_numbers=('NWC', 'WIO', 'NWC'),
                                    feature_group_count=u.shape[-1])

def attn_conv_mixer(h, p, ctx_cache, rope):
    b, n, _ = h.shape
    proj = jnp.einsum('bnd,df->bnf', h, p['w_in'])
    cuts = [Q_LORA, Q_LORA + KV_LORA, Q_LORA + KV_LORA + QK_ROPE,
            Q_LORA + KV_LORA + QK_ROPE + CONV_CH, Q_LORA + KV_LORA + QK_ROPE + 2 * CONV_CH]
    c_q, c_kv, k_rope, gate_b, gate_c, u = jnp.split(proj, cuts, axis=-1)
    q = jnp.einsum('bnr,rf->bnf', rmsnorm(c_q, p['q_a_norm']), p['w_q_up']).reshape(b, n, N_HEADS, QK_DIM)
    q = rmsnorm(q, p['q_norm'])
    c_kv = rmsnorm(c_kv, p['kv_a_norm'])
    k, v = mla_expand_kv(c_kv, k_rope, p['w_kv_up'], p['k_norm'])
    if rope is not None:
        cos, sin = rope
        q = rotate_rope_part(q, cos, sin)
        k = rotate_rope_part(k, cos, sin)
        k_ctx, v_ctx = mla_expand_kv(ctx_cache[0], ctx_cache[1], p['w_kv_up'], p['k_norm'])
        k = jnp.concatenate([k_ctx, k], axis=1)
        v = jnp.concatenate([v_ctx, v], axis=1)
    attn = softmax_attention(q, k, v)
    conv = gate_b * short_conv(gate_c * u, p['conv_w'])
    out = jnp.einsum('bnf,fd->bnd', jnp.concatenate([attn, conv], axis=-1), p['w_o'])
    return out, (c_kv, k_rope)

def fourier_mixer(h, w_f):
    b, n, d = h.shape
    hg = h.astype(jnp.float32).reshape(b, n, FNET_GROUPS, d // FNET_GROUPS)
    f = jnp.fft.fftn(hg, axes=(1, 3), norm='ortho').real.reshape(b, n, d).astype(h.dtype)
    return jnp.einsum('bnd,de->bne', f, w_f)

def expert_choice_ffn(x, w_router, w_gate, w_up, w_down):
    b, n, d = x.shape
    t = x.reshape(b * n, d)
    cap = CAPACITY_FACTOR * (b * n) // N_EXPERTS
    aff = jax.nn.softmax(jnp.einsum('td,de->te', t, w_router).astype(jnp.float32), axis=-1)
    g, idx = lax.top_k(aff.T, cap)
    xe = t[idx]
    hid = jax.nn.silu(jnp.einsum('ecd,edf->ecf', xe, w_gate)) * jnp.einsum('ecd,edf->ecf', xe, w_up)
    ye = jnp.einsum('ecf,efd->ecd', hid, w_down) * g[..., None].astype(x.dtype)
    out = jnp.zeros_like(t).at[idx.reshape(-1)].add(ye.reshape(-1, d))
    return out.reshape(b, n, d)

def trunk(x, cond, layers, caches, rope):
    new_caches = []
    for l in range(DEPTH):
        p = layers[l]
        sh1, sc1, g1, sh2, sc2, g2 = modulation(cond, p['w_mod'], p['b_mod'])
        h = rmsnorm(x, p['norm1']) * (1 + sc1) + sh1
        if l % 2 == 0:
            mix, ctx_kv = attn_conv_mixer(h, p, caches[l], rope)
            new_caches.append(ctx_kv)
        else:
            mix = fourier_mixer(h, p['w_f'])
        x = x + g1 * mix
        h = rmsnorm(x, p['norm2']) * (1 + sc2) + sh2
        x = x + g2 * expert_choice_ffn(h, p['w_router'], p['w_gate'], p['w_up'], p['w_down'])
    return x, new_caches

def setup_inputs(seed: int = 0) -> dict:
    key = jax.random.key(seed)
    ks = iter(jax.random.split(key, 40))
    f32 = jnp.float32

    def nrm(shape, scale):
        return jax.random.normal(next(ks), shape, f32) * scale

    def gain(n):
        return 1.0 + 0.05 * jax.random.normal(next(ks), (n,), f32)

    inp = {}
    inp['x_prompt'] = nrm((BATCH, SEQ, D_MODEL), 1.0)
    inp['x_sample'] = nrm((DEC_BATCH, DEC_SEQ, D_MODEL), 1.0)
    inp['c'] = nrm((DEC_BATCH, D_MODEL), 1.0)
    inp['cache_c_kv_l0'] = nrm((DEC_BATCH, PAST_LEN, KV_LORA), 1.0)
    inp['cache_k_rope_l0'] = nrm((DEC_BATCH, PAST_LEN, QK_ROPE), 1.0)
    inp['c_ctx'] = nrm((D_MODEL,), 1.0)
    inp['norm1_l0'] = gain(D_MODEL)
    inp['norm2_l0'] = gain(D_MODEL)
    inp['w_mod_l0'] = nrm((D_MODEL, 6 * D_MODEL), D_MODEL ** -0.5)
    inp['b_mod_l0'] = nrm((6 * D_MODEL,), 0.02)
    inp['w_in_l0'] = nrm((D_MODEL, IN0_COLS), D_MODEL ** -0.5)
    inp['q_a_norm_l0'] = gain(Q_LORA)
    inp['w_q_up_l0'] = nrm((Q_LORA, N_HEADS * QK_DIM), Q_LORA ** -0.5)
    inp['q_norm_l0'] = gain(QK_DIM)
    inp['kv_a_norm_l0'] = gain(KV_LORA)
    inp['w_kv_up_l0'] = nrm((KV_LORA, N_HEADS * (QK_NOPE + V_HEAD)), KV_LORA ** -0.5)
    inp['k_norm_l0'] = gain(QK_DIM)
    inp['conv_w_l0'] = nrm((CONV_K, CONV_CH), CONV_K ** -0.5)
    inp['w_o_l0'] = nrm((MIX0_OUT, D_MODEL), MIX0_OUT ** -0.5)
    inp['w_router_l0'] = nrm((D_MODEL, N_EXPERTS), D_MODEL ** -0.5)
    inp['w_gate_l0'] = nrm((N_EXPERTS, D_MODEL, EXPERT_FF), D_MODEL ** -0.5)
    inp['w_up_l0'] = nrm((N_EXPERTS, D_MODEL, EXPERT_FF), D_MODEL ** -0.5)
    inp['w_down_l0'] = nrm((N_EXPERTS, EXPERT_FF, D_MODEL), EXPERT_FF ** -0.5)
    inp['norm1_l1'] = gain(D_MODEL)
    inp['norm2_l1'] = gain(D_MODEL)
    inp['w_mod_l1'] = nrm((D_MODEL, 6 * D_MODEL), D_MODEL ** -0.5)
    inp['b_mod_l1'] = nrm((6 * D_MODEL,), 0.02)
    inp['w_f_l1'] = nrm((D_MODEL, D_MODEL), D_MODEL ** -0.5)
    inp['w_router_l1'] = nrm((D_MODEL, N_EXPERTS), D_MODEL ** -0.5)
    inp['w_gate_l1'] = nrm((N_EXPERTS, D_MODEL, EXPERT_FF), D_MODEL ** -0.5)
    inp['w_up_l1'] = nrm((N_EXPERTS, D_MODEL, EXPERT_FF), D_MODEL ** -0.5)
    inp['w_down_l1'] = nrm((N_EXPERTS, EXPERT_FF, D_MODEL), EXPERT_FF ** -0.5)
    return inp

def reference(x_prompt, x_sample, c, cache_c_kv_l0, cache_k_rope_l0, c_ctx,
              norm1_l0, norm2_l0, w_mod_l0, b_mod_l0, w_in_l0, q_a_norm_l0, w_q_up_l0, q_norm_l0,
              kv_a_norm_l0, w_kv_up_l0, k_norm_l0, conv_w_l0, w_o_l0,
              w_router_l0, w_gate_l0, w_up_l0, w_down_l0,
              norm1_l1, norm2_l1, w_mod_l1, b_mod_l1, w_f_l1,
              w_router_l1, w_gate_l1, w_up_l1, w_down_l1):
    layers = [
        dict(norm1=norm1_l0, norm2=norm2_l0, w_mod=w_mod_l0, b_mod=b_mod_l0, w_in=w_in_l0,
             q_a_norm=q_a_norm_l0, w_q_up=w_q_up_l0, q_norm=q_norm_l0, kv_a_norm=kv_a_norm_l0,
             w_kv_up=w_kv_up_l0, k_norm=k_norm_l0, conv_w=conv_w_l0, w_o=w_o_l0,
             w_router=w_router_l0, w_gate=w_gate_l0, w_up=w_up_l0, w_down=w_down_l0),
        dict(norm1=norm1_l1, norm2=norm2_l1, w_mod=w_mod_l1, b_mod=b_mod_l1, w_f=w_f_l1,
             w_router=w_router_l1, w_gate=w_gate_l1, w_up=w_up_l1, w_down=w_down_l1),
    ]
    y_prompt, ctx_state = trunk(x_prompt, c_ctx[None, :], layers, [None, None], None)
    new_c_kv_l0, new_k_rope_l0 = ctx_state[0]
    rope = axial_rope(x_sample.shape[1])
    y_sample, _ = trunk(x_sample, c, layers, [(cache_c_kv_l0, cache_k_rope_l0), None], rope)
    return (y_prompt, y_sample, new_c_kv_l0, new_k_rope_l0)


_drawn_inputs = setup_inputs


def setup_inputs(seed=0):
    import zlib

    import numpy as np

    out = dict(_drawn_inputs(seed))
    spreads = {}
    factors = {'cache_c_kv_l0': 3.856,
     'cache_k_rope_l0': 6.15,
     'q_a_norm_l0': 5.23,
     'q_norm_l0': 8.0,
     'k_norm_l0': 7.612,
     'b_mod_l1': 2.693,
     'norm1_l1': 2.677,
     'norm2_l1': 3.282}
    for name, (base, spread) in spreads.items():
        noise = np.random.default_rng([zlib.crc32(name.encode()), seed]).standard_normal(out[name].shape)
        drawn = base * np.exp(spread * noise) if base else spread * noise
        out[name] = __import__('jax').numpy.asarray(drawn.astype(out[name].dtype))
    for name, factor in factors.items():
        out[name] = (out[name] * factor).astype(out[name].dtype)
    return out
```

```python
from contextlib import ExitStack, contextmanager

import numpy as np

import concourse.bass as bass
from concourse import mybir

F32 = mybir.dt.float32
F32R = mybir.dt.float32r
U32 = mybir.dt.uint32
ALU = mybir.AluOpType
ACT = mybir.ActivationFunctionType
AX = mybir.AxisListType

P = 128
D = 1024
KD = D // P
SEQ, DEC, PAST = 256, 1024, 256
TOK = SEQ + DEC
NT = TOK // P
PT, ST, CT = SEQ // P, DEC // P, PAST // P
KEYT = NT + CT
HEADS, NOPE, ROPE, VH = 8, 64, 32, 64
QK = NOPE + ROPE
QL, KVL = 384, 256
LAT = QL + KVL + ROPE
CONV = 512
CJ = CONV // P
IN0 = LAT + 3 * CONV
NE, FF = 16, 512
KF = FF // P
CAP_S, CAP_P = 2 * DEC // NE, 2 * SEQ // NE
SLOTS = CAP_S + CAP_P
GROUPS = 4
GW = D // GROUPS
HG = GW // 2
EPS = 1e-6
GRID_W = 64
THETA = 10000.0
MOD = 6 * D
BANK = 512


class Chain:

    def __init__(self, eng, sem):
        self.eng, self.sem, self.base, self.n = eng, sem, 0, 0

    def add(self, instruction):
        instruction.then_inc(self.sem, 1)
        self.n += 1

    def settle(self):
        self.eng.wait_ge(self.sem, self.base + self.n)

    def link(self, instruction):
        self.add(instruction)
        self.settle()

    @contextmanager
    def over(self, count, per):
        start = self.base + self.n
        with self.eng.Fori(0, count) as i:
            self.base, self.n = start + i * per, 0
            yield i
            assert self.n == per, f"{self.n} links in the loop, {per} said"
        self.base, self.n = start + count * per, 0


class Lasting:

    def __init__(self, s):
        self.ident = s.sb("ident", [P, P])
        self.scale1, self.shift1 = s.sb("scale1", [P, NT // 2, KD]), s.sb("shift1", [P, NT // 2, KD])
        self.scale2, self.shift2, self.gate2 = (s.sb(name, [P, 2, KD]) for name in ("scale2", "shift2", "gate2"))
        self.at_s, self.at_p = s.sb("at_s", [P, NE], U32), s.sb("at_p", [CAP_P, NE], U32)
        self.g_s, self.g_p = s.sb("g_s", [P, NE]), s.sb("g_p", [CAP_P, NE])


def wait(eng, sem, value):
    if not isinstance(value, int) or value > 0:
        eng.wait_ge(sem, value)


def turns(eng, count, body, ch=None, per=0):
    body(0)
    if count > 1:
        with (ch.over(count - 1, per) if ch else eng.Fori(0, count - 1)) as i:
            body(i + 1)


class Stage:

    def __init__(self, nc, name):
        self.nc, self.name, self.stack, self.own = nc, name, ExitStack(), []

    def __enter__(self):
        self.stack.__enter__()
        return self

    def __exit__(self, *a):
        self.nc.clear_and_free_semaphores(self.own)
        self.nc.all_engine_barrier()
        return self.stack.__exit__(*a)

    def sb(self, name, shape, dt=F32):
        return self.stack.enter_context(self.nc.sbuf_tensor(f"{self.name}_{name}", shape, dt))

    def ps(self, name, banks=1):
        return self.stack.enter_context(self.nc.psum_tensor(f"{self.name}_{name}", [P, banks * BANK], F32))

    def sem(self, name):
        self.own.append(self.nc.alloc_semaphore(f"{self.name}_{name}"))
        return self.own[-1]

    def sems(self, name, n):
        return [self.sem(f"{name}{k}") for k in range(n)]


def modulation(nc, t, per, layer):
    CH = 512
    NCH, NB, Q = MOD // CH, 4, 4
    w_mod = t[f"w_mod_l{layer}"].rearrange("(k p) f -> p k f", p=P)
    with Stage(nc, f"mod{layer}") as s:
        rows = s.sb("rows", [2 * KD, 2, P])
        cond = s.sb("cond", [P, KD, 2])
        gains = s.sb("gains", [P, 2, KD])
        mrow = s.sb("mrow", [2, MOD])
        mcol = s.sb("mcol", [P, MOD // P, 2])
        w = [s.sb(f"w{b}", [P, KD, CH]) for b in range(NB)]
        tp = s.ps("tp")
        acc = [s.ps(f"acc{b}") for b in range(NB)]
        rows_in, w_in = s.sem("rows_in"), s.sems("w_in", NB)
        turned, summed, kept = s.sem("turned"), s.sems("summed", NB), s.sems("kept", NB)
        rows_out, silu_done, chain = s.sem("rows_out"), s.sem("silu_done"), s.sem("chain")
        with nc.Block() as block:

            @block.sync
            def _(sp):
                sp.dma_start(rows[:, 0, :], t["cond"]).then_inc(rows_in, 16)
                sp.dma_start(rows[0:KD, 1, :], t[f"norm1_l{layer}"].rearrange("(k p) -> k p", p=P)).then_inc(rows_in, 16)
                sp.dma_start(rows[KD:2 * KD, 1, :], t[f"norm2_l{layer}"].rearrange("(k p) -> k p", p=P)).then_inc(rows_in, 16)
                sp.dma_start(mrow[:], t[f"b_mod_l{layer}"].partition_broadcast(2)).then_inc(rows_in, 16)

                def load(i):
                    for b in range(NB):
                        wait(sp, summed[b], i)
                        sp.dma_start(w[b][:], w_mod[:, :, bass.ts(i * NB + b, CH)]).then_inc(w_in[b], 16)

                turns(sp, NCH // NB, load)
                for b in range(NB):
                    sp.wait_ge(kept[b], NCH // NB)
                sp.dma_start(t["mod_rows"], mrow[:, 0:3 * D]).then_inc(rows_out, 16)
                sp.wait_ge(rows_out, 16)

            @block.tensor
            def _(pe):
                pe.wait_ge(rows_in, 64)
                pe.transpose(tp[:, 0:2 * KD], rows[:, 0, :], per.ident[0:2 * KD, 0:2 * KD])
                pe.transpose(tp[:, 16:16 + 2 * KD], rows[:, 1, :], per.ident[0:2 * KD, 0:2 * KD]).then_inc(turned, 1)
                pe.wait_ge(silu_done, 1)

                def products(i):
                    for b in range(NB):
                        pe.wait_ge(w_in[b], (i + 1) * 16)
                        wait(pe, kept[b], i)
                        for k in range(KD):
                            q = k % Q
                            last = pe.matmul(acc[b][32 * q:32 * q + 2, :], cond[:, k, :], w[b][:, k, :],
                                             start=(k < Q), stop=(k >= KD - Q), skip_group_check=True)
                            if k == KD - 1:
                                last.then_inc(summed[b], 1)

                turns(pe, NCH // NB, products)
                for b in range(NB):
                    pe.wait_ge(kept[b], NCH // NB)
                pe.wait_ge(chain, 1)
                for j in range(MOD // P):
                    last = pe.transpose(tp[:, 2 * j:2 * j + 2], mrow[:, j * P:(j + 1) * P], per.ident[0:2, 0:2])
                last.then_inc(turned, 1)

            @block.scalar
            def _(act):
                act.wait_ge(turned, 1)
                act.activation(cond[:].rearrange("p k c -> p c k"), tp[:, 0:2 * KD].rearrange("p (c k) -> p c k", c=2),
                               ACT.Silu).then_inc(silu_done, 1)

            @block.vector
            def _(dve):
                ch = Chain(dve, chain)
                dve.wait_ge(silu_done, 1)
                ch.link(dve.tensor_copy(gains[:].rearrange("p c k -> p (c k)"), tp[:, 16:16 + 2 * KD]))
                dve.wait_ge(rows_in, 64)

                def sums(i):
                    for b in range(NB):
                        dve.wait_ge(summed[b], i + 1)
                        m = mrow[:, bass.ts(i * NB + b, CH)]
                        for q in range(Q):
                            add = dve.tensor_tensor(m, acc[b][32 * q:32 * q + 2, :], m, ALU.add)
                            if q < Q - 1:
                                ch.link(add)
                        add.then_inc(kept[b], 1)

                turns(dve, NCH // NB, sums, ch, NB * (Q - 1))

                dve.wait_ge(turned, 2)
                ch.link(dve.tensor_copy(mcol[:].rearrange("p j c -> p (j c)"), tp[:, 0:2 * MOD // P]))

                def piece(c, n):
                    return mcol[:, n * KD:(n + 1) * KD, c]

                for tile in range(5):
                    c = min(tile, 1)
                    dve.scalar_tensor_tensor(out=per.scale1[:, tile, :], in0=piece(c, 1), scalar=1.0,
                                             in1=gains[:, 0, :], op0=ALU.add, op1=ALU.mult)
                    dve.tensor_copy(per.shift1[:, tile, :], piece(c, 0))
                for c in range(2):
                    dve.scalar_tensor_tensor(out=per.scale2[:, c, :], in0=piece(c, 4), scalar=1.0,
                                             in1=gains[:, 1, :], op0=ALU.add, op1=ALU.mult)
                    dve.tensor_copy(per.shift2[:, c, :], piece(c, 3))
                    dve.tensor_copy(per.gate2[:, c, :], piece(c, 5))
def projections(nc, t, per):
    TP = 4
    HALF = NT // 2 - 1
    with Stage(nc, "proj") as s:
        w_in = s.sb("w_in", [P, KD, IN0])
        w_q = s.sb("w_q", [P, QL // P, HEADS * QK])
        w_kv = s.sb("w_kv", [P, KVL // P, HEADS * 2 * VH])
        conv_w = s.sb("conv_w", [P, 3 * CJ])
        conv_rows = s.sb("conv_rows", [3 * CJ, P])
        lat_gain = s.sb("lat_gain", [P, QL + KVL])
        q_gain, k_gain = s.sb("q_gain", [P, QK]), s.sb("k_gain", [P, QK])
        eps = s.sb("eps", [P, 1])
        x_t = [s.sb(f"x{u}", [P, D]) for u in range(2)]
        rope_t = s.sb("rope", [P, 2, ROPE // 2])
        junk = s.sb("junk", [P, D])
        xh = s.sb("xh", [P, D])
        h_t = s.sb("h_t", [P, KD, P])
        ms, rstd = s.sb("ms", [P, 1]), s.sb("rstd", [P, 1])
        lms, lrstd = s.sb("lms", [P, 2]), s.sb("lrstd", [P, 2])
        lat = [s.sb(f"lat{u}", [P, LAT]) for u in range(2)]
        lat_t = s.sb("lat_t", [P, (QL + KVL) // P, P])
        q_sq, k_sq = s.sb("q_sq", [P, HEADS, QK]), s.sb("k_sq", [P, HEADS, QK])
        q_n, k_n = s.sb("q_n", [P, HEADS, QK]), s.sb("k_n", [P, HEADS, QK])
        q_ms, k_ms = s.sb("q_ms", [P, 2, HEADS]), s.sb("k_ms", [P, 2, HEADS])
        turn = s.sb("turn", [P, 4, HEADS, ROPE // 2])
        gate_b = s.sb("gate_b", [P, CJ, TOK])
        taps = s.sb("taps", [P, TOK])
        q_out = s.sb("q_out", [QK, HEADS * P])
        k_out = s.sb("k_out", [QK, HEADS * P])
        v_out = s.sb("v_out", [P, HEADS * VH])
        u_sb = s.sb("u_sb", [P, CJ * P])
        gated = s.sb("gated", [P, CJ, TOK])

        tp = [s.ps(f"tp{b}") for b in range(2)]
        lp = s.ps("lp", 2)
        up = s.ps("up", 2)
        cv = [s.ps(f"cv{b}") for b in range(2)]

        w_ready, gains_in, conv_in = s.sem("w_ready"), s.sem("gains_in"), s.sem("conv_in")
        x_in, rope_in = s.sems("x_in", 2), s.sem("rope_in")
        ms_ready, x_ready, h_ready = s.sem("ms_ready"), s.sem("x_ready"), s.sem("h_ready")
        tp_full, tp_free = s.sems("tp_full", 2), s.sems("tp_free", 2)
        lp_full, kv_kept = s.sem("lp_full"), s.sem("kv_kept")
        lms_ready, lat_ready, lat_in = s.sem("lms_ready"), s.sem("lat_ready"), s.sem("lat_in")
        up_full, up_free = s.sem("up_full"), s.sem("up_free")
        q_sq_ready, q_sum, q_ms_ready = s.sem("q_sq_ready"), s.sem("q_sum"), s.sem("q_ms_ready")
        k_sq_ready, k_sum, k_ms_ready = s.sem("k_sq_ready"), s.sem("k_sum"), s.sem("k_ms_ready")
        q_ready, k_ready = s.sem("q_ready"), s.sem("k_ready")
        q_stored, k_stored, v_stored = s.sem("q_stored"), s.sem("k_stored"), s.sem("v_stored")
        lat_stored = s.sems("lat_stored", 2)
        u_full, c_full, b_full = s.sem("u_full"), s.sem("c_full"), s.sem("b_full")
        u_kept, c_kept, b_kept = s.sem("u_kept"), s.sem("c_kept"), s.sem("b_kept")
        taps_full, taps_kept, mixed = s.sem("taps_full"), s.sem("taps_kept"), s.sem("mixed")
        late_out, a_chain, v_chain = s.sem("late_out"), s.sem("a_chain"), s.sem("v_chain")

        def tiles(eng, body, ch=None, per_turn=0):
            def pair(i):
                body(2 * i, i, 0, True)
                body(2 * i + 1, i, 1, True)

            turns(eng, HALF, pair, ch, per_turn)
            body(NT - 2, HALF, 0, True)
            body(NT - 1, HALF, 1, False)

        with nc.Block() as block:

            @block.sync
            def _(sp):
                w_in_d = t["w_in_l0"].rearrange("(k p) f -> p k f", p=P)
                sp.dma_start(w_in[:, :, 0:LAT], w_in_d[:, :, 0:LAT]).then_inc(w_ready, 16)
                sp.dma_start(lat_gain[:, 0:QL], t["q_a_norm_l0"].partition_broadcast(P)).then_inc(gains_in, 16)
                sp.dma_start(lat_gain[:, QL:QL + KVL], t["kv_a_norm_l0"].partition_broadcast(P)).then_inc(gains_in, 16)
                sp.dma_start(q_gain[:], t["q_norm_l0"].partition_broadcast(P)).then_inc(gains_in, 16)
                sp.dma_start(k_gain[:], t["k_norm_l0"].partition_broadcast(P)).then_inc(gains_in, 16)
                sp.dma_start(conv_rows[:], t["conv_w_l0"].rearrange("a (j p) -> (a j) p", p=P)).then_inc(conv_in, 16)
                sp.dma_start(w_in[:, :, LAT:IN0], w_in_d[:, :, LAT:IN0]).then_inc(w_ready, 16)
                sp.dma_start(w_q[:], t["w_q_up_l0"].rearrange("(k p) f -> p k f", p=P)).then_inc(w_ready, 16)
                sp.dma_start(w_kv[:], t["w_kv_up_l0"].rearrange("(k p) f -> p k f", p=P)).then_inc(w_ready, 16)

                def rope_load(n):
                    wait(sp, k_stored, 16 * n)
                    sp.dma_start(rope_t[:].rearrange("p a r -> p (a r)"), t["rope"][bass.ts(n, P), :]).then_inc(rope_in, 16)

                def keys_store(n, tp_use):
                    sp.wait_ge(kv_kept, 2 * n + 2)
                    sp.dma_start(t["v"][bass.ts(n, P), :], v_out[:]).then_inc(v_stored, 16)
                    for b in range(2):
                        sp.wait_ge(tp_free[b], tp_use)
                    sp.dma_start(t["kt"][bass.ts(n, QK), :], k_out[:]).then_inc(k_stored, 16)

                def stores(i):
                    for u in range(2):
                        n = 2 * i + u
                        rope_load(n)
                        sp.wait_ge(lat_ready, 3 * n + 3)
                        sp.dma_start(t["state"][bass.ts(n, P), :], lat[u][:, QL:LAT]).then_inc(lat_stored[u], 16)
                        for b in range(2):
                            sp.wait_ge(tp_free[b], TP * n + 3)
                        sp.dma_start(t["qt"][bass.ts(n, QK), :], q_out[:]).then_inc(q_stored, 16)
                        keys_store(n, TP * n + 4)

                turns(sp, NT // 2, stores)
                for c in range(CT):
                    n = NT + c
                    rope_load(n)
                    sp.wait_ge(lat_stored[c], 16 * NT // 2)
                    sp.dma_start(lat[c][:, QL:QL + KVL], t["cache_c_kv_l0"][c * P:(c + 1) * P, :]).then_inc(lat_in, 16)
                    sp.dma_start(lat[c][:, QL + KVL:LAT], t["cache_k_rope_l0"][c * P:(c + 1) * P, :]).then_inc(lat_in, 16)
                    keys_store(n, TP * NT + 2 * c + 2)
                sp.dma_start(t["new_c_kv"], t["state"][0:SEQ, 0:KVL]).then_inc(late_out, 16)
                sp.dma_start(t["new_k_rope"], t["state"][0:SEQ, KVL:KVL + ROPE]).then_inc(late_out, 16)
                for j in range(CJ):
                    sp.wait_ge(mixed, j + 1)
                    sp.dma_start(t["conv"][j], gate_b[:, j, :]).then_inc(late_out, 16)
                for done, value in ((q_stored, 16 * NT), (k_stored, 16 * KEYT), (v_stored, 16 * KEYT), (late_out, 16 * (2 + CJ))):
                    sp.wait_ge(done, value)

            @block.gpsimd
            def _(pool):
                for u in range(2):
                    pool.dma_start(x_t[u][:], t["x"][u * P:(u + 1) * P, :]).then_inc(x_in[u], 16)
                with pool.Fori(1, NT // 2) as i:
                    for u in range(2):
                        pool.wait_ge(x_ready, 2 * i + u - 1)
                        pool.dma_start(x_t[u][:], t["x"][bass.ts(2 * i + u, P), :]).then_inc(x_in[u], 16)

            @block.tensor
            def _(pe):
                def latent_turns(use, first, u):
                    for b, lo, hi in ((0, first, 4), (1, 4, 5)):
                        pe.wait_ge(tp_free[b], use)
                        for j in range(lo, hi):
                            last = pe.transpose(tp[b][:, (j % 4) * P:(j % 4 + 1) * P], lat[u][:, j * P:(j + 1) * P], per.ident[:])
                        last.then_inc(tp_full[b], 1)

                def kv_up(use):
                    for b in range(2):
                        pe.wait_ge(tp_free[b], use)
                    for half in range(2):
                        for k in range(KVL // P):
                            last = pe.matmul(lp[:, half * BANK:(half + 1) * BANK], lat_t[:, QL // P + k, :],
                                             w_kv[:, k, half * BANK:(half + 1) * BANK], start=(k == 0), stop=(k == KVL // P - 1))
                    last.then_inc(lp_full, 1)

                def head_turns(src, ready, n, use):
                    pe.wait_ge(ready, 2 * n + 2)
                    for b in range(2):
                        pe.wait_ge(tp_free[b], use)
                        for j in range(4):
                            last = pe.transpose(tp[b][0:QK, j * P:(j + 1) * P], src[:, 4 * b + j, :], per.ident[:])
                        last.then_inc(tp_full[b], 1)

                def conv_part(base, bank, full):
                    for j in range(CJ):
                        for k in range(KD):
                            last = pe.matmul(cv[bank][:, j * P:(j + 1) * P], w_in[:, k, base + j * P:base + (j + 1) * P],
                                             h_t[:, k, :], start=(k == 0), stop=(k == KD - 1))
                    last.then_inc(full, 1)

                pe.wait_ge(conv_in, 16)
                pe.transpose(cv[0][:, 0:3 * CJ], conv_rows[:], per.ident[0:3 * CJ, 0:3 * CJ]).then_inc(taps_full, 1)
                pe.wait_ge(taps_kept, 1)

                def pair(i):
                    for u in range(2):
                        n = 2 * i + u
                        pe.wait_ge(x_ready, n + 1)
                        for b in range(2):
                            wait(pe, tp_free[b], TP * n)
                            for j in range(4):
                                k = 4 * b + j
                                last = pe.transpose(tp[b][:, j * P:(j + 1) * P], xh[:, k * P:(k + 1) * P], per.ident[:])
                            last.then_inc(tp_full[b], 1)
                        pe.wait_ge(h_ready, 2 * n + 2)
                        pe.wait_ge(w_ready, 64)
                        wait(pe, kv_kept, 2 * n)
                        for base, lo, hi in ((0, 0, QL), (BANK, QL, LAT)):
                            for k in range(KD):
                                last = pe.matmul(lp[:, base:base + hi - lo], h_t[:, k, :], w_in[:, k, lo:hi],
                                                 start=(k == 0), stop=(k == KD - 1))
                        last.then_inc(lp_full, 1)
                        wait(pe, b_kept, n)
                        conv_part(LAT + 2 * CONV, 0, u_full)
                        pe.wait_ge(lat_ready, 3 * n + 3)
                        latent_turns(TP * n + 1, 0, u)
                        wait(pe, c_kept, n)
                        conv_part(LAT + CONV, 1, c_full)
                        for b in range(2):
                            pe.wait_ge(tp_free[b], TP * n + 2)
                        wait(pe, up_free, n)
                        for lo, hi in ((0, BANK), (BANK, HEADS * QK)):
                            for k in range(QL // P):
                                last = pe.matmul(up[:, lo:hi], lat_t[:, k, :], w_q[:, k, lo:hi],
                                                 start=(k == 0), stop=(k == QL // P - 1))
                        last.then_inc(up_full, 1)
                        kv_up(TP * n + 2)
                        pe.wait_ge(u_kept, n + 1)
                        conv_part(LAT, 0, b_full)
                        head_turns(q_n, q_ready, n, TP * n + 2)
                        head_turns(k_n, k_ready, n, TP * n + 3)

                turns(pe, NT // 2, pair)
                for c in range(CT):
                    pe.wait_ge(lat_in, 32 * (c + 1))
                    latent_turns(TP * NT + 2 * c, QL // P, c)
                    pe.wait_ge(kv_kept, 2 * (NT + c))
                    kv_up(TP * NT + 2 * c + 1)
                    head_turns(k_n, k_ready, NT + c, TP * NT + 2 * c + 1)

            @block.scalar
            def _(act):
                ch = Chain(act, a_chain)

                def x_square(n, i, u):
                    act.wait_ge(x_in[u], 16 * (i + 1))
                    wait(act, x_ready, n)
                    ch.link(act.activation(junk[:], x_t[u][:], ACT.Square, accum_out=ms[:]))
                    act.activation(rstd[:], ms[:], ACT.Sqrt, bias=eps[:], scale=1.0 / D).then_inc(ms_ready, 1)

                def latents_kept(use, first):
                    for b, lo, hi in ((0, first, 4), (1, 4, 5)):
                        act.wait_ge(tp_full[b], use)
                        act.activation(lat_t[:, lo:hi, :].rearrange("p j c -> p (j c)"),
                                       tp[b][:, (lo % 4) * P:(lo % 4 + hi - lo) * P], ACT.Copy).then_inc(tp_free[b], 1)

                def keys_values(n, lp_use, rope_cols):
                    act.wait_ge(lp_full, lp_use)
                    kv = lp[:].rearrange("p (h c) -> p h c", h=HEADS)
                    ch.add(act.activation(k_n[:, :, NOPE:QK], rope_cols.unsqueeze(1).broadcast_to([P, HEADS, ROPE]), ACT.Copy))
                    act.activation(k_n[:, :, 0:NOPE], kv[:, :, 0:NOPE], ACT.Copy).then_inc(kv_kept, 1)
                    wait(act, v_stored, 16 * n)
                    act.activation(v_out[:].rearrange("p (h c) -> p h c", h=HEADS), kv[:, :, NOPE:NOPE + VH], ACT.Copy).then_inc(kv_kept, 1)
                    ch.settle()
                    act.wait_ge(kv_kept, 2 * n + 1)
                    wait(act, k_sum, n)
                    act.activation(k_sq[:], k_n[:], ACT.Square).then_inc(k_sq_ready, 1)

                def root(n, sums, src, ready):
                    act.wait_ge(sums, n + 1)
                    act.activation(src[:, 1, :], src[:, 0, :], ACT.Sqrt, bias=eps[:], scale=1.0 / QK).then_inc(ready, 1)

                def tile(n, i, u, more):
                    if more:
                        x_square(n + 1, i + u, 1 - u)
                    act.wait_ge(lp_full, 2 * n + 1)
                    ch.add(act.activation(junk[:, 0:QL], lp[:, 0:QL], ACT.Square, accum_out=lms[:, 0:1]))
                    ch.settle()
                    ch.link(act.activation(junk[:, 0:KVL], lp[:, BANK:BANK + KVL], ACT.Square, accum_out=lms[:, 1:2]))
                    act.activation(lrstd[:, 0:1], lms[:, 0:1], ACT.Sqrt, bias=eps[:], scale=1.0 / QL).then_inc(lms_ready, 1)
                    act.activation(lrstd[:, 1:2], lms[:, 1:2], ACT.Sqrt, bias=eps[:], scale=1.0 / KVL).then_inc(lms_ready, 1)
                    act.wait_ge(u_full, n + 1)
                    wait(act, c_kept, n)
                    act.activation(u_sb[:], cv[0][:], ACT.Copy).then_inc(u_kept, 1)
                    latents_kept(TP * n + 2, 0)
                    act.wait_ge(up_full, n + 1)
                    act.activation(q_sq[:].rearrange("p h c -> p (h c)"), up[:, 0:HEADS * QK], ACT.Square).then_inc(q_sq_ready, 1)
                    keys_values(n, 2 * n + 2, lat[u][:, QL + KVL:LAT])
                    root(n, q_sum, q_ms, q_ms_ready)
                    root(n, k_sum, k_ms, k_ms_ready)
                    act.wait_ge(b_full, n + 1)
                    act.activation(gate_b[:, :, bass.ts(n, P)], cv[0][:].rearrange("p (j c) -> p j c", j=CJ), ACT.Copy).then_inc(b_kept, 1)
                    wait(act, q_stored, 16 * n)
                    for b in range(2):
                        act.wait_ge(tp_full[b], TP * n + 3)
                        act.activation(q_out[:, b * BANK:(b + 1) * BANK], tp[b][0:QK, :], ACT.Copy).then_inc(tp_free[b], 1)

                act.wait_ge(v_chain, 1)
                x_square(0, 0, 0)
                tiles(act, tile, ch, 2 * 4)
                for c in range(CT):
                    n = NT + c
                    latents_kept(TP * NT + 2 * c + 1, QL // P)
                    keys_values(n, 2 * NT + c + 1, lat[c][:, QL + KVL:LAT])
                    root(n, k_sum, k_ms, k_ms_ready)

            @block.vector
            def _(dve):
                ch = Chain(dve, v_chain)

                def normalise_x(n, u):
                    dve.wait_ge(ms_ready, n + 1)
                    ch.link(dve.reciprocal(rstd[:], rstd[:]))
                    dve.tensor_scalar(xh[:], x_t[u][:], rstd[:], None, ALU.mult).then_inc(x_ready, 1)

                def normalise_heads(src, dst, ms_, ready_in, n, gain, freed, ready):
                    dve.wait_ge(ready_in, n + 1)
                    ch.link(dve.reciprocal(ms_[:, 1, :], ms_[:, 1, :]))
                    first = dve.tensor_tensor(dst[:], src, ms_[:, 1, :].unsqueeze(2).broadcast_to([P, HEADS, QK]), ALU.mult)
                    if freed is None:
                        ch.link(first)
                    else:
                        first.then_inc(freed, 1)
                        dve.wait_ge(freed, n + 1)
                    ch.link(dve.tensor_tensor(dst[:], dst[:], gain[:].unsqueeze(1).broadcast_to([P, HEADS, QK]), ALU.mult))
                    pair = dst[:, :, NOPE:QK].rearrange("p h (r two) -> p h r two", two=2)
                    cos = rope_t[:, 0, :].unsqueeze(1).broadcast_to([P, HEADS, ROPE // 2])
                    sin = rope_t[:, 1, :].unsqueeze(1).broadcast_to([P, HEADS, ROPE // 2])
                    dve.wait_ge(rope_in, 16 * (n + 1))
                    for m, (x, f) in enumerate(((0, cos), (1, sin), (0, sin), (1, cos))):
                        ch.add(dve.tensor_tensor(turn[:, m, :, :], pair[:, :, :, x], f, ALU.mult))
                    ch.settle()
                    dve.tensor_tensor(pair[:, :, :, 0], turn[:, 0, :, :], turn[:, 1, :, :], ALU.subtract).then_inc(ready, 1)
                    dve.tensor_tensor(pair[:, :, :, 1], turn[:, 2, :, :], turn[:, 3, :, :], ALU.add).then_inc(ready, 1)

                def sums(sq, ready_in, n, out, ready):
                    dve.wait_ge(ready_in, n + 1)
                    dve.tensor_reduce(out[:, 0, :], sq[:], AX.X, ALU.add).then_inc(ready, 1)

                def keys_kept(n, use):
                    wait(dve, k_stored, 16 * n)
                    for b in range(2):
                        dve.wait_ge(tp_full[b], use)
                        dve.tensor_copy(k_out[:, b * BANK:(b + 1) * BANK], tp[b][0:QK, :]).then_inc(tp_free[b], 1)

                def tile(n, i, u, more):
                    for b in range(2):
                        dve.wait_ge(tp_full[b], TP * n + 1)
                        cols = slice(4 * b, 4 * b + 4)
                        dve.tensor_tensor(h_t[:, cols, :], tp[b][:].rearrange("p (k c) -> p k c", k=4),
                                          per.scale1[:, i, cols].unsqueeze(2).broadcast_to([P, 4, P]), ALU.mult).then_inc(tp_free[b], 1)
                        dve.wait_ge(tp_free[b], TP * n + 1)
                        dve.tensor_tensor(h_t[:, cols, :], h_t[:, cols, :],
                                          per.shift1[:, i, cols].unsqueeze(2).broadcast_to([P, 4, P]), ALU.add).then_inc(h_ready, 1)
                    if more:
                        normalise_x(n + 1, 1 - u)
                    dve.wait_ge(lms_ready, 2 * n + 2)
                    ch.link(dve.reciprocal(lrstd[:], lrstd[:]))
                    wait(dve, lat_stored[u], 16 * i)
                    dve.scalar_tensor_tensor(out=lat[u][:, 0:QL], in0=lp[:, 0:QL], scalar=lrstd[:, 0:1], in1=lat_gain[:, 0:QL],
                                             op0=ALU.mult, op1=ALU.mult).then_inc(lat_ready, 1)
                    dve.scalar_tensor_tensor(out=lat[u][:, QL:QL + KVL], in0=lp[:, BANK:BANK + KVL], scalar=lrstd[:, 1:2],
                                             in1=lat_gain[:, QL:QL + KVL], op0=ALU.mult, op1=ALU.mult).then_inc(lat_ready, 1)
                    dve.tensor_copy(lat[u][:, QL + KVL:LAT], lp[:, BANK + KVL:BANK + LAT - QL]).then_inc(lat_ready, 1)
                    dve.wait_ge(c_full, n + 1)
                    dve.wait_ge(u_kept, n + 1)
                    dve.tensor_tensor(gated[:, :, bass.ts(n, P)], cv[1][:].rearrange("p (j c) -> p j c", j=CJ),
                                      u_sb[:].rearrange("p (j c) -> p j c", j=CJ), ALU.mult).then_inc(c_kept, 1)
                    sums(q_sq, q_sq_ready, n, q_ms, q_sum)
                    sums(k_sq, k_sq_ready, n, k_ms, k_sum)
                    normalise_heads(up[:, 0:HEADS * QK].rearrange("p (h c) -> p h c", h=HEADS), q_n, q_ms, q_ms_ready, n, q_gain,
                                    up_free, q_ready)
                    dve.wait_ge(q_ready, 2 * n + 2)
                    normalise_heads(k_n[:], k_n, k_ms, k_ms_ready, n, k_gain, None, k_ready)
                    keys_kept(n, TP * n + 4)

                ch.link(dve.memset(eps[:], EPS))
                dve.wait_ge(taps_full, 1)
                dve.tensor_copy(conv_w[:], cv[0][:, 0:3 * CJ]).then_inc(taps_kept, 1)
                dve.wait_ge(gains_in, 64)
                normalise_x(0, 0)
                tiles(dve, tile, ch, 2 * 15)
                for c in range(CT):
                    n = NT + c
                    sums(k_sq, k_sq_ready, n, k_ms, k_sum)
                    normalise_heads(k_n[:], k_n, k_ms, k_ms_ready, n, k_gain, None, k_ready)
                    keys_kept(n, TP * NT + 2 * c + 2)
                dve.wait_ge(b_kept, NT)
                dve.wait_ge(c_kept, NT)
                for j in range(CJ):
                    ch.link(dve.tensor_scalar(taps[:], gated[:, j, :], conv_w[:, CJ + j:CJ + j + 1], None, ALU.mult))
                    for a, shift in ((0, -1), (2, 1)):
                        for lo, hi in ((0, SEQ), (SEQ, TOK)):
                            o = slice(lo + max(0, -shift), hi - max(0, shift))
                            i_ = slice(lo + max(0, shift), hi - max(0, -shift))
                            ch.add(dve.scalar_tensor_tensor(out=taps[:, o], in0=gated[:, j, i_],
                                                            scalar=conv_w[:, a * CJ + j:a * CJ + j + 1], in1=taps[:, o],
                                                            op0=ALU.mult, op1=ALU.add))
                        ch.settle()
                    dve.tensor_tensor(gate_b[:, j, :], gate_b[:, j, :], taps[:], ALU.mult).then_inc(mixed, 1)
                    dve.wait_ge(mixed, j + 1)


def attention(nc, t, per, name, q_first, q_tiles, k_first, nk):
    K = nk * P
    SCALE = float(QK) ** -0.5
    PAIRS = q_tiles // 2
    spans = [(lo, min(lo + BANK, K)) for lo in range(0, K, BANK)]
    with Stage(nc, name) as s:
        keys = s.sb("keys", [QK, HEADS, K])
        vals = s.sb("vals", [P, nk, HEADS * VH])
        q_t = [s.sb(f"q{u}", [QK, HEADS * P]) for u in range(2)]
        pr = [s.sb(f"pr{b}", [P, K]) for b in range(2)]
        pr_t = [s.sb(f"pr_t{b}", [P, K]) for b in range(2)]
        top, neg = s.sb("top", [P, 1]), [s.sb(f"neg{b}", [P, 1]) for b in range(2)]
        total, inv = [s.sb(f"total{b}", [P, 1]) for b in range(2)], s.sb("inv", [P, 1])
        o_sb = [s.sb(f"o_sb{u}", [P, HEADS // 2 * P]) for u in range(2)]
        sc = [s.ps(f"sc{b}", 3) for b in range(2)]
        o_ps = [s.ps(f"o{u}") for u in range(2)]

        keys_in, vals_in, q_in, o_out = s.sem("keys_in"), s.sem("vals_in"), s.sems("q_in", 2), s.sems("o_out", 2)
        s_full, neg_ready, p_ready, p_scaled = s.sem("s_full"), s.sem("neg_ready"), s.sem("p_ready"), s.sem("p_scaled")
        t_full, v_kept, a_kept = s.sem("t_full"), s.sem("v_kept"), s.sem("a_kept")
        o_full, o_kept, chain = s.sem("o_full"), s.sem("o_kept"), s.sem("chain")

        def tiles(eng, body, ch=None, per_turn=0):
            if PAIRS > 1:
                body(0, 0, 0, True)
                body(1, 0, 1, True)
            if PAIRS > 2:
                with (ch.over(PAIRS - 2, per_turn) if ch else eng.Fori(0, PAIRS - 2)) as turn:
                    i = turn + 1
                    body(2 * i, i, 0, True)
                    body(2 * i + 1, i, 1, True)
            body(q_tiles - 2, PAIRS - 1, 0, True)
            body(q_tiles - 1, PAIRS - 1, 1, False)

        def count(n, h, less):
            return HEADS * n + h - less

        with nc.Block() as block:

            @block.sync
            def _(sp):
                for u in range(2):
                    sp.dma_start(q_t[u][:], t["qt"][(q_first + u) * QK:(q_first + u + 1) * QK, :]).then_inc(q_in[u], 16)
                for m in range(nk):
                    sp.dma_start(keys[:, :, m * P:(m + 1) * P],
                                 t["kt"][(k_first + m) * QK:(k_first + m + 1) * QK, :].rearrange("c (h k) -> c h k", h=HEADS)).then_inc(keys_in, 16)
                sp.dma_start(vals[:], t["v"][k_first * P:(k_first + nk) * P, :].rearrange("(m p) c -> p m c", p=P)).then_inc(vals_in, 16)

                if PAIRS > 1:
                    with sp.Fori(0, PAIRS - 1) as i:
                        for u in range(2):
                            n = 2 * i + u
                            sp.wait_ge(s_full, HEADS * (n + 1))
                            sp.dma_start(q_t[u][:], t["qt"][bass.ds((q_first + 2 + n) * QK, QK), :]).then_inc(q_in[u], 16)
                            sp.wait_ge(o_kept, n + 1)
                            sp.dma_start(t["attn"][bass.ds((q_first + n) * P, P), :], o_sb[u][:]).then_inc(o_out[u], 16)
                for u in range(2):
                    n = q_tiles - 2 + u
                    sp.wait_ge(o_kept, n + 1)
                    sp.dma_start(t["attn"][(q_first + n) * P:(q_first + n + 1) * P, :], o_sb[u][:]).then_inc(o_out[u], 16)
                for u in range(2):
                    sp.wait_ge(o_out[u], 16 * (q_tiles // 2))

            @block.tensor
            def _(pe):
                def scores(n, h, i, u):
                    if h == 0:
                        pe.wait_ge(q_in[u], 16 * (i + 1))
                    b = h % 2
                    for kept in (v_kept, a_kept) if K > BANK else (v_kept,):
                        wait(pe, kept, count(n, h, 1))
                    for lo, hi in spans:
                        last = pe.matmul(sc[b][:, lo:hi], q_t[u][:, h * P:(h + 1) * P], keys[:, h, lo:hi], start=True, stop=True)
                    last.then_inc(s_full, 1)

                def turns(n, h):
                    pe.wait_ge(p_scaled, HEADS * n + h + 1)
                    for m in range(nk):
                        last = pe.transpose(sc[h % 2][:, m * P:(m + 1) * P], pr[h % 2][:, m * P:(m + 1) * P], per.ident[:])
                    last.then_inc(t_full, 1)

                def mix(n, h, u):
                    for kept in (v_kept, a_kept) if K > BANK else (v_kept,):
                        pe.wait_ge(kept, HEADS * n + h + 1)
                    if h == 0:
                        wait(pe, o_kept, n - 1)
                    lo = 64 * (h % 2)
                    out = o_ps[u][lo:lo + VH, (h // 2) * P:(h // 2 + 1) * P]
                    for m in range(nk):
                        last = pe.matmul(out, vals[:, m, h * VH:(h + 1) * VH], pr_t[h % 2][:, m * P:(m + 1) * P],
                                         start=(m == 0), stop=(m == nk - 1))
                    last.then_inc(o_full, 1)

                def tile(n, i, u, more):
                    for h in range(HEADS):
                        if h < HEADS - 1:
                            scores(n, h + 1, i, u)
                        elif more:
                            scores(n + 1, 0, i + u, 1 - u)
                        turns(n, h)
                        if h:
                            mix(n, h - 1, u)
                    mix(n, HEADS - 1, u)

                pe.wait_ge(keys_in, 16 * nk)
                scores(0, 0, 0, 0)
                pe.wait_ge(vals_in, 16)
                tiles(pe, tile)

            @block.scalar
            def _(act):
                def exp(n, h):
                    b = h % 2
                    act.wait_ge(neg_ready, HEADS * n + h + 1)
                    wait(act, t_full, count(n, h, 1))
                    act.activation(pr[b][:], sc[b][:, 0:K], ACT.Exp, bias=neg[b][:], scale=SCALE, accum_out=total[b][:]).then_inc(p_ready, 1)

                def tile(n, i, u, more):
                    for h in range(HEADS):
                        b = h % 2
                        if K > BANK:
                            act.wait_ge(t_full, HEADS * n + h + 1)
                            wait(act, o_full, count(n, h, 1))
                            act.activation(pr_t[b][:, BANK:K], sc[b][:, BANK:K], ACT.Copy).then_inc(a_kept, 1)
                        if h < HEADS - 1:
                            exp(n, h + 1)
                        elif more:
                            exp(n + 1, 0)
                    act.wait_ge(o_full, HEADS * (n + 1))
                    wait(act, o_out[u], 16 * i)
                    act.activation(o_sb[u][:], o_ps[u][:], ACT.Copy).then_inc(o_kept, 1)

                exp(0, 0)
                tiles(act, tile)

            @block.vector
            def _(dve):
                ch = Chain(dve, chain)

                def maximum(n, h):
                    b = h % 2
                    dve.wait_ge(s_full, HEADS * n + h + 1)
                    ch.link(dve.tensor_reduce(top[:], sc[b][:, 0:K], AX.X, ALU.max))
                    wait(dve, p_ready, count(n, h, 1))
                    dve.tensor_scalar(neg[b][:], top[:], -SCALE, None, ALU.mult).then_inc(neg_ready, 1)

                def tile(n, i, u, more):
                    for h in range(HEADS):
                        b = h % 2
                        dve.wait_ge(p_ready, HEADS * n + h + 1)
                        ch.link(dve.reciprocal(inv[:], total[b][:]))
                        dve.tensor_scalar(pr[b][:], pr[b][:], inv[:], None, ALU.mult).then_inc(p_scaled, 1)
                        if h < HEADS - 1:
                            maximum(n, h + 1)
                        elif more:
                            maximum(n + 1, 0)
                        dve.wait_ge(t_full, HEADS * n + h + 1)
                        wait(dve, o_full, count(n, h, 1))
                        dve.tensor_copy(pr_t[b][:, 0:min(K, BANK)], sc[b][:, 0:min(K, BANK)]).then_inc(v_kept, 1)

                maximum(0, 0)
                tiles(dve, tile, ch, 2 * 2 * HEADS)


def mixer_out(nc, t, per):
    with Stage(nc, "out") as s:
        w_o = s.sb("w_o", [P, KD, D])
        gate = s.sb("gate", [P, 2, D])
        a_t = [s.sb(f"a{u}", [P, KD, P]) for u in range(2)]
        x_t = [s.sb(f"x{u}", [P, D]) for u in range(2)]
        y_t = [s.sb(f"y{u}", [P, D]) for u in range(2)]
        acc = [s.ps(f"acc{u}", 2) for u in range(2)]
        w_ready, gate_in, a_in, x_in = s.sem("w_ready"), s.sem("gate_in"), s.sems("a_in", 2), s.sems("x_in", 2)
        full, kept, y_ready, y_out = s.sem("full"), s.sem("kept"), s.sem("y_ready"), s.sems("y_out", 2)

        def pairs(eng, body):
            body(0, 0)
            with eng.Fori(1, NT // 2) as i:
                body(i, 1)

        with nc.Block() as block:

            @block.sync
            def _(sp):
                sp.dma_start(w_o[:], t["w_o_l0"].rearrange("(k p) f -> p k f", p=P)).then_inc(w_ready, 16)
                for c in range(2):
                    sp.dma_start(gate[:, c, :], t["mod_rows"][c, 2 * D:3 * D].partition_broadcast(P)).then_inc(gate_in, 16)

                def pair(i, c):
                    for u in range(2):
                        n = 2 * i + u
                        wait(sp, full, n - 1)
                        sp.dma_start(a_t[u][:, 0:KD // 2, :].rearrange("p k c -> p (k c)"), t["attn"][bass.ts(n, P), :]).then_inc(a_in[u], 16)
                        sp.dma_start(a_t[u][:, KD // 2:KD, :], t["conv"].rearrange("j p n -> p j n")[:, :, bass.ts(n, P)]).then_inc(a_in[u], 16)
                        wait(sp, y_ready, n - 1)
                        sp.dma_start(x_t[u][:], t["x"][bass.ts(n, P), :]).then_inc(x_in[u], 16)

                pairs(sp, pair)

            @block.tensor
            def _(pe):
                pe.wait_ge(w_ready, 16)

                def pair(i, c):
                    for u in range(2):
                        n = 2 * i + u
                        pe.wait_ge(a_in[u], 32 * (i + 1))
                        wait(pe, kept, n - 1)
                        for half in range(2):
                            for k in range(KD):
                                last = pe.matmul(acc[u][:, half * BANK:(half + 1) * BANK], a_t[u][:, k, :],
                                                 w_o[:, k, half * BANK:(half + 1) * BANK], start=(k == 0), stop=(k == KD - 1))
                        last.then_inc(full, 1)

                pairs(pe, pair)

            @block.vector
            def _(dve):
                dve.wait_ge(gate_in, 32)

                def pair(i, c):
                    for u in range(2):
                        n = 2 * i + u
                        dve.wait_ge(full, n + 1)
                        wait(dve, y_out[u], 16 * i)
                        dve.tensor_tensor(y_t[u][:], acc[u][:], gate[:, c, :], ALU.mult).then_inc(kept, 1)
                        dve.wait_ge(kept, n + 1)
                        dve.wait_ge(x_in[u], 16 * (i + 1))
                        dve.tensor_tensor(y_t[u][:], y_t[u][:], x_t[u][:], ALU.add).then_inc(y_ready, 1)

                pairs(dve, pair)

            @block.scalar
            def _(act):
                def pair(i, c):
                    out = t["x1"][c]
                    for u in range(2):
                        act.wait_ge(y_ready, 2 * i + u + 1)
                        act.dma_start(out[bass.ts(2 * (i - c) + u, P), :], y_t[u][:]).then_inc(y_out[u], 16)

                pairs(act, pair)
                for u in range(2):
                    act.wait_ge(y_out[u], 16 * NT // 2)


def route(nc, t, per, layer):
    with Stage(nc, f"route{layer}") as s:
        w_r = s.sb("w_r", [P, KD, NE])
        eps = s.sb("eps", [P, 1])
        x_t = [s.sb(f"x{u}", [P, D]) for u in range(2)]
        xh = [s.sb(f"xh{u}", [P, D]) for u in range(2)]
        junk = s.sb("junk", [P, D])
        ms, rt = [s.sb(f"ms{u}", [P, 1]) for u in range(2)], [s.sb(f"rt{u}", [P, 1]) for u in range(2)]
        h_t = s.sb("h_t", [P, KD, P])
        logits = s.sb("logits", [P, NT, NE])
        top, den = s.sb("top", [P, NT]), s.sb("den", [P, NT])
        aff = s.sb("aff", [NE, TOK])
        left = s.sb("left", [NE, DEC])
        best = {c: s.sb(f"best{c}", [NE, cap]) for c, cap in ((0, CAP_P), (1, CAP_S))}
        at = {c: s.sb(f"at{c}", [NE, cap], U32) for c, cap in ((0, CAP_P), (1, CAP_S))}
        at_f = {c: s.sb(f"at_f{c}", [NE, cap]) for c, cap in ((0, CAP_P), (1, CAP_S))}
        tp = [s.ps(f"tp{b}") for b in range(2)]
        lg = s.ps("lg")
        wide = s.ps("wide", 3)
        w_ready, x_in, ms_ready, xh_ready = s.sem("w_ready"), s.sems("x_in", 2), s.sem("ms_ready"), s.sem("xh_ready")
        xh_out, tp_full, tp_kept, h_ready = s.sems("xh_out", 2), s.sem("tp_full"), s.sem("tp_kept"), s.sem("h_ready")
        lg_full, lg_kept, shifted, raised = s.sem("lg_full"), s.sem("lg_kept"), s.sem("shifted"), s.sem("raised")
        aff_ready, wide_full, best_ready, cols_full = s.sem("aff_ready"), s.sem("wide_full"), s.sem("best_ready"), s.sem("cols_full")
        a_chain, chain = s.sem("a_chain"), s.sem("chain")

        def pairs(eng, body, ch=None, per_turn=0):
            body(0, 0)
            if ch:
                with ch.over(NT // 2 - 1, per_turn) as j:
                    body(j + 1, 1)
            else:
                with eng.Fori(1, NT // 2) as i:
                    body(i, 1)

        with nc.Block() as block:

            @block.sync
            def _(sp):
                sp.dma_start(w_r[:], t[f"w_router_l{layer}"].rearrange("(k p) e -> p k e", p=P)).then_inc(w_ready, 16)

                def pair(i, c):
                    for u in range(2):
                        wait(sp, xh_ready, 2 * i + u - 1)
                        sp.dma_start(x_t[u][:], t["x1"][c][bass.ts(2 * (i - c) + u, P), :]).then_inc(x_in[u], 16)

                pairs(sp, pair)

            @block.gpsimd
            def _(pool):
                def pair(i, c):
                    for u in range(2):
                        pool.wait_ge(xh_ready, 2 * i + u + 1)
                        pool.dma_start(t["xh"][c][bass.ts(2 * (i - c) + u, P), :], xh[u][:]).then_inc(xh_out[u], 16)

                pairs(pool, pair)
                for u in range(2):
                    pool.wait_ge(xh_out[u], 16 * NT // 2)

            @block.scalar
            def _(act):
                ch = Chain(act, a_chain)
                act.wait_ge(chain, 1)

                def pair(i, c):
                    for u in range(2):
                        n = 2 * i + u
                        act.wait_ge(x_in[u], 16 * (i + 1))
                        if c:
                            act.wait_ge(xh_ready, n - 1)
                        ch.link(act.activation(junk[:], x_t[u][:], ACT.Square, accum_out=ms[u][:]))
                        act.activation(rt[u][:], ms[u][:], ACT.Sqrt, bias=eps[:], scale=1.0 / D).then_inc(ms_ready, 1)

                pairs(act, pair, ch, 2)
                act.wait_ge(shifted, 1)
                flat = logits[:].rearrange("p n e -> p (n e)")
                act.activation(flat, flat, ACT.Exp).then_inc(raised, 1)

            @block.tensor
            def _(pe):
                pe.wait_ge(w_ready, 16)

                def pair(i, c):
                    for u in range(2):
                        n = 2 * i + u
                        pe.wait_ge(xh_ready, n + 1)
                        for b in range(2):
                            wait(pe, tp_kept, 2 * n + b - 1)
                            for j in range(4):
                                k = 4 * b + j
                                last = pe.transpose(tp[b][:, j * P:(j + 1) * P], xh[u][:, k * P:(k + 1) * P], per.ident[:])
                            last.then_inc(tp_full, 1)
                        pe.wait_ge(h_ready, 2 * n + 2)
                        wait(pe, lg_kept, n)
                        for k in range(KD):
                            last = pe.matmul(lg[:, 0:NE], h_t[:, k, :], w_r[:, k, :], start=(k == 0), stop=(k == KD - 1))
                        last.then_inc(lg_full, 1)

                pairs(pe, pair)
                pe.wait_ge(aff_ready, 1)
                for n in range(NT):
                    last = pe.transpose(wide[0:NE, n * P:(n + 1) * P], logits[:, n, :], per.ident[:])
                last.then_inc(wide_full, 1)
                pe.wait_ge(best_ready, 2)
                for m, src in enumerate((at_f[1], best[1], at_f[0], best[0])):
                    cap = src.shape[1]
                    last = pe.transpose(tp[0][0:cap, m * NE:(m + 1) * NE], src[:], per.ident[0:NE, 0:NE])
                last.then_inc(cols_full, 1)

            @block.vector
            def _(dve):
                ch = Chain(dve, chain)
                ch.link(dve.memset(eps[:], EPS))

                def pair(i, c):
                    for u in range(2):
                        n = 2 * i + u
                        dve.wait_ge(ms_ready, n + 1)
                        ch.link(dve.reciprocal(rt[u][:], rt[u][:]))
                        wait(dve, xh_out[u], 16 * i)
                        if c:
                            dve.wait_ge(tp_full, 2 * n - 2)
                        dve.tensor_scalar(xh[u][:], x_t[u][:], rt[u][:], None, ALU.mult).then_inc(xh_ready, 1)
                    for u in range(2):
                        n = 2 * i + u
                        for b in range(2):
                            cols = slice(4 * b, 4 * b + 4)
                            dve.wait_ge(tp_full, 2 * n + b + 1)
                            dve.tensor_tensor(h_t[:, cols, :], tp[b][:].rearrange("p (k c) -> p k c", k=4),
                                              per.scale2[:, c, cols].unsqueeze(2).broadcast_to([P, 4, P]), ALU.mult).then_inc(tp_kept, 1)
                            dve.wait_ge(tp_kept, 2 * n + b + 1)
                            dve.tensor_tensor(h_t[:, cols, :], h_t[:, cols, :],
                                              per.shift2[:, c, cols].unsqueeze(2).broadcast_to([P, 4, P]), ALU.add).then_inc(h_ready, 1)
                        dve.wait_ge(lg_full, n + 1)
                        dve.tensor_copy(logits[:, bass.ds(n, 1), :], lg[:, 0:NE].unsqueeze(1)).then_inc(lg_kept, 1)

                pairs(dve, pair, ch, 2)
                dve.wait_ge(lg_kept, NT)
                ch.link(dve.tensor_reduce(top[:], logits[:], AX.X, ALU.max))
                dve.tensor_tensor(logits[:], logits[:], top[:].unsqueeze(2).broadcast_to([P, NT, NE]), ALU.subtract).then_inc(shifted, 1)
                dve.wait_ge(raised, 1)
                ch.link(dve.tensor_reduce(den[:], logits[:], AX.X, ALU.add))
                ch.link(dve.reciprocal(den[:], den[:]))
                dve.tensor_tensor(logits[:], logits[:], den[:].unsqueeze(2).broadcast_to([P, NT, NE]), ALU.mult).then_inc(aff_ready, 1)
                dve.wait_ge(wide_full, 1)
                ch.link(dve.tensor_copy(aff[:], wide[0:NE, 0:TOK]))
                for c, lo, hi, cap in ((0, 0, SEQ, CAP_P), (1, SEQ, TOK, CAP_S)):
                    src = aff[:, lo:hi]
                    for r in range(cap // 8):
                        eight = slice(8 * r, 8 * r + 8)
                        ch.link(dve.max(best[c][:, eight], src))
                        ch.add(dve.max_index(at[c][:, eight], best[c][:, eight], src))
                        ch.add(dve.match_replace(left[:, 0:hi - lo], best[c][:, eight], src, -1.0))
                        ch.settle()
                        src = left[:, 0:hi - lo]
                    dve.tensor_copy(at_f[c][:], at[c][:]).then_inc(best_ready, 1)
                dve.wait_ge(cols_full, 1)
                dve.tensor_copy(per.at_s[:], tp[0][:, 0:NE])
                dve.tensor_copy(per.g_s[:], tp[0][:, NE:2 * NE])
                dve.tensor_copy(per.at_p[:], tp[0][0:CAP_P, 2 * NE:3 * NE])
                dve.tensor_copy(per.g_p[:], tp[0][0:CAP_P, 3 * NE:4 * NE])


def experts(nc, t, per, layer):
    groups = [(0, 3), (3, 6), (6, 8)]
    w_gu = [t[f"{m}_l{layer}"].rearrange("e (k p) f -> p (e k) f", p=P) for m in ("w_gate", "w_up")]
    w_dn = t[f"w_down_l{layer}"].rearrange("e (k p) d -> p (e k) d", p=P)
    with Stage(nc, f"experts{layer}") as s:
        wg = [s.sb(f"wg{u}", [P, KD, FF]) for u in range(2)]
        wu = [s.sb(f"wu{u}", [P, KD, FF]) for u in range(2)]
        wd = [s.sb(f"wd{u}", [P, KF, D]) for u in range(2)]
        scale, shift, gate = (s.sb(m, [P, KD, SLOTS]) for m in ("scale", "shift", "gate"))
        g_s = [s.sb(f"g_s{u}", [P, 1]) for u in range(2)]
        g_p = [s.sb(f"g_p{u}", [CAP_P, 1]) for u in range(2)]
        xs = [s.sb(f"xs{u}", [P, D]) for u in range(2)]
        xp = [s.sb(f"xp{u}", [CAP_P, D]) for u in range(2)]
        h_t = [s.sb(f"h_t{u}", [P, KD, SLOTS]) for u in range(2)]
        act_sb = [s.sb(f"act{b}", [P, SLOTS]) for b in range(2)]
        hid = s.sb("hid", [P, KF, SLOTS])
        y_t = s.sb("y_t", [P, KD, SLOTS])
        ys = [s.sb(f"ys{u}", [P, D]) for u in range(2)]
        yp = [s.sb(f"yp{u}", [CAP_P, D]) for u in range(2)]
        tp = [s.ps(f"tp{b}") for b in range(2)]
        gu = [s.ps(f"gu{b}") for b in range(2)]
        dn = [s.ps(f"dn{b}") for b in range(2)]
        to = [s.ps(f"to{b}") for b in range(2)]
        wgu_in, wd_in = s.sems("wgu_in", 2), s.sems("wd_in", 2)
        spread, g_ready, x_in = s.sem("spread"), s.sem("g_ready"), s.sems("x_in", 2)
        tp_full, tp_kept, h_ready = s.sem("tp_full"), s.sem("tp_kept"), s.sem("h_ready")
        gu_full, silu_ready, hid_ready = s.sem("gu_full"), s.sem("silu_ready"), s.sem("hid_ready")
        dn_full, dn_kept, to_full, to_kept, y_out = s.sem("dn_full"), s.sem("dn_kept"), s.sem("to_full"), s.sem("to_kept"), s.sem("y_out")

        def middle(eng, body):
            body(1, 0, 1)
            body(2, 1, 0)
            with eng.Fori(1, NE // 2 - 1) as i:
                body(2 * i + 1, i, 1)
                body(2 * i + 2, i + 1, 0)

        def turn_bank(u, g):
            return tp[(g + u) % 2]

        def down_bank(u, g):
            return dn[(g + u) % 2]

        with nc.Block() as block:

            @block.sync
            def _(sp):
                def load(e, u):
                    for w, src in ((wg, w_gu[0]), (wu, w_gu[1])):
                        sp.dma_start(w[u][:], src[:, bass.ts(e, KD), :]).then_inc(wgu_in[u], 16)
                    wait(sp, dn_full, 3 * (e - 1))
                    sp.dma_start(wd[u][:], w_dn[:, bass.ts(e, KF), :]).then_inc(wd_in[u], 16)

                load(0, 0)
                load(1, 1)
                with sp.Fori(1, NE // 2) as i:
                    for u in range(2):
                        sp.wait_ge(gu_full, KF * (2 * i + u - 1))
                        load(2 * i + u, u)

            @block.gpsimd
            def _(pool):
                def fetch(e):
                    if e >= 2:
                        pool.wait_ge(tp_full, 3 * (e - 1))
                    for dst, src, at in ((xs, 1, per.at_s), (xp, 0, per.at_p)):
                        pool.indirect_dma_start(dst[e % 2][:], None, t["xh"][src], bass.IndirectOffsetOnAxis(at[:, e:e + 1], 0)).then_inc(x_in[e % 2], 16)
                    if e >= 2:
                        pool.wait_ge(to_kept, 4 * (e - 1))
                    for dst, src in ((g_s, per.g_s), (g_p, per.g_p)):
                        pool.tensor_copy(dst[e % 2][:], src[:, e:e + 1]).then_inc(g_ready, 1)

                def scatter(e):
                    pool.wait_ge(to_kept, 4 * e + 4)
                    if e:
                        pool.wait_ge(y_out, 32 * e)
                    for dst, src, at in ((1, ys, per.at_s), (0, yp, per.at_p)):
                        pool.indirect_dma_start(t["x1"][dst], bass.IndirectOffsetOnAxis(at[:, e:e + 1], 0), src[e % 2][:], None,
                                                compute_op=ALU.add).then_inc(y_out, 16)

                fetch(0)
                for e in range(NE):
                    if e + 1 < NE:
                        fetch(e + 1)
                    scatter(e)
                pool.wait_ge(y_out, 32 * NE)

            @block.tensor
            def _(pe):
                def turns_in(e, i, u):
                    pe.wait_ge(x_in[u], 32 * (i + 1))
                    for g, (lo, hi) in enumerate(groups):
                        wait(pe, tp_kept, 3 * e + g - 1)
                        bank = turn_bank(u, g)
                        for k in range(lo, hi):
                            o = (k - lo) * SLOTS
                            pe.transpose(bank[:, o:o + CAP_S], xs[u][:, k * P:(k + 1) * P], per.ident[:])
                            last = pe.transpose(bank[:, o + CAP_S:o + SLOTS], xp[u][:, k * P:(k + 1) * P], per.ident[0:CAP_P, 0:CAP_P])
                        last.then_inc(tp_full, 1)

                def up_part(e, i, u):
                    pe.wait_ge(wgu_in[u], 32 * (i + 1))
                    pe.wait_ge(h_ready, 3 * e + 3)
                    for j in range(KF):
                        wait(pe, hid_ready, KF * e + j - 1)
                        for m, w in enumerate((wg, wu)):
                            for k in range(KD):
                                last = pe.matmul(gu[j % 2][:, m * SLOTS:(m + 1) * SLOTS], w[u][:, k, j * P:(j + 1) * P],
                                                 h_t[u][:, k, :], start=(k == 0), stop=(k == KD - 1))
                        last.then_inc(gu_full, 1)

                def down_part(e, i, u):
                    pe.wait_ge(wd_in[u], 16 * (i + 1))
                    pe.wait_ge(hid_ready, KF * e + KF)
                    for g, (lo, hi) in enumerate(groups):
                        wait(pe, dn_kept, 3 * e + g - 1)
                        for d in range(lo, hi):
                            for k in range(KF):
                                last = pe.matmul(down_bank(u, g)[:, (d - lo) * SLOTS:(d - lo + 1) * SLOTS], wd[u][:, k, d * P:(d + 1) * P],
                                                 hid[:, k, :], start=(k == 0), stop=(k == KF - 1))
                        last.then_inc(dn_full, 1)

                def turns_out(e, u):
                    pe.wait_ge(dn_kept, 3 * e + 3)
                    for m, (rows, lo) in enumerate(((CAP_S, 0), (CAP_P, CAP_S))):
                        for half in range(2):
                            wait(pe, to_kept, 4 * e + 2 * m + half - 1)
                            for j in range(4):
                                last = pe.transpose(to[half][0:rows, j * P:(j + 1) * P], y_t[:, 4 * half + j, lo:lo + rows], per.ident[:])
                            last.then_inc(to_full, 1)

                turns_in(0, 0, 0)
                up_part(0, 0, 0)
                turns_in(1, 0, 1)
                down_part(0, 0, 0)

                def body(e, j, u):
                    up_part(e, j, u)
                    turns_out(e - 1, 1 - u)
                    turns_in(e + 1, j + u, 1 - u)
                    down_part(e, j, u)

                middle(pe, body)
                up_part(NE - 1, NE // 2 - 1, 1)
                turns_out(NE - 2, 0)
                down_part(NE - 1, NE // 2 - 1, 1)
                turns_out(NE - 1, 1)

            @block.scalar
            def _(act):
                def silu(e):
                    for j in range(KF):
                        act.wait_ge(gu_full, KF * e + j + 1)
                        wait(act, hid_ready, KF * e + j - 1)
                        act.activation(act_sb[j % 2][:], gu[j % 2][:, 0:SLOTS], ACT.Silu).then_inc(silu_ready, 1)

                def rows_out(e, u):
                    wait(act, y_out, 32 * (e - 1))
                    act.wait_ge(g_ready, 2 * e + 2)
                    for m, (rows, dst, g) in enumerate(((CAP_S, ys, g_s), (CAP_P, yp, g_p))):
                        for half in range(2):
                            act.wait_ge(to_full, 4 * e + 2 * m + half + 1)
                            act.activation(dst[u][:, half * BANK:(half + 1) * BANK], to[half][0:rows, :], ACT.Copy,
                                           scale=g[u][:]).then_inc(to_kept, 1)

                silu(0)

                def body(e, j, u):
                    silu(e)
                    rows_out(e - 1, 1 - u)

                middle(act, body)
                silu(NE - 1)
                rows_out(NE - 2, 0)
                rows_out(NE - 1, 1)

            @block.vector
            def _(dve):
                for dst, src in ((scale, per.scale2), (shift, per.shift2), (gate, per.gate2)):
                    for c, lo, hi in ((1, 0, CAP_S), (0, CAP_S, SLOTS)):
                        dve.tensor_copy(dst[:, :, lo:hi], src[:, c, :].unsqueeze(2).broadcast_to([P, KD, hi - lo])).then_inc(spread, 1)
                dve.wait_ge(spread, 6)

                def hidden(e):
                    for j in range(KF):
                        dve.wait_ge(silu_ready, KF * e + j + 1)
                        dve.tensor_tensor(hid[:, j, :], act_sb[j % 2][:], gu[j % 2][:, SLOTS:2 * SLOTS], ALU.mult).then_inc(hid_ready, 1)

                def modulate(e, u):
                    for g, (lo, hi) in enumerate(groups):
                        dve.wait_ge(tp_full, 3 * e + g + 1)
                        dve.tensor_tensor(h_t[u][:, lo:hi, :], turn_bank(u, g)[:, 0:(hi - lo) * SLOTS].rearrange("p (k c) -> p k c", c=SLOTS),
                                          scale[:, lo:hi, :], ALU.mult).then_inc(tp_kept, 1)
                        dve.wait_ge(tp_kept, 3 * e + g + 1)
                        dve.tensor_tensor(h_t[u][:, lo:hi, :], h_t[u][:, lo:hi, :], shift[:, lo:hi, :], ALU.add).then_inc(h_ready, 1)

                def gated(e, u):
                    for g, (lo, hi) in enumerate(groups):
                        dve.wait_ge(dn_full, 3 * e + g + 1)
                        dve.tensor_tensor(y_t[:, lo:hi, :], down_bank(u, g)[:, 0:(hi - lo) * SLOTS].rearrange("p (k c) -> p k c", c=SLOTS),
                                          gate[:, lo:hi, :], ALU.mult).then_inc(dn_kept, 1)

                modulate(0, 0)
                hidden(0)
                modulate(1, 1)
                gated(0, 0)

                def body(e, j, u):
                    hidden(e)
                    modulate(e + 1, 1 - u)
                    gated(e, u)

                middle(dve, body)
                hidden(NE - 1)
                gated(NE - 1, 1)


def fourier(nc, t, per):
    PAIRS = 1 + ST // 2
    HP, HS = SEQ // 2, DEC // 2
    KP, KS = HP + 1, HS + 1
    CE = GROUPS * HG
    with Stage(nc, "fourier") as s:
        x_a, x_b = s.sb("x_a", [P, PAIRS, D]), s.sb("x_b", [P, PAIRS, D])
        w = s.sb("w", [P, GROUPS, 2, D])
        fold = s.sb("fold", [P, 2 * GROUPS * D])
        w_even = fold[:, 0:GROUPS * D].rearrange("p (g e) -> p g e", g=GROUPS)
        w_odd = fold[:, GROUPS * D:2 * GROUPS * D].rearrange("p (g e) -> p g e", g=GROUPS)
        p_t = fold[:, 0:GROUPS * (KP + KS)].rearrange("p (g k) -> p g k", g=GROUPS)
        q_t = fold[:, GROUPS * D:GROUPS * (D + HP + HS)].rearrange("p (g k) -> p g k", g=GROUPS)
        p_mid = s.sb("p_mid", [GROUPS, KP + KS])
        w_mid = s.sb("w_mid", [GROUPS, D])
        h_even, h_odd = s.sb("h_even", [P, PAIRS, CE + GROUPS]), s.sb("h_odd", [P, PAIRS, CE])
        edge = s.sb("edge", [2, 2, CE + GROUPS])
        scale, gate = s.sb("scale", [P, 2, D]), s.sb("gate", [P, 2, D])
        x_mid, gate_mid = s.sb("x_mid", [2, D]), s.sb("gate_mid", [2, D])
        work = s.sb("work", [P, 4, D])
        norm_g, shift_rows = work[:, 1, :], work[0:2, 2:4, :]
        ms, rt, eps = s.sb("ms", [P, PAIRS, 2]), s.sb("rt", [P, PAIRS, 2]), s.sb("eps", [P, 1])
        cos_s, sin_s = s.sb("cos_s", [P, ST // 2, KS]), s.sb("sin_s", [P, ST // 2, HS])
        cos_p, sin_p = s.sb("cos_p", [P, KP]), s.sb("sin_p", [P, HP])
        cos_c, sin_c = s.sb("cos_c", [P, HG]), s.sb("sin_c", [P, HG])
        alt_c, odd_c = s.sb("alt_c", [P, GROUPS, GROUPS]), s.sb("odd_c", [1, HG])
        edge_n = s.sb("edge_n", [2, KP + KS])
        partner = s.sb("partner", [P, PAIRS], U32)
        banks = s.ps("banks", 8)

        w_in, tables_in, x_in, scale_in = s.sem("w_in"), s.sem("tables_in"), s.sems("x_in", PAIRS), s.sem("scale_in")
        shift_in, late_in, mid_in = s.sem("shift_in"), s.sem("late_in"), s.sem("mid_in")
        w_folded, ms_ready, h_ready = s.sem("w_folded"), s.sem("ms_ready"), s.sem("h_ready")
        full, kept = s.sem("full"), s.sem("kept")
        tile_full, odd_kept, tile_used = s.sem("tile_full"), s.sem("odd_kept"), s.sem("tile_used")
        partner_in, far_in = s.sem("partner_in"), s.sems("far_in", PAIRS)
        first_out, far_out = s.sem("first_out"), s.sem("far_out")
        y_ready, y_out, a_chain, chain = s.sem("y_ready"), s.sem("y_out"), s.sem("a_chain"), s.sem("chain")

        def bank(n):
            return banks[:, (n % 8) * BANK:(n % 8 + 1) * BANK]

        def near(x, q):
            return x[0][0:P, :] if q == 0 else x[1][(q - 1) * P:q * P, :]

        def products():
            for half in range(2):
                e = slice(half * BANK, (half + 1) * BANK)
                for g in range(GROUPS):
                    yield [(w[:, g, 0, e], slice(0, BANK), [(cos_c[:], w_even[:, g, e]), (odd_c[:], w_odd[0:1, g, e])])]
                    yield [(w[:, g, 1, e], slice(0, BANK), [(sin_c[:], w_odd[:, g, e])])]
                yield [(w_mid[:, e], slice(0, BANK), [(alt_c[:, g, :], w_even[:, g, e]) for g in range(GROUPS)])]
            for g in range(GROUPS + 1):
                c = slice(g * HG, (g + 1) * HG if g < GROUPS else CE + GROUPS)
                done = [(p_t[:, g, 0:KP] if g < GROUPS else p_mid[:, 0:KP], slice(0, KP),
                         [(h_even[:, 0, c], cos_p[:]), (edge[:, 0, c], edge_n[:, 0:KP])])]
                if g < GROUPS:
                    done.append((q_t[:, g, 0:HP], slice(256, 256 + HP), [(h_odd[:, 0, c], sin_p[:])]))
                yield done
            for g in range(GROUPS + 1):
                c = slice(g * HG, (g + 1) * HG if g < GROUPS else CE + GROUPS)
                for lo, hi in ((0, KS // 2 + 1), (KS // 2 + 1, KS)):
                    yield [(p_t[:, g, KP + lo:KP + hi] if g < GROUPS else p_mid[:, KP + lo:KP + hi], slice(0, hi - lo),
                            [(h_even[:, 1 + j, c], cos_s[:, j, lo:hi]) for j in range(ST // 2)] + [(edge[:, 1, c], edge_n[:, KP + lo:KP + hi])])]
                if g < GROUPS:
                    yield [(q_t[:, g, HP:HP + HS], slice(0, HS), [(h_odd[:, 1 + j, c], sin_s[:, j, :]) for j in range(ST // 2)])]

        N_W, N_PROMPT = 2 * (2 * GROUPS + 1), GROUPS + 1
        N_PRODUCTS = N_W + N_PROMPT + 3 * GROUPS + 2
        OUT = [(0, slice(0, HP), slice(0, HP)), (1, slice(KP, KP + P), slice(HP, HP + P)), (None, slice(HP, KP + KS, KS), None)]
        OUT += [(1 + j, slice(KP + j * P, KP + (j + 1) * P), slice(HP + j * P, HP + (j + 1) * P)) for j in range(1, ST // 2)]

        with nc.Block() as block:

            @block.sync
            def _(sp):
                for g in range(GROUPS):
                    sp.dma_start(w[:, g, :, :], t["w_f_pairs"][g].rearrange("a p e -> p a e")).then_inc(w_in, 16)
                for dst, name in ((cos_c[:], "chan_cos"), (sin_c[:], "chan_sin"), (odd_c[:], "chan_odd"),
                                  (alt_c[:].rearrange("p g a -> p (g a)"), "chan_alt")):
                    sp.dma_start(dst, t[name]).then_inc(w_in, 16)
                for q in range(PAIRS):
                    sp.dma_start(x_a[:, q, :], near(t["x2"], q)).then_inc(x_in[q], 16)
                for dst, name in ((cos_p[:], "pos_cos_p"), (sin_p[:], "pos_sin_p"), (edge_n[:], "pos_edge")):
                    sp.dma_start(dst, t[name]).then_inc(tables_in, 16)
                sp.dma_start(cos_s[:], t["pos_cos_s"].rearrange("(j p) k -> p j k", p=P)).then_inc(tables_in, 16)
                sp.dma_start(sin_s[:], t["pos_sin_s"].rearrange("(j p) k -> p j k", p=P)).then_inc(tables_in, 16)
                for c in range(2):
                    sp.dma_start(gate[:, c, :], t["mod_rows"][c, 2 * D:3 * D].partition_broadcast(P)).then_inc(late_in, 16)
                sp.dma_start(gate_mid[:], t["mod_rows"][:, 2 * D:3 * D]).then_inc(mid_in, 16)
                sp.dma_start(x_mid[0:1, :], t["x2"][0][SEQ // 2:SEQ // 2 + 1, :]).then_inc(mid_in, 16)
                sp.dma_start(x_mid[1:2, :], t["x2"][1][DEC // 2:DEC // 2 + 1, :]).then_inc(mid_in, 16)

                for n, (q, _, _) in enumerate(OUT):
                    sp.wait_ge(y_ready, n + 1)
                    if q is None:
                        sp.wait_ge(first_out, 32)
                        for c, mid in ((0, SEQ // 2), (1, DEC // 2)):
                            sp.dma_start(t["y"][c][mid:mid + 1, :], x_mid[c:c + 1, :]).then_inc(y_out, 16)
                    else:
                        sp.dma_start(near(t["y"], q), x_a[:, q, :]).then_inc(y_out, 16)
                sp.wait_ge(y_out, 16 * (PAIRS + 2))

            @block.gpsimd
            def _(pool):
                pool.dma_start(partner[:], t["partner"]).then_inc(partner_in, 16)
                pool.wait_ge(partner_in, 16)
                for q in range(PAIRS):
                    pool.indirect_dma_start(x_b[:, q, :], None, t["x2"][min(q, 1)], bass.IndirectOffsetOnAxis(partner[:, q:q + 1], 0)).then_inc(far_in[q], 16)
                pool.dma_start(norm_g, t["norm1_l1"].partition_broadcast(P)).then_inc(scale_in, 16)
                for c in range(2):
                    pool.dma_start(scale[:, c, :], t["mod_rows"][c, D:2 * D].partition_broadcast(P)).then_inc(scale_in, 16)
                    pool.dma_start(shift_rows[:, c, :], t["mod_rows"][c, 0:D].partition_broadcast(2)).then_inc(shift_in, 16)
                for n, (q, _, _) in enumerate(OUT):
                    if q is not None:
                        pool.wait_ge(y_ready, n + 1)
                        pool.indirect_dma_start(t["y"][min(q, 1)], bass.IndirectOffsetOnAxis(partner[:, q:q + 1], 0),
                                                x_b[:, q, :], None).then_inc(first_out if q < 2 else far_out, 16)
                pool.wait_ge(far_out, 16 * (PAIRS - 2))

            @block.tensor
            def _(pe):
                pe.wait_ge(w_folded, 2 * GROUPS)
                for n, results in enumerate(products()):
                    if n == N_W:
                        pe.wait_ge(tables_in, 80)
                        pe.wait_ge(h_ready, 1)
                    if n == N_W + N_PROMPT:
                        pe.wait_ge(h_ready, PAIRS)
                    if n >= 8:
                        pe.wait_ge(kept, n - 7)
                    for dst, cols, terms in results:
                        for m, (stationary, moving) in enumerate(terms):
                            last = pe.matmul(bank(n)[0:dst.shape[0], cols], stationary, moving, start=(m == 0), stop=(m == len(terms) - 1))
                    last.then_inc(full, 1)
                pe.wait_ge(kept, N_PRODUCTS)
                for n, (q, ks, qs) in enumerate(OUT):
                    if n >= 2:
                        pe.wait_ge(tile_used, n - 1)
                    m = 2 if q is None else P
                    for half in range(2):
                        e = slice(half * BANK, (half + 1) * BANK)
                        even = bank(4 * n + half)[0:m, :]
                        for g in range(GROUPS):
                            pe.matmul(even, p_t[:, g, ks], w[:, g, 0, e], start=(g == 0), stop=False)
                        last = pe.matmul(even, p_mid[:, ks], w_mid[:, e], start=False, stop=True)
                        if q is not None:
                            for g in range(GROUPS):
                                last = pe.matmul(bank(4 * n + 2 + half), q_t[:, g, qs], w[:, g, 1, e], start=(g == 0), stop=(g == GROUPS - 1))
                    last.then_inc(tile_full, 1)

            @block.scalar
            def _(act):
                ch = Chain(act, a_chain)
                act.wait_ge(chain, 1)

                def move(n, results):
                    act.wait_ge(full, n + 1)
                    for m, (dst, cols, _) in enumerate(results):
                        done = act.activation(dst, bank(n)[0:dst.shape[0], cols], ACT.Copy)
                        if m < len(results) - 1:
                            ch.link(done)
                    done.then_inc(kept, 1)

                results = enumerate(products())
                for q in range(PAIRS):
                    act.wait_ge(x_in[q], 16)
                    act.wait_ge(far_in[q], 16)
                    for side, x in enumerate((x_a, x_b)):
                        ch.link(act.activation(work[:, 0, :], x[:, q, :], ACT.Square, accum_out=ms[:, q, side:side + 1]))
                    act.activation(rt[:, q, :], ms[:, q, :], ACT.Sqrt, bias=eps[:], scale=1.0 / D).then_inc(ms_ready, 1)
                    for _ in range(3):
                        move(*next(results))
                for n, result in results:
                    move(n, result)
                for n, (q, _, _) in enumerate(OUT):
                    if q is not None:
                        act.wait_ge(tile_full, n + 1)
                        if n >= 2:
                            act.wait_ge(tile_used, n - 1)
                        act.activation(work[:, 2 + n % 2, :], banks[:, (4 * n % 8 + 2) * BANK:(4 * n % 8 + 4) * BANK], ACT.Copy).then_inc(odd_kept, 1)

            @block.vector
            def _(dve):
                ch = Chain(dve, chain)

                def columns(x):
                    x = x.rearrange("p (g c) -> p g c", g=GROUPS)
                    return x[:, :, 1:HG], x[:, :, GW - 1:HG:-1], x[:, :, 0:1], x[:, :, HG:HG + 1]

                def fold_even(dst, src):
                    near, far, zero, mid = columns(src)
                    main = dst[:, 0:CE].rearrange("p (g c) -> p g c", g=GROUPS)
                    ch.add(dve.tensor_tensor(main[:, :, 1:HG], near, far, ALU.add))
                    ch.add(dve.tensor_copy(main[:, :, 0:1], zero))
                    ch.add(dve.tensor_copy(dst[:, CE:CE + GROUPS].unsqueeze(2), mid))

                ch.link(dve.memset(eps[:], EPS))
                ch.add(dve.memset(h_odd[:].rearrange("p q (g c) -> p q g c", g=GROUPS)[:, :, :, 0:1], 0.0))
                dve.wait_ge(w_in, 16 * (GROUPS + 4))
                for g in range(GROUPS):
                    dve.tensor_tensor(w_even[:, g, :], w[:, g, 0, :], w[:, g, 1, :], ALU.add).then_inc(w_folded, 1)
                    dve.tensor_tensor(w_odd[:, g, :], w[:, g, 0, :], w[:, g, 1, :], ALU.subtract).then_inc(w_folded, 1)
                dve.wait_ge(scale_in, 48)
                for c in range(2):
                    ch.add(dve.scalar_tensor_tensor(out=scale[:, c, :], in0=scale[:, c, :], scalar=1.0, in1=norm_g, op0=ALU.add, op1=ALU.mult))
                dve.wait_ge(shift_in, 32)
                for c in range(2):
                    fold_even(edge[:, c, :], shift_rows[:, c, :])
                ch.settle()
                for q in range(PAIRS):
                    c = min(q, 1)
                    total, diff, far = work[:, 1, :], work[:, 2, :], work[:, 3, :]
                    dve.wait_ge(ms_ready, q + 1)
                    ch.link(dve.reciprocal(rt[:, q, :], rt[:, q, :]))
                    ch.link(dve.tensor_scalar(far, x_b[:, q, :], rt[:, q, 1:2], None, ALU.mult))
                    for dst, op in ((total, ALU.add), (diff, ALU.subtract)):
                        ch.add(dve.scalar_tensor_tensor(out=dst, in0=x_a[:, q, :], scalar=rt[:, q, 0:1], in1=far, op0=ALU.mult, op1=op))
                    ch.settle()
                    for dst in (total, diff):
                        ch.add(dve.tensor_tensor(dst, dst, scale[:, c, :], ALU.mult))
                    ch.settle()
                    fold_even(h_even[:, q, :], total)
                    if q < 2:
                        fold_even(edge[0:1, c, :], diff[0:1, :])
                    ch.settle()
                    near, back, _, _ = columns(diff)
                    dve.tensor_tensor(h_odd[:, q, :].rearrange("p (g c) -> p g c", g=GROUPS)[:, :, 1:HG], near, back, ALU.subtract).then_inc(h_ready, 1)
                    dve.wait_ge(h_ready, q + 1)

                dve.wait_ge(late_in, 32)
                dve.wait_ge(mid_in, 48)
                for n, (q, _, _) in enumerate(OUT):
                    dve.wait_ge(tile_full, n + 1)
                    if n:
                        dve.wait_ge(y_ready, n)
                    even = banks[:, (4 * n % 8) * BANK:(4 * n % 8 + 2) * BANK]
                    odd = work[:, 2 + n % 2, :]
                    if q is None:
                        dve.tensor_tensor(work[0:2, 0, :], even[0:2, :], gate_mid[:], ALU.mult).then_inc(tile_used, 1)
                        dve.wait_ge(tile_used, n + 1)
                        dve.tensor_tensor(x_mid[:], x_mid[:], work[0:2, 0, :], ALU.add).then_inc(y_ready, 1)
                        continue
                    dve.wait_ge(odd_kept, n + 1 if n < 2 else n)
                    ch.link(dve.tensor_tensor(work[:, 0, :], even, odd, ALU.subtract))
                    dve.tensor_tensor(work[:, 1, :], even, odd, ALU.add).then_inc(tile_used, 1)
                    dve.wait_ge(tile_used, n + 1)
                    for m in range(2):
                        ch.add(dve.tensor_tensor(work[:, m, :], work[:, m, :], gate[:, min(q, 1), :], ALU.mult))
                    ch.settle()
                    ch.link(dve.tensor_tensor(x_a[:, q, :], x_a[:, q, :], work[:, 0, :], ALU.add))
                    dve.tensor_tensor(x_b[:, q, :], x_b[:, q, :], work[:, 1, :], ALU.add).then_inc(y_ready, 1)


def _trunk(nc, t):
    with Stage(nc, "all") as s:
        per = Lasting(s)
        ident_in = s.sem("ident_in")
        with nc.Block() as block:

            @block.sync
            def _(sp):
                sp.dma_start(per.ident[:], t["ident"]).then_inc(ident_in, 16)
                sp.wait_ge(ident_in, 16)

        modulation(nc, t, per, 0)
        projections(nc, t, per)
        attention(nc, t, per, "attn_p", 0, PT, 0, PT)
        attention(nc, t, per, "attn_s", PT, ST, PT, ST + CT)
        mixer_out(nc, t, per)
        route(nc, t, per, 0)
        experts(nc, t, per, 0)
        modulation(nc, t, per, 1)
        last = dict(t, x1=t["y"])
        fourier(nc, t, per)
        route(nc, last, per, 1)
        experts(nc, last, per, 1)


def _tables():
    inv = (np.float32(THETA) ** (-np.arange(0, ROPE // 2, 2, dtype=np.float32) / np.float32(ROPE // 2))).astype(np.float32)
    token = np.arange(DEC)
    angle = np.concatenate([(token // GRID_W).astype(np.float32)[:, None] * inv,
                            (token % GRID_W).astype(np.float32)[:, None] * inv], axis=1)
    rope = np.zeros((KEYT * P, ROPE), np.float32)
    rope[:, 0:ROPE // 2] = 1.0
    rope[SEQ:TOK, 0:ROPE // 2] = np.cos(angle)
    rope[SEQ:TOK, ROPE // 2:] = np.sin(angle)

    def dft(n, wave, rows, cols):
        return wave(2 * np.pi * (np.outer(np.arange(rows), np.arange(cols)) % n) / n) / np.sqrt(n)

    def cos_table(n, cols):
        table = dft(n, np.cos, n // 2, cols)
        table[0, 1::2] = 0.0
        return table

    def edge_table(n):
        table = np.zeros((2, n // 2 + 1))
        table[0, 1::2] = n ** -0.5
        table[1, 0] = n ** 0.5
        return table

    alt = np.zeros((HG, GROUPS, GROUPS))
    for g in range(GROUPS):
        alt[:, g, g] = (-1.0) ** np.arange(HG) / np.sqrt(GW)
    tables = dict(ident=np.eye(P), rope=rope,
                  pos_cos_p=cos_table(SEQ, SEQ // 2 + 1), pos_sin_p=dft(SEQ, np.sin, SEQ // 2, SEQ // 2),
                  pos_cos_s=cos_table(DEC, DEC // 2 + 1), pos_sin_s=dft(DEC, np.sin, DEC // 2, DEC // 2),
                  pos_edge=np.concatenate([edge_table(SEQ), edge_table(DEC)], axis=1),
                  chan_cos=cos_table(GW, HG), chan_sin=dft(GW, np.sin, HG, HG),
                  chan_odd=edge_table(GW)[0:1, 0:HG], chan_alt=alt.reshape(HG, GROUPS * GROUPS))
    tables = {name: np.ascontiguousarray(a, dtype=np.float32) for name, a in tables.items()}
    slot = np.arange(P)[:, None]
    partner = np.concatenate([SEQ - slot] + [DEC - j * P - slot for j in range(ST // 2)], axis=1)
    partner[0, 0:2] = SEQ // 2, DEC // 2
    tables["partner"] = partner.astype(np.uint32)
    return tables


_PLAIN = ["norm1_l0", "norm2_l0", "w_mod_l0", "b_mod_l0", "w_in_l0", "q_a_norm_l0", "w_q_up_l0", "q_norm_l0",
          "kv_a_norm_l0", "w_kv_up_l0", "k_norm_l0", "conv_w_l0", "w_o_l0", "w_router_l0", "w_gate_l0", "w_up_l0",
          "w_down_l0", "norm1_l1", "norm2_l1", "w_mod_l1", "b_mod_l1", "w_router_l1", "w_gate_l1", "w_up_l1", "w_down_l1"]
_SCRATCH = dict(mod_rows=[2, 3 * D], state=[TOK, KVL + ROPE], qt=[NT * QK, HEADS * P], kt=[KEYT * QK, HEADS * P],
                v=[KEYT * P, HEADS * VH], conv=[CJ, P, TOK], attn=[TOK, HEADS * VH],
                x_prompt_1=[SEQ, D], x_sample_1=[DEC, D], xh_prompt=[SEQ, D], xh_sample=[DEC, D])
_OUTPUTS = dict(y_prompt=[SEQ, D], y_sample=[DEC, D], new_c_kv=[SEQ, KVL], new_k_rope=[SEQ, ROPE])


def _layout(inputs):
    w_f = inputs["w_f_l1"].reshape(GROUPS, GW, D)
    partner = np.concatenate([[HG], np.arange(GW - 1, HG, -1)])
    arrays = {name: inputs[name] for name in _PLAIN}
    arrays["x"] = np.concatenate([inputs["x_prompt"][0], inputs["x_sample"][0]])
    arrays["cond"] = np.concatenate([inputs["c_ctx"].reshape(KD, P), inputs["c"].reshape(KD, P)])
    arrays["cache_c_kv_l0"] = inputs["cache_c_kv_l0"][0]
    arrays["cache_k_rope_l0"] = inputs["cache_k_rope_l0"][0]
    arrays["w_f_pairs"] = np.stack([w_f[:, 0:HG], w_f[:, partner]], axis=1)
    return arrays


def kernel(**inputs):
    import concourse.bacc as bacc
    from concourse.bass_utils import run_bass_kernel_spmd

    inputs = {name: np.asarray(a) for name, a in inputs.items()}
    arrays = {name: np.ascontiguousarray(a) for name, a in {**_layout(inputs), **_tables()}.items()}
    nc = bacc.Bacc("TRN2", target_bir_lowering=False, num_devices=1)
    t = {name: nc.dram_tensor(name, list(a.shape), mybir.dt.from_np(a.dtype), kind="ExternalInput").ap() for name, a in arrays.items()}
    t.update({name: nc.dram_tensor(name, shape, F32, kind="Internal").ap() for name, shape in _SCRATCH.items()})
    t.update({name: nc.dram_tensor(name, shape, F32, kind="ExternalOutput").ap() for name, shape in _OUTPUTS.items()})
    t["x1"] = t["x2"] = (t["x_prompt_1"], t["x_sample_1"])
    t["xh"] = (t["xh_prompt"], t["xh_sample"])
    t["y"] = (t["y_prompt"], t["y_sample"])
    _trunk(nc, t)
    out = run_bass_kernel_spmd(nc, [arrays], core_ids=[0]).results[0]
    return (out["y_prompt"][None], out["y_sample"][None], out["new_c_kv"][None], out["new_k_rope"][None])
```

```python
from contextlib import ExitStack, contextmanager

import numpy as np

import concourse.bass as bass
from concourse import mybir

F32 = mybir.dt.float32
F32R = mybir.dt.float32r
U32 = mybir.dt.uint32
ALU = mybir.AluOpType
ACT = mybir.ActivationFunctionType
AX = mybir.AxisListType

P = 128
D = 1024
KD = D // P
SEQ, DEC, PAST = 256, 1024, 256
TOK = SEQ + DEC
NT = TOK // P
PT, ST, CT = SEQ // P, DEC // P, PAST // P
KEYT = NT + CT
HEADS, NOPE, ROPE, VH = 8, 64, 32, 64
QK = NOPE + ROPE
QL, KVL = 384, 256
LAT = QL + KVL + ROPE
CONV = 512
CJ = CONV // P
IN0 = LAT + 3 * CONV
NE, FF = 16, 512
KF = FF // P
CAP_S, CAP_P = 2 * DEC // NE, 2 * SEQ // NE
SLOTS = CAP_S + CAP_P
GROUPS = 4
GW = D // GROUPS
HG = GW // 2
EPS = 1e-6
GRID_W = 64
THETA = 10000.0
MOD = 6 * D
BANK = 512


class Chain:

    def __init__(self, eng, sem):
        self.eng, self.sem, self.base, self.n = eng, sem, 0, 0

    def add(self, instruction):
        instruction.then_inc(self.sem, 1)
        self.n += 1

    def settle(self):
        self.eng.wait_ge(self.sem, self.base + self.n)

    def link(self, instruction):
        self.add(instruction)
        self.settle()

    @contextmanager
    def over(self, count, per):
        start = self.base + self.n
        with self.eng.Fori(0, count) as i:
            self.base, self.n = start + i * per, 0
            yield i
            assert self.n == per, f"{self.n} links in the loop, {per} said"
        self.base, self.n = start + count * per, 0


class Lasting:

    def __init__(self, s):
        self.ident = s.sb("ident", [P, P])
        self.scale1, self.shift1 = s.sb("scale1", [P, NT // 2, KD]), s.sb("shift1", [P, NT // 2, KD])
        self.scale2, self.shift2, self.gate2 = ([s.sb(f"{name}_l{layer}", [P, 2, KD]) for layer in range(2)]
                                                for name in ("scale2", "shift2", "gate2"))
        self.at_s, self.at_p = s.sb("at_s", [P, NE], U32), s.sb("at_p", [CAP_P, NE], U32)
        self.g_s, self.g_p = s.sb("g_s", [P, NE]), s.sb("g_p", [CAP_P, NE])


def wait(eng, sem, value):
    if not isinstance(value, int) or value > 0:
        eng.wait_ge(sem, value)


def turns(eng, count, body, ch=None, per=0):
    body(0)
    if count > 1:
        with (ch.over(count - 1, per) if ch else eng.Fori(0, count - 1)) as i:
            body(i + 1)


class Stage:

    def __init__(self, nc, name):
        self.nc, self.name, self.stack, self.own = nc, name, ExitStack(), []

    def __enter__(self):
        self.stack.__enter__()
        return self

    def __exit__(self, *a):
        self.nc.clear_and_free_semaphores(self.own)
        self.nc.all_engine_barrier()
        return self.stack.__exit__(*a)

    def sb(self, name, shape, dt=F32):
        return self.stack.enter_context(self.nc.sbuf_tensor(f"{self.name}_{name}", shape, dt))

    def ps(self, name, banks=1):
        return self.stack.enter_context(self.nc.psum_tensor(f"{self.name}_{name}", [P, banks * BANK], F32))

    def sem(self, name):
        self.own.append(self.nc.alloc_semaphore(f"{self.name}_{name}"))
        return self.own[-1]

    def sems(self, name, n):
        return [self.sem(f"{name}{k}") for k in range(n)]


class Modulation:
    CH, NB, Q = 512, 2, 4

    def __init__(self, nc, s, t, per, layer, first, end):
        self.t, self.per, self.layer, self.first, self.end = t, per, layer, first, end
        self.w_mod = t[f"w_mod_l{layer}"].rearrange("(k p) f -> p k f", p=P)
        self.rows = s.sb("mod_in", [2 * KD, 2, P])
        self.cond, self.gains, self.pick = s.sb("cond", [P, KD, 2]), s.sb("gains", [P, 2, KD]), s.sb("pick", [P, 2])
        self.mrow = s.sb("mrow", [2, (end - first) * self.CH])
        self.mcol = s.sb("mcol", [P, (end - first) * self.CH // P, 2])
        self.w = [s.sb(f"w_mod{b}", [P, KD, self.CH]) for b in range(self.NB)]
        self.parts = [s.sb(f"parts{b}", [P, self.CH]) for b in range(self.NB)]
        self.sums = [s.sb(f"sums{b}", [2, self.CH]) for b in range(self.NB)]
        self.tp, self.acc, self.total = s.ps("mod_tp"), [s.ps(f"mod_acc{b}") for b in range(self.NB)], s.ps("mod_total")
        self.rows_in, self.w_in = s.sem("rows_in"), s.sems("w_mod_in", self.NB)
        self.turned, self.zeroed, self.gains_kept, self.silu_done = s.sem("turned"), s.sem("zeroed"), s.sem("gains_kept"), s.sem("silu_done")
        self.summed, self.moved, self.added, self.fetched = s.sems("summed", self.NB), s.sems("moved", self.NB), s.sem("added"), s.sem("fetched")
        self.biased, self.columns, self.rows_out = s.sem("biased"), s.sem("columns"), s.sem("rows_out")

    def start_loads(self, sp):
        t, lo = self.t, self.first * self.CH
        sp.dma_start(self.rows[:, 0, :], t["cond"]).then_inc(self.rows_in, 16)
        sp.dma_start(self.rows[0:KD, 1, :], t[f"norm1_l{self.layer}"].rearrange("(k p) -> k p", p=P)).then_inc(self.rows_in, 16)
        sp.dma_start(self.rows[KD:2 * KD, 1, :], t[f"norm2_l{self.layer}"].rearrange("(k p) -> k p", p=P)).then_inc(self.rows_in, 16)
        sp.dma_start(self.pick[:], t["pick"]).then_inc(self.rows_in, 16)
        sp.dma_start(self.mrow[:], t[f"b_mod_l{self.layer}"][lo:self.end * self.CH].partition_broadcast(2)).then_inc(self.rows_in, 16)
        self.load(sp, 0)

    def load(self, sp, i):
        for b in range(self.NB):
            wait(sp, self.summed[b], i)
            sp.dma_start(self.w[b][:], self.w_mod[:, :, bass.ts(self.first + i * self.NB + b, self.CH)]).then_inc(self.w_in[b], 16)

    def loads(self, sp):
        with sp.Fori(1, (self.end - self.first) // self.NB) as i:
            self.load(sp, i)

    def store(self, sp):
        lo, hi = self.first * self.CH, min(self.end * self.CH, 3 * D)
        sp.wait_ge(self.biased, self.end - self.first)
        sp.dma_start(self.t["mod_rows"][:, lo:hi], self.mrow[:, 0:hi - lo]).then_inc(self.rows_out, 16)
        sp.wait_ge(self.rows_out, 16)

    def tensor(self, pe):
        tp, rows = self.tp, self.rows
        pe.wait_ge(self.rows_in, 80)
        pe.transpose(tp[:, 0:2 * KD], rows[:, 0, :], self.per.ident[0:2 * KD, 0:2 * KD])
        pe.transpose(tp[:, 16:16 + 2 * KD], rows[:, 1, :], self.per.ident[0:2 * KD, 0:2 * KD]).then_inc(self.turned, 1)
        pe.wait_ge(self.silu_done, 1)
        pe.wait_ge(self.zeroed, self.NB)

        def products(i):
            for b in range(self.NB):
                n = i * self.NB + b
                pe.wait_ge(self.w_in[b], (i + 1) * 16)
                wait(pe, self.moved[b], i)
                for k in range(KD):
                    q = k % self.Q
                    last = pe.matmul(self.acc[b][32 * q:32 * q + 2, :], self.cond[:, k, :], self.w[b][:, k, :],
                                     start=(k < self.Q), stop=(k >= KD - self.Q), skip_group_check=True)
                last.then_inc(self.summed[b], 1)
                pe.wait_ge(self.moved[b], i + 1)
                wait(pe, self.fetched, n)
                pe.matmul(self.total[0:2, :], self.pick[:], self.parts[b][:], start=True, stop=True).then_inc(self.added, 1)

        turns(pe, (self.end - self.first) // self.NB, products)
        pe.wait_ge(self.biased, self.end - self.first)
        pe.wait_ge(self.gains_kept, 1)
        for j in range((self.end - self.first) * self.CH // P):
            last = pe.transpose(tp[:, 2 * j:2 * j + 2], self.mrow[:, j * P:(j + 1) * P], self.per.ident[0:2, 0:2])
        last.then_inc(self.turned, 1)

    def scalar(self, act):
        act.wait_ge(self.turned, 1)
        act.activation(self.cond[:].rearrange("p k c -> p c k"), self.tp[:, 0:2 * KD].rearrange("p (c k) -> p c k", c=2),
                       ACT.Silu).then_inc(self.silu_done, 1)

        def moves(i):
            for b in range(self.NB):
                n = i * self.NB + b
                act.wait_ge(self.summed[b], i + 1)
                wait(act, self.added, n - 1)
                act.activation(self.parts[b][:], self.acc[b][:], ACT.Copy).then_inc(self.moved[b], 1)
                act.wait_ge(self.added, n + 1)
                wait(act, self.biased, n - 1)
                act.activation(self.sums[b][:], self.total[0:2, :], ACT.Copy).then_inc(self.fetched, 1)

        turns(act, (self.end - self.first) // self.NB, moves)

    def gpsimd(self, pool):
        pool.wait_ge(self.rows_in, 80)

        def bias(i):
            for b in range(self.NB):
                n = i * self.NB + b
                m = self.mrow[:, bass.ts(n, self.CH)]
                pool.wait_ge(self.fetched, n + 1)
                pool.tensor_tensor(m, self.sums[b][:], m, ALU.add).then_inc(self.biased, 1)

        turns(pool, (self.end - self.first) // self.NB, bias)

    def prepare(self, dve):
        for b in range(self.NB):
            dve.memset(self.acc[b][:], 0.0).then_inc(self.zeroed, 1)
        dve.wait_ge(self.silu_done, 1)
        dve.tensor_copy(self.gains[:].rearrange("p c k -> p (c k)"), self.tp[:, 16:16 + 2 * KD]).then_inc(self.gains_kept, 1)

    def vector(self, dve):
        per, gains, layer = self.per, self.gains, self.layer
        dve.wait_ge(self.gains_kept, 1)
        dve.wait_ge(self.turned, 2)
        dve.tensor_copy(self.mcol[:].rearrange("p j c -> p (j c)"), self.tp[:, 0:self.mcol.shape[1] * 2]).then_inc(self.columns, 1)
        dve.wait_ge(self.columns, 1)

        def piece(c, n):
            lo = n * KD - self.first * self.CH // P
            return self.mcol[:, lo:lo + KD, c]

        if self.first == 0 and layer == 0:
            for tile in range(NT // 2):
                c = min(tile, 1)
                dve.scalar_tensor_tensor(out=per.scale1[:, tile, :], in0=piece(c, 1), scalar=1.0,
                                         in1=gains[:, 0, :], op0=ALU.add, op1=ALU.mult)
                dve.tensor_copy(per.shift1[:, tile, :], piece(c, 0))
        if self.end == MOD // self.CH:
            for c in range(2):
                dve.scalar_tensor_tensor(out=per.scale2[layer][:, c, :], in0=piece(c, 4), scalar=1.0,
                                         in1=gains[:, 1, :], op0=ALU.add, op1=ALU.mult)
                dve.tensor_copy(per.shift2[layer][:, c, :], piece(c, 3))
                dve.tensor_copy(per.gate2[layer][:, c, :], piece(c, 5))


def first_modulation(nc, t, per):
    with Stage(nc, "mod0") as s:
        mod = Modulation(nc, s, t, per, 0, 0, 2 * D // Modulation.CH)
        with nc.Block() as block:

            @block.sync
            def _(sp):
                mod.start_loads(sp)
                mod.loads(sp)

            @block.tensor
            def _(pe):
                mod.tensor(pe)

            @block.scalar
            def _(act):
                mod.scalar(act)

            @block.gpsimd
            def _(pool):
                mod.gpsimd(pool)

            @block.vector
            def _(dve):
                mod.prepare(dve)
                mod.vector(dve)
def projections(nc, t, per):
    TP = 4
    HALF = NT // 2 - 1
    with Stage(nc, "proj") as s:
        w_in = s.sb("w_in", [P, KD, IN0])
        w_q = s.sb("w_q", [P, QL // P, HEADS * QK])
        w_kv = s.sb("w_kv", [P, KVL // P, HEADS * 2 * VH])
        conv_w = s.sb("conv_w", [P, 3 * CJ])
        conv_rows = s.sb("conv_rows", [3 * CJ, P])
        lat_gain = s.sb("lat_gain", [P, QL + KVL])
        q_gain, k_gain = s.sb("q_gain", [P, QK]), s.sb("k_gain", [P, QK])
        eps = s.sb("eps", [P, 1])
        x_t = [s.sb(f"x{u}", [P, D]) for u in range(2)]
        rope_t = s.sb("rope", [P, 2, ROPE // 2])
        junk = s.sb("junk", [P, D])
        xh = s.sb("xh", [P, D])
        h_t = s.sb("h_t", [P, KD, P])
        ms, rstd = s.sb("ms", [P, 1]), s.sb("rstd", [P, 1])
        lms, lrstd = s.sb("lms", [P, 2]), s.sb("lrstd", [P, 2])
        lat = [s.sb(f"lat{u}", [P, LAT]) for u in range(2)]
        lat_t = s.sb("lat_t", [P, (QL + KVL) // P, P])
        q_sq, k_sq = s.sb("q_sq", [P, HEADS, QK]), s.sb("k_sq", [P, HEADS, QK])
        q_n, k_n = s.sb("q_n", [P, HEADS, QK]), s.sb("k_n", [P, HEADS, QK])
        q_ms, k_ms = s.sb("q_ms", [P, 2, HEADS]), s.sb("k_ms", [P, 2, HEADS])
        turn = s.sb("turn", [P, 4, HEADS, ROPE // 2])
        gate_b = s.sb("gate_b", [P, CJ, TOK])
        taps = s.sb("taps", [P, TOK])
        q_out = s.sb("q_out", [QK, HEADS * P])
        k_out = s.sb("k_out", [QK, HEADS * P])
        v_out = s.sb("v_out", [P, HEADS * VH])
        u_sb = s.sb("u_sb", [P, CJ * P])
        gated = s.sb("gated", [P, CJ, TOK])

        tp = [s.ps(f"tp{b}") for b in range(2)]
        lp = s.ps("lp", 2)
        up = s.ps("up", 2)
        cv = [s.ps(f"cv{b}") for b in range(2)]

        w_ready, gains_in, conv_in = s.sem("w_ready"), s.sem("gains_in"), s.sem("conv_in")
        x_in, rope_in = s.sems("x_in", 2), s.sem("rope_in")
        ms_ready, x_ready, h_ready = s.sem("ms_ready"), s.sem("x_ready"), s.sem("h_ready")
        tp_full, tp_free = s.sems("tp_full", 2), s.sems("tp_free", 2)
        lp_full, kv_kept = s.sem("lp_full"), s.sem("kv_kept")
        lms_ready, lat_ready, lat_in = s.sem("lms_ready"), s.sem("lat_ready"), s.sem("lat_in")
        up_full, up_free = s.sem("up_full"), s.sem("up_free")
        q_sq_ready, q_sum, q_ms_ready = s.sem("q_sq_ready"), s.sem("q_sum"), s.sem("q_ms_ready")
        k_sq_ready, k_sum, k_ms_ready = s.sem("k_sq_ready"), s.sem("k_sum"), s.sem("k_ms_ready")
        q_ready, k_ready = s.sem("q_ready"), s.sem("k_ready")
        q_stored, k_stored, v_stored = s.sem("q_stored"), s.sem("k_stored"), s.sem("v_stored")
        lat_stored = s.sems("lat_stored", 2)
        u_full, c_full, b_full = s.sem("u_full"), s.sem("c_full"), s.sem("b_full")
        u_kept, c_kept, b_kept = s.sem("u_kept"), s.sem("c_kept"), s.sem("b_kept")
        taps_full, taps_kept, mixed = s.sem("taps_full"), s.sem("taps_kept"), s.sem("mixed")
        late_out, a_chain, v_chain = s.sem("late_out"), s.sem("a_chain"), s.sem("v_chain")

        def tiles(eng, body, ch=None, per_turn=0):
            def pair(i):
                body(2 * i, i, 0, True)
                body(2 * i + 1, i, 1, True)

            turns(eng, HALF, pair, ch, per_turn)
            body(NT - 2, HALF, 0, True)
            body(NT - 1, HALF, 1, False)

        with nc.Block() as block:

            @block.sync
            def _(sp):
                w_in_d = t["w_in_l0"].rearrange("(k p) f -> p k f", p=P)
                sp.dma_start(w_in[:, :, 0:LAT], w_in_d[:, :, 0:LAT]).then_inc(w_ready, 16)
                sp.dma_start(lat_gain[:, 0:QL], t["q_a_norm_l0"].partition_broadcast(P)).then_inc(gains_in, 16)
                sp.dma_start(lat_gain[:, QL:QL + KVL], t["kv_a_norm_l0"].partition_broadcast(P)).then_inc(gains_in, 16)
                sp.dma_start(q_gain[:], t["q_norm_l0"].partition_broadcast(P)).then_inc(gains_in, 16)
                sp.dma_start(k_gain[:], t["k_norm_l0"].partition_broadcast(P)).then_inc(gains_in, 16)
                sp.dma_start(conv_rows[:], t["conv_w_l0"].rearrange("a (j p) -> (a j) p", p=P)).then_inc(conv_in, 16)
                sp.dma_start(w_in[:, :, LAT:IN0], w_in_d[:, :, LAT:IN0]).then_inc(w_ready, 16)
                sp.dma_start(w_q[:], t["w_q_up_l0"].rearrange("(k p) f -> p k f", p=P)).then_inc(w_ready, 16)
                sp.dma_start(w_kv[:], t["w_kv_up_l0"].rearrange("(k p) f -> p k f", p=P)).then_inc(w_ready, 16)

                def rope_load(n):
                    wait(sp, k_stored, 16 * n)
                    sp.dma_start(rope_t[:].rearrange("p a r -> p (a r)"), t["rope"][bass.ts(n, P), :]).then_inc(rope_in, 16)

                def keys_store(n, tp_use):
                    sp.wait_ge(kv_kept, 2 * n + 2)
                    sp.dma_start(t["v"][bass.ts(n, P), :], v_out[:]).then_inc(v_stored, 16)
                    for b in range(2):
                        sp.wait_ge(tp_free[b], tp_use)
                    sp.dma_start(t["kt"][bass.ts(n, QK), :], k_out[:]).then_inc(k_stored, 16)

                def stores(i):
                    for u in range(2):
                        n = 2 * i + u
                        rope_load(n)
                        sp.wait_ge(lat_ready, 3 * n + 3)
                        sp.dma_start(t["state"][bass.ts(n, P), :], lat[u][:, QL:LAT]).then_inc(lat_stored[u], 16)
                        for b in range(2):
                            sp.wait_ge(tp_free[b], TP * n + 3)
                        sp.dma_start(t["qt"][bass.ts(n, QK), :], q_out[:]).then_inc(q_stored, 16)
                        keys_store(n, TP * n + 4)

                turns(sp, NT // 2, stores)
                for c in range(CT):
                    n = NT + c
                    rope_load(n)
                    sp.wait_ge(lat_stored[c], 16 * NT // 2)
                    sp.dma_start(lat[c][:, QL:QL + KVL], t["cache_c_kv_l0"][c * P:(c + 1) * P, :]).then_inc(lat_in, 16)
                    sp.dma_start(lat[c][:, QL + KVL:LAT], t["cache_k_rope_l0"][c * P:(c + 1) * P, :]).then_inc(lat_in, 16)
                    keys_store(n, TP * NT + 2 * c + 2)
                sp.dma_start(t["new_c_kv"], t["state"][0:SEQ, 0:KVL]).then_inc(late_out, 16)
                sp.dma_start(t["new_k_rope"], t["state"][0:SEQ, KVL:KVL + ROPE]).then_inc(late_out, 16)
                for j in range(CJ):
                    sp.wait_ge(mixed, j + 1)
                    sp.dma_start(t["conv"][j], gate_b[:, j, :]).then_inc(late_out, 16)
                for done, value in ((q_stored, 16 * NT), (k_stored, 16 * KEYT), (v_stored, 16 * KEYT), (late_out, 16 * (2 + CJ))):
                    sp.wait_ge(done, value)

            @block.gpsimd
            def _(pool):
                for u in range(2):
                    pool.dma_start(x_t[u][:], t["x"][u * P:(u + 1) * P, :]).then_inc(x_in[u], 16)
                with pool.Fori(1, NT // 2) as i:
                    for u in range(2):
                        pool.wait_ge(x_ready, 2 * i + u - 1)
                        pool.dma_start(x_t[u][:], t["x"][bass.ts(2 * i + u, P), :]).then_inc(x_in[u], 16)

            @block.tensor
            def _(pe):
                def latent_turns(use, first, u):
                    for b, lo, hi in ((0, first, 4), (1, 4, 5)):
                        pe.wait_ge(tp_free[b], use)
                        for j in range(lo, hi):
                            last = pe.transpose(tp[b][:, (j % 4) * P:(j % 4 + 1) * P], lat[u][:, j * P:(j + 1) * P], per.ident[:])
                        last.then_inc(tp_full[b], 1)

                def kv_up(use):
                    for b in range(2):
                        pe.wait_ge(tp_free[b], use)
                    for half in range(2):
                        for k in range(KVL // P):
                            last = pe.matmul(lp[:, half * BANK:(half + 1) * BANK], lat_t[:, QL // P + k, :],
                                             w_kv[:, k, half * BANK:(half + 1) * BANK], start=(k == 0), stop=(k == KVL // P - 1))
                    last.then_inc(lp_full, 1)

                def head_turns(src, ready, n, use):
                    pe.wait_ge(ready, 2 * n + 2)
                    for b in range(2):
                        pe.wait_ge(tp_free[b], use)
                        for j in range(4):
                            last = pe.transpose(tp[b][0:QK, j * P:(j + 1) * P], src[:, 4 * b + j, :], per.ident[:])
                        last.then_inc(tp_full[b], 1)

                def conv_part(base, bank, full):
                    for j in range(CJ):
                        for k in range(KD):
                            last = pe.matmul(cv[bank][:, j * P:(j + 1) * P], w_in[:, k, base + j * P:base + (j + 1) * P],
                                             h_t[:, k, :], start=(k == 0), stop=(k == KD - 1))
                    last.then_inc(full, 1)

                pe.wait_ge(conv_in, 16)
                pe.transpose(cv[0][:, 0:3 * CJ], conv_rows[:], per.ident[0:3 * CJ, 0:3 * CJ]).then_inc(taps_full, 1)
                pe.wait_ge(taps_kept, 1)

                def pair(i):
                    for u in range(2):
                        n = 2 * i + u
                        pe.wait_ge(x_ready, n + 1)
                        for b in range(2):
                            wait(pe, tp_free[b], TP * n)
                            for j in range(4):
                                k = 4 * b + j
                                last = pe.transpose(tp[b][:, j * P:(j + 1) * P], xh[:, k * P:(k + 1) * P], per.ident[:])
                            last.then_inc(tp_full[b], 1)
                        pe.wait_ge(h_ready, 2 * n + 2)
                        pe.wait_ge(w_ready, 64)
                        wait(pe, kv_kept, 2 * n)
                        for base, lo, hi in ((0, 0, QL), (BANK, QL, LAT)):
                            for k in range(KD):
                                last = pe.matmul(lp[:, base:base + hi - lo], h_t[:, k, :], w_in[:, k, lo:hi],
                                                 start=(k == 0), stop=(k == KD - 1))
                        last.then_inc(lp_full, 1)
                        wait(pe, b_kept, n)
                        conv_part(LAT + 2 * CONV, 0, u_full)
                        pe.wait_ge(lat_ready, 3 * n + 3)
                        latent_turns(TP * n + 1, 0, u)
                        wait(pe, c_kept, n)
                        conv_part(LAT + CONV, 1, c_full)
                        for b in range(2):
                            pe.wait_ge(tp_free[b], TP * n + 2)
                        wait(pe, up_free, n)
                        for lo, hi in ((0, BANK), (BANK, HEADS * QK)):
                            for k in range(QL // P):
                                last = pe.matmul(up[:, lo:hi], lat_t[:, k, :], w_q[:, k, lo:hi],
                                                 start=(k == 0), stop=(k == QL // P - 1))
                        last.then_inc(up_full, 1)
                        kv_up(TP * n + 2)
                        pe.wait_ge(u_kept, n + 1)
                        conv_part(LAT, 0, b_full)
                        head_turns(q_n, q_ready, n, TP * n + 2)
                        head_turns(k_n, k_ready, n, TP * n + 3)

                turns(pe, NT // 2, pair)
                for c in range(CT):
                    pe.wait_ge(lat_in, 32 * (c + 1))
                    latent_turns(TP * NT + 2 * c, QL // P, c)
                    pe.wait_ge(kv_kept, 2 * (NT + c))
                    kv_up(TP * NT + 2 * c + 1)
                    head_turns(k_n, k_ready, NT + c, TP * NT + 2 * c + 1)

            @block.scalar
            def _(act):
                ch = Chain(act, a_chain)

                def x_square(n, i, u):
                    act.wait_ge(x_in[u], 16 * (i + 1))
                    wait(act, x_ready, n)
                    ch.link(act.activation(junk[:], x_t[u][:], ACT.Square, accum_out=ms[:]))
                    act.activation(rstd[:], ms[:], ACT.Sqrt, bias=eps[:], scale=1.0 / D).then_inc(ms_ready, 1)

                def latents_kept(use, first):
                    for b, lo, hi in ((0, first, 4), (1, 4, 5)):
                        act.wait_ge(tp_full[b], use)
                        act.activation(lat_t[:, lo:hi, :].rearrange("p j c -> p (j c)"),
                                       tp[b][:, (lo % 4) * P:(lo % 4 + hi - lo) * P], ACT.Copy).then_inc(tp_free[b], 1)

                def keys_values(n, lp_use, rope_cols):
                    act.wait_ge(lp_full, lp_use)
                    kv = lp[:].rearrange("p (h c) -> p h c", h=HEADS)
                    ch.add(act.activation(k_n[:, :, NOPE:QK], rope_cols.unsqueeze(1).broadcast_to([P, HEADS, ROPE]), ACT.Copy))
                    act.activation(k_n[:, :, 0:NOPE], kv[:, :, 0:NOPE], ACT.Copy).then_inc(kv_kept, 1)
                    wait(act, v_stored, 16 * n)
                    act.activation(v_out[:].rearrange("p (h c) -> p h c", h=HEADS), kv[:, :, NOPE:NOPE + VH], ACT.Copy).then_inc(kv_kept, 1)
                    ch.settle()
                    act.wait_ge(kv_kept, 2 * n + 1)
                    wait(act, k_sum, n)
                    act.activation(k_sq[:], k_n[:], ACT.Square).then_inc(k_sq_ready, 1)

                def root(n, sums, src, ready):
                    act.wait_ge(sums, n + 1)
                    act.activation(src[:, 1, :], src[:, 0, :], ACT.Sqrt, bias=eps[:], scale=1.0 / QK).then_inc(ready, 1)

                def tile(n, i, u, more):
                    if more:
                        x_square(n + 1, i + u, 1 - u)
                    act.wait_ge(lp_full, 2 * n + 1)
                    ch.add(act.activation(junk[:, 0:QL], lp[:, 0:QL], ACT.Square, accum_out=lms[:, 0:1]))
                    ch.settle()
                    ch.link(act.activation(junk[:, 0:KVL], lp[:, BANK:BANK + KVL], ACT.Square, accum_out=lms[:, 1:2]))
                    act.activation(lrstd[:, 0:1], lms[:, 0:1], ACT.Sqrt, bias=eps[:], scale=1.0 / QL).then_inc(lms_ready, 1)
                    act.activation(lrstd[:, 1:2], lms[:, 1:2], ACT.Sqrt, bias=eps[:], scale=1.0 / KVL).then_inc(lms_ready, 1)
                    act.wait_ge(u_full, n + 1)
                    wait(act, c_kept, n)
                    act.activation(u_sb[:], cv[0][:], ACT.Copy).then_inc(u_kept, 1)
                    latents_kept(TP * n + 2, 0)
                    act.wait_ge(up_full, n + 1)
                    act.activation(q_sq[:].rearrange("p h c -> p (h c)"), up[:, 0:HEADS * QK], ACT.Square).then_inc(q_sq_ready, 1)
                    keys_values(n, 2 * n + 2, lat[u][:, QL + KVL:LAT])
                    root(n, q_sum, q_ms, q_ms_ready)
                    root(n, k_sum, k_ms, k_ms_ready)
                    act.wait_ge(b_full, n + 1)
                    act.activation(gate_b[:, :, bass.ts(n, P)], cv[0][:].rearrange("p (j c) -> p j c", j=CJ), ACT.Copy).then_inc(b_kept, 1)
                    wait(act, q_stored, 16 * n)
                    for b in range(2):
                        act.wait_ge(tp_full[b], TP * n + 3)
                        act.activation(q_out[:, b * BANK:(b + 1) * BANK], tp[b][0:QK, :], ACT.Copy).then_inc(tp_free[b], 1)

                act.wait_ge(v_chain, 1)
                x_square(0, 0, 0)
                tiles(act, tile, ch, 2 * 4)
                for c in range(CT):
                    n = NT + c
                    latents_kept(TP * NT + 2 * c + 1, QL // P)
                    keys_values(n, 2 * NT + c + 1, lat[c][:, QL + KVL:LAT])
                    root(n, k_sum, k_ms, k_ms_ready)

            @block.vector
            def _(dve):
                ch = Chain(dve, v_chain)

                def normalise_x(n, u):
                    dve.wait_ge(ms_ready, n + 1)
                    ch.link(dve.reciprocal(rstd[:], rstd[:]))
                    dve.tensor_scalar(xh[:], x_t[u][:], rstd[:], None, ALU.mult).then_inc(x_ready, 1)

                def normalise_heads(src, dst, ms_, ready_in, n, gain, freed, ready):
                    dve.wait_ge(ready_in, n + 1)
                    ch.link(dve.reciprocal(ms_[:, 1, :], ms_[:, 1, :]))
                    first = dve.tensor_tensor(dst[:], src, ms_[:, 1, :].unsqueeze(2).broadcast_to([P, HEADS, QK]), ALU.mult)
                    if freed is None:
                        ch.link(first)
                    else:
                        first.then_inc(freed, 1)
                        dve.wait_ge(freed, n + 1)
                    ch.link(dve.tensor_tensor(dst[:], dst[:], gain[:].unsqueeze(1).broadcast_to([P, HEADS, QK]), ALU.mult))
                    pair = dst[:, :, NOPE:QK].rearrange("p h (r two) -> p h r two", two=2)
                    cos = rope_t[:, 0, :].unsqueeze(1).broadcast_to([P, HEADS, ROPE // 2])
                    sin = rope_t[:, 1, :].unsqueeze(1).broadcast_to([P, HEADS, ROPE // 2])
                    dve.wait_ge(rope_in, 16 * (n + 1))
                    for m, (x, f) in enumerate(((0, cos), (1, sin), (0, sin), (1, cos))):
                        ch.add(dve.tensor_tensor(turn[:, m, :, :], pair[:, :, :, x], f, ALU.mult))
                    ch.settle()
                    dve.tensor_tensor(pair[:, :, :, 0], turn[:, 0, :, :], turn[:, 1, :, :], ALU.subtract).then_inc(ready, 1)
                    dve.tensor_tensor(pair[:, :, :, 1], turn[:, 2, :, :], turn[:, 3, :, :], ALU.add).then_inc(ready, 1)

                def sums(sq, ready_in, n, out, ready):
                    dve.wait_ge(ready_in, n + 1)
                    dve.tensor_reduce(out[:, 0, :], sq[:], AX.X, ALU.add).then_inc(ready, 1)

                def keys_kept(n, use):
                    wait(dve, k_stored, 16 * n)
                    for b in range(2):
                        dve.wait_ge(tp_full[b], use)
                        dve.tensor_copy(k_out[:, b * BANK:(b + 1) * BANK], tp[b][0:QK, :]).then_inc(tp_free[b], 1)

                def tile(n, i, u, more):
                    for b in range(2):
                        dve.wait_ge(tp_full[b], TP * n + 1)
                        cols = slice(4 * b, 4 * b + 4)
                        dve.tensor_tensor(h_t[:, cols, :], tp[b][:].rearrange("p (k c) -> p k c", k=4),
                                          per.scale1[:, i, cols].unsqueeze(2).broadcast_to([P, 4, P]), ALU.mult).then_inc(tp_free[b], 1)
                        dve.wait_ge(tp_free[b], TP * n + 1)
                        dve.tensor_tensor(h_t[:, cols, :], h_t[:, cols, :],
                                          per.shift1[:, i, cols].unsqueeze(2).broadcast_to([P, 4, P]), ALU.add).then_inc(h_ready, 1)
                    if more:
                        normalise_x(n + 1, 1 - u)
                    dve.wait_ge(lms_ready, 2 * n + 2)
                    ch.link(dve.reciprocal(lrstd[:], lrstd[:]))
                    wait(dve, lat_stored[u], 16 * i)
                    dve.scalar_tensor_tensor(out=lat[u][:, 0:QL], in0=lp[:, 0:QL], scalar=lrstd[:, 0:1], in1=lat_gain[:, 0:QL],
                                             op0=ALU.mult, op1=ALU.mult).then_inc(lat_ready, 1)
                    dve.scalar_tensor_tensor(out=lat[u][:, QL:QL + KVL], in0=lp[:, BANK:BANK + KVL], scalar=lrstd[:, 1:2],
                                             in1=lat_gain[:, QL:QL + KVL], op0=ALU.mult, op1=ALU.mult).then_inc(lat_ready, 1)
                    dve.tensor_copy(lat[u][:, QL + KVL:LAT], lp[:, BANK + KVL:BANK + LAT - QL]).then_inc(lat_ready, 1)
                    dve.wait_ge(c_full, n + 1)
                    dve.wait_ge(u_kept, n + 1)
                    dve.tensor_tensor(gated[:, :, bass.ts(n, P)], cv[1][:].rearrange("p (j c) -> p j c", j=CJ),
                                      u_sb[:].rearrange("p (j c) -> p j c", j=CJ), ALU.mult).then_inc(c_kept, 1)
                    sums(q_sq, q_sq_ready, n, q_ms, q_sum)
                    sums(k_sq, k_sq_ready, n, k_ms, k_sum)
                    normalise_heads(up[:, 0:HEADS * QK].rearrange("p (h c) -> p h c", h=HEADS), q_n, q_ms, q_ms_ready, n, q_gain,
                                    up_free, q_ready)
                    dve.wait_ge(q_ready, 2 * n + 2)
                    normalise_heads(k_n[:], k_n, k_ms, k_ms_ready, n, k_gain, None, k_ready)
                    keys_kept(n, TP * n + 4)

                ch.link(dve.memset(eps[:], EPS))
                dve.wait_ge(taps_full, 1)
                dve.tensor_copy(conv_w[:], cv[0][:, 0:3 * CJ]).then_inc(taps_kept, 1)
                dve.wait_ge(gains_in, 64)
                normalise_x(0, 0)
                tiles(dve, tile, ch, 2 * 15)
                for c in range(CT):
                    n = NT + c
                    sums(k_sq, k_sq_ready, n, k_ms, k_sum)
                    normalise_heads(k_n[:], k_n, k_ms, k_ms_ready, n, k_gain, None, k_ready)
                    keys_kept(n, TP * NT + 2 * c + 2)
                dve.wait_ge(b_kept, NT)
                dve.wait_ge(c_kept, NT)
                for j in range(CJ):
                    ch.link(dve.tensor_scalar(taps[:], gated[:, j, :], conv_w[:, CJ + j:CJ + j + 1], None, ALU.mult))
                    for a, shift in ((0, -1), (2, 1)):
                        for lo, hi in ((0, SEQ), (SEQ, TOK)):
                            o = slice(lo + max(0, -shift), hi - max(0, shift))
                            i_ = slice(lo + max(0, shift), hi - max(0, -shift))
                            ch.add(dve.scalar_tensor_tensor(out=taps[:, o], in0=gated[:, j, i_],
                                                            scalar=conv_w[:, a * CJ + j:a * CJ + j + 1], in1=taps[:, o],
                                                            op0=ALU.mult, op1=ALU.add))
                        ch.settle()
                    dve.tensor_tensor(gate_b[:, j, :], gate_b[:, j, :], taps[:], ALU.mult).then_inc(mixed, 1)
                    dve.wait_ge(mixed, j + 1)


def attention(nc, t, per, name, q_first, q_tiles, k_first, nk, rest_of_modulation=False):
    K = nk * P
    SCALE = float(QK) ** -0.5
    PAIRS = q_tiles // 2
    spans = [(lo, min(lo + BANK, K)) for lo in range(0, K, BANK)]
    with Stage(nc, name) as s:
        keys = s.sb("keys", [QK, HEADS, K])
        vals = s.sb("vals", [P, nk, HEADS * VH])
        q_t = [s.sb(f"q{u}", [QK, HEADS * P]) for u in range(2)]
        pr = [s.sb(f"pr{b}", [P, K]) for b in range(2)]
        pr_t = [s.sb(f"pr_t{b}", [P, K]) for b in range(2)]
        top, neg = s.sb("top", [P, 1]), [s.sb(f"neg{b}", [P, 1]) for b in range(2)]
        total, inv = [s.sb(f"total{b}", [P, 1]) for b in range(2)], s.sb("inv", [P, 1])
        o_sb = [s.sb(f"o_sb{u}", [P, HEADS // 2 * P]) for u in range(2)]
        sc = [s.ps(f"sc{b}", len(spans)) for b in range(2)]
        o_ps = [s.ps(f"o{u}") for u in range(2)]

        keys_in, vals_in, q_in, o_out = s.sem("keys_in"), s.sem("vals_in"), s.sems("q_in", 2), s.sems("o_out", 2)
        s_full, neg_ready, p_ready, p_scaled = s.sem("s_full"), s.sem("neg_ready"), s.sem("p_ready"), s.sem("p_scaled")
        t_full, v_kept, a_kept = s.sem("t_full"), s.sem("v_kept"), s.sem("a_kept")
        o_full, o_kept, chain = s.sem("o_full"), s.sem("o_kept"), s.sem("chain")

        def tiles(eng, body, ch=None, per_turn=0):
            if PAIRS > 1:
                body(0, 0, 0, True)
                body(1, 0, 1, True)
            if PAIRS > 2:
                with (ch.over(PAIRS - 2, per_turn) if ch else eng.Fori(0, PAIRS - 2)) as turn:
                    i = turn + 1
                    body(2 * i, i, 0, True)
                    body(2 * i + 1, i, 1, True)
            body(q_tiles - 2, PAIRS - 1, 0, True)
            body(q_tiles - 1, PAIRS - 1, 1, False)

        def count(n, h, less):
            return HEADS * n + h - less

        mod = Modulation(nc, s, t, per, 0, 2 * D // Modulation.CH, MOD // Modulation.CH) if rest_of_modulation else None

        with nc.Block() as block:

            @block.sync
            def _(sp):
                for u in range(2):
                    sp.dma_start(q_t[u][:], t["qt"][(q_first + u) * QK:(q_first + u + 1) * QK, :]).then_inc(q_in[u], 16)
                for m in range(nk):
                    sp.dma_start(keys[:, :, m * P:(m + 1) * P],
                                 t["kt"][(k_first + m) * QK:(k_first + m + 1) * QK, :].rearrange("c (h k) -> c h k", h=HEADS)).then_inc(keys_in, 16)
                sp.dma_start(vals[:], t["v"][k_first * P:(k_first + nk) * P, :].rearrange("(m p) c -> p m c", p=P)).then_inc(vals_in, 16)
                if mod:
                    mod.start_loads(sp)
                    mod.loads(sp)
                    mod.store(sp)

                if PAIRS > 1:
                    with sp.Fori(0, PAIRS - 1) as i:
                        for u in range(2):
                            n = 2 * i + u
                            sp.wait_ge(s_full, HEADS * (n + 1))
                            sp.dma_start(q_t[u][:], t["qt"][bass.ds((q_first + 2 + n) * QK, QK), :]).then_inc(q_in[u], 16)
                            sp.wait_ge(o_kept, n + 1)
                            sp.dma_start(t["attn"][bass.ds((q_first + n) * P, P), :], o_sb[u][:]).then_inc(o_out[u], 16)
                for u in range(2):
                    n = q_tiles - 2 + u
                    sp.wait_ge(o_kept, n + 1)
                    sp.dma_start(t["attn"][(q_first + n) * P:(q_first + n + 1) * P, :], o_sb[u][:]).then_inc(o_out[u], 16)
                for u in range(2):
                    sp.wait_ge(o_out[u], 16 * (q_tiles // 2))

            @block.tensor
            def _(pe):
                def scores(n, h, i, u):
                    if h == 0:
                        pe.wait_ge(q_in[u], 16 * (i + 1))
                    b = h % 2
                    for kept in (v_kept, a_kept) if K > BANK else (v_kept,):
                        wait(pe, kept, count(n, h, 1))
                    for lo, hi in spans:
                        last = pe.matmul(sc[b][:, lo:hi], q_t[u][:, h * P:(h + 1) * P], keys[:, h, lo:hi], start=True, stop=True)
                    last.then_inc(s_full, 1)

                def turns(n, h):
                    pe.wait_ge(p_scaled, HEADS * n + h + 1)
                    for m in range(nk):
                        last = pe.transpose(sc[h % 2][:, m * P:(m + 1) * P], pr[h % 2][:, m * P:(m + 1) * P], per.ident[:])
                    last.then_inc(t_full, 1)

                def mix(n, h, u):
                    for kept in (v_kept, a_kept) if K > BANK else (v_kept,):
                        pe.wait_ge(kept, HEADS * n + h + 1)
                    if h == 0:
                        wait(pe, o_kept, n - 1)
                    lo = 64 * (h % 2)
                    out = o_ps[u][lo:lo + VH, (h // 2) * P:(h // 2 + 1) * P]
                    for m in range(nk):
                        last = pe.matmul(out, vals[:, m, h * VH:(h + 1) * VH], pr_t[h % 2][:, m * P:(m + 1) * P],
                                         start=(m == 0), stop=(m == nk - 1))
                    last.then_inc(o_full, 1)

                def tile(n, i, u, more):
                    for h in range(HEADS):
                        if h < HEADS - 1:
                            scores(n, h + 1, i, u)
                        elif more:
                            scores(n + 1, 0, i + u, 1 - u)
                        turns(n, h)
                        if h:
                            mix(n, h - 1, u)
                    mix(n, HEADS - 1, u)

                pe.wait_ge(keys_in, 16 * nk)
                scores(0, 0, 0, 0)
                pe.wait_ge(vals_in, 16)
                tiles(pe, tile)
                if mod:
                    mod.tensor(pe)

            @block.scalar
            def _(act):
                def exp(n, h):
                    b = h % 2
                    act.wait_ge(neg_ready, HEADS * n + h + 1)
                    wait(act, t_full, count(n, h, 1))
                    act.activation(pr[b][:], sc[b][:, 0:K], ACT.Exp, bias=neg[b][:], scale=SCALE, accum_out=total[b][:]).then_inc(p_ready, 1)

                def tile(n, i, u, more):
                    for h in range(HEADS):
                        b = h % 2
                        if K > BANK:
                            act.wait_ge(t_full, HEADS * n + h + 1)
                            wait(act, o_full, count(n, h, 1))
                            act.activation(pr_t[b][:, BANK:K], sc[b][:, BANK:K], ACT.Copy).then_inc(a_kept, 1)
                        if h < HEADS - 1:
                            exp(n, h + 1)
                        elif more:
                            exp(n + 1, 0)
                    act.wait_ge(o_full, HEADS * (n + 1))
                    wait(act, o_out[u], 16 * i)
                    act.activation(o_sb[u][:], o_ps[u][:], ACT.Copy).then_inc(o_kept, 1)

                exp(0, 0)
                tiles(act, tile)
                if mod:
                    mod.scalar(act)

            @block.gpsimd
            def _(pool):
                if mod:
                    mod.gpsimd(pool)

            @block.vector
            def _(dve):
                ch = Chain(dve, chain)

                def maximum(n, h):
                    b = h % 2
                    dve.wait_ge(s_full, HEADS * n + h + 1)
                    ch.link(dve.tensor_reduce(top[:], sc[b][:, 0:K], AX.X, ALU.max))
                    wait(dve, p_ready, count(n, h, 1))
                    dve.tensor_scalar(neg[b][:], top[:], -SCALE, None, ALU.mult).then_inc(neg_ready, 1)

                def tile(n, i, u, more):
                    for h in range(HEADS):
                        b = h % 2
                        dve.wait_ge(p_ready, HEADS * n + h + 1)
                        ch.link(dve.reciprocal(inv[:], total[b][:]))
                        dve.tensor_scalar(pr[b][:], pr[b][:], inv[:], None, ALU.mult).then_inc(p_scaled, 1)
                        if h < HEADS - 1:
                            maximum(n, h + 1)
                        elif more:
                            maximum(n + 1, 0)
                        dve.wait_ge(t_full, HEADS * n + h + 1)
                        wait(dve, o_full, count(n, h, 1))
                        dve.tensor_copy(pr_t[b][:, 0:min(K, BANK)], sc[b][:, 0:min(K, BANK)]).then_inc(v_kept, 1)

                maximum(0, 0)
                tiles(dve, tile, ch, 2 * 2 * HEADS)
                if mod:
                    mod.prepare(dve)
                    mod.vector(dve)


def mixer_out(nc, t, per):
    with Stage(nc, "out") as s:
        w_o = s.sb("w_o", [P, KD, D])
        gate = s.sb("gate", [P, 2, D])
        a_t = [s.sb(f"a{u}", [P, KD, P]) for u in range(2)]
        x_t = [s.sb(f"x{u}", [P, D]) for u in range(2)]
        y_t = [s.sb(f"y{u}", [P, D]) for u in range(2)]
        acc = [s.ps(f"acc{u}", 2) for u in range(2)]
        w_ready, gate_in, a_in, x_in = s.sem("w_ready"), s.sem("gate_in"), s.sems("a_in", 2), s.sems("x_in", 2)
        full, kept, y_ready, y_out = s.sem("full"), s.sem("kept"), s.sem("y_ready"), s.sems("y_out", 2)

        def pairs(eng, body):
            body(0, 0)
            with eng.Fori(1, NT // 2) as i:
                body(i, 1)

        with nc.Block() as block:

            @block.sync
            def _(sp):
                sp.dma_start(w_o[:], t["w_o_l0"].rearrange("(k p) f -> p k f", p=P)).then_inc(w_ready, 16)
                for c in range(2):
                    sp.dma_start(gate[:, c, :], t["mod_rows"][c, 2 * D:3 * D].partition_broadcast(P)).then_inc(gate_in, 16)

                def pair(i, c):
                    for u in range(2):
                        n = 2 * i + u
                        wait(sp, full, n - 1)
                        sp.dma_start(a_t[u][:, 0:KD // 2, :].rearrange("p k c -> p (k c)"), t["attn"][bass.ts(n, P), :]).then_inc(a_in[u], 16)
                        sp.dma_start(a_t[u][:, KD // 2:KD, :], t["conv"].rearrange("j p n -> p j n")[:, :, bass.ts(n, P)]).then_inc(a_in[u], 16)
                        wait(sp, y_ready, n - 1)
                        sp.dma_start(x_t[u][:], t["x"][bass.ts(n, P), :]).then_inc(x_in[u], 16)

                pairs(sp, pair)

            @block.tensor
            def _(pe):
                pe.wait_ge(w_ready, 16)

                def pair(i, c):
                    for u in range(2):
                        n = 2 * i + u
                        pe.wait_ge(a_in[u], 32 * (i + 1))
                        wait(pe, kept, n - 1)
                        for half in range(2):
                            for k in range(KD):
                                last = pe.matmul(acc[u][:, half * BANK:(half + 1) * BANK], a_t[u][:, k, :],
                                                 w_o[:, k, half * BANK:(half + 1) * BANK], start=(k == 0), stop=(k == KD - 1))
                        last.then_inc(full, 1)

                pairs(pe, pair)

            @block.vector
            def _(dve):
                dve.wait_ge(gate_in, 32)

                def pair(i, c):
                    for u in range(2):
                        n = 2 * i + u
                        dve.wait_ge(full, n + 1)
                        wait(dve, y_out[u], 16 * i)
                        dve.tensor_tensor(y_t[u][:], acc[u][:], gate[:, c, :], ALU.mult).then_inc(kept, 1)
                        dve.wait_ge(kept, n + 1)
                        dve.wait_ge(x_in[u], 16 * (i + 1))
                        dve.tensor_tensor(y_t[u][:], y_t[u][:], x_t[u][:], ALU.add).then_inc(y_ready, 1)

                pairs(dve, pair)

            @block.scalar
            def _(act):
                def pair(i, c):
                    out = t["x1"][c]
                    for u in range(2):
                        act.wait_ge(y_ready, 2 * i + u + 1)
                        act.dma_start(out[bass.ts(2 * (i - c) + u, P), :], y_t[u][:]).then_inc(y_out[u], 16)

                pairs(act, pair)
                for u in range(2):
                    act.wait_ge(y_out[u], 16 * NT // 2)


def route(nc, t, per, layer, weights):
    with Stage(nc, f"route{layer}") as s:
        w_r = s.sb("w_r", [P, KD, NE])
        eps = s.sb("eps", [P, 1])
        x_t = [s.sb(f"x{u}", [P, D]) for u in range(2)]
        xh = [s.sb(f"xh{u}", [P, D]) for u in range(2)]
        junk = s.sb("junk", [P, D])
        ms, rt = [s.sb(f"ms{u}", [P, 1]) for u in range(2)], [s.sb(f"rt{u}", [P, 1]) for u in range(2)]
        h_t = s.sb("h_t", [P, KD, P])
        logits = s.sb("logits", [P, NT, NE])
        top, den = s.sb("top", [P, NT]), s.sb("den", [P, NT])
        aff = s.sb("aff", [NE, TOK])
        left = s.sb("left", [NE, DEC])
        best = {c: s.sb(f"best{c}", [NE, cap]) for c, cap in ((0, CAP_P), (1, CAP_S))}
        at = {c: s.sb(f"at{c}", [NE, cap], U32) for c, cap in ((0, CAP_P), (1, CAP_S))}
        at_f = {c: s.sb(f"at_f{c}", [NE, cap]) for c, cap in ((0, CAP_P), (1, CAP_S))}
        tp = [s.ps(f"tp{b}") for b in range(2)]
        lg = s.ps("lg")
        wide = s.ps("wide")
        mod = Modulation(nc, s, t, per, 1, 0, MOD // Modulation.CH) if layer == 0 else None
        w_ready, x_in, ms_ready, xh_ready = s.sem("w_ready"), s.sems("x_in", 2), s.sem("ms_ready"), s.sem("xh_ready")
        xh_out, tp_full, tp_kept, h_ready = s.sems("xh_out", 2), s.sem("tp_full"), s.sem("tp_kept"), s.sem("h_ready")
        lg_full, lg_kept, shifted, raised = s.sem("lg_full"), s.sem("lg_kept"), s.sem("shifted"), s.sem("raised")
        aff_ready, wide_full, wide_kept, best_ready, cols_full = s.sem("aff_ready"), s.sem("wide_full"), s.sem("wide_kept"), s.sem("best_ready"), s.sem("cols_full")
        a_chain, chain = s.sem("a_chain"), s.sem("chain")

        def pairs(eng, body, ch=None, per_turn=0):
            body(0, 0)
            if ch:
                with ch.over(NT // 2 - 1, per_turn) as j:
                    body(j + 1, 1)
            else:
                with eng.Fori(1, NT // 2) as i:
                    body(i, 1)

        with nc.Block() as block:

            @block.sync
            def _(sp):
                sp.dma_start(w_r[:], t[f"w_router_l{layer}"].rearrange("(k p) e -> p k e", p=P)).then_inc(w_ready, 16)
                if mod:
                    mod.start_loads(sp)

                def pair(i, c):
                    for u in range(2):
                        wait(sp, xh_ready, 2 * i + u - 1)
                        sp.dma_start(x_t[u][:], t["x1"][c][bass.ts(2 * (i - c) + u, P), :]).then_inc(x_in[u], 16)

                pairs(sp, pair)
                weights.load(sp, 0, 0)
                if mod:
                    mod.loads(sp)
                weights.load(sp, 1, 1)
                if mod:
                    mod.store(sp)

            @block.gpsimd
            def _(pool):
                def pair(i, c):
                    for u in range(2):
                        pool.wait_ge(xh_ready, 2 * i + u + 1)
                        pool.dma_start(t["xh"][c][bass.ts(2 * (i - c) + u, P), :], xh[u][:]).then_inc(xh_out[u], 16)

                pairs(pool, pair)
                if mod:
                    mod.gpsimd(pool)
                for u in range(2):
                    pool.wait_ge(xh_out[u], 16 * NT // 2)

            @block.scalar
            def _(act):
                ch = Chain(act, a_chain)
                act.wait_ge(chain, 1)

                def pair(i, c):
                    for u in range(2):
                        n = 2 * i + u
                        act.wait_ge(x_in[u], 16 * (i + 1))
                        if c:
                            act.wait_ge(xh_ready, n - 1)
                        ch.link(act.activation(junk[:], x_t[u][:], ACT.Square, accum_out=ms[u][:]))
                        act.activation(rt[u][:], ms[u][:], ACT.Sqrt, bias=eps[:], scale=1.0 / D).then_inc(ms_ready, 1)

                pairs(act, pair, ch, 2)
                act.wait_ge(shifted, 1)
                flat = logits[:].rearrange("p n e -> p (n e)")
                act.activation(flat, flat, ACT.Exp).then_inc(raised, 1)
                if mod:
                    mod.scalar(act)

            @block.tensor
            def _(pe):
                pe.wait_ge(w_ready, 16)

                def pair(i, c):
                    for u in range(2):
                        n = 2 * i + u
                        pe.wait_ge(xh_ready, n + 1)
                        for b in range(2):
                            wait(pe, tp_kept, 2 * n + b - 1)
                            for j in range(4):
                                k = 4 * b + j
                                last = pe.transpose(tp[b][:, j * P:(j + 1) * P], xh[u][:, k * P:(k + 1) * P], per.ident[:])
                            last.then_inc(tp_full, 1)
                        pe.wait_ge(h_ready, 2 * n + 2)
                        wait(pe, lg_kept, n)
                        for k in range(KD):
                            last = pe.matmul(lg[:, 0:NE], h_t[:, k, :], w_r[:, k, :], start=(k == 0), stop=(k == KD - 1))
                        last.then_inc(lg_full, 1)

                pairs(pe, pair)
                pe.wait_ge(aff_ready, 1)
                for lo in range(0, NT, 4):
                    wait(pe, wide_kept, lo // 4)
                    for n in range(lo, min(lo + 4, NT)):
                        last = pe.transpose(wide[0:NE, (n - lo) * P:(n - lo + 1) * P], logits[:, n, :], per.ident[:])
                    last.then_inc(wide_full, 1)
                if mod:
                    mod.tensor(pe)
                pe.wait_ge(best_ready, 2)
                for m, src in enumerate((at_f[1], best[1], at_f[0], best[0])):
                    cap = src.shape[1]
                    last = pe.transpose(tp[0][0:cap, m * NE:(m + 1) * NE], src[:], per.ident[0:NE, 0:NE])
                last.then_inc(cols_full, 1)

            @block.vector
            def _(dve):
                ch = Chain(dve, chain)
                ch.link(dve.memset(eps[:], EPS))

                def pair(i, c):
                    for u in range(2):
                        n = 2 * i + u
                        dve.wait_ge(ms_ready, n + 1)
                        ch.link(dve.reciprocal(rt[u][:], rt[u][:]))
                        wait(dve, xh_out[u], 16 * i)
                        if c:
                            dve.wait_ge(tp_full, 2 * n - 2)
                        dve.tensor_scalar(xh[u][:], x_t[u][:], rt[u][:], None, ALU.mult).then_inc(xh_ready, 1)
                    for u in range(2):
                        n = 2 * i + u
                        for b in range(2):
                            cols = slice(4 * b, 4 * b + 4)
                            dve.wait_ge(tp_full, 2 * n + b + 1)
                            dve.tensor_tensor(h_t[:, cols, :], tp[b][:].rearrange("p (k c) -> p k c", k=4),
                                              per.scale2[layer][:, c, cols].unsqueeze(2).broadcast_to([P, 4, P]), ALU.mult).then_inc(tp_kept, 1)
                            dve.wait_ge(tp_kept, 2 * n + b + 1)
                            dve.tensor_tensor(h_t[:, cols, :], h_t[:, cols, :],
                                              per.shift2[layer][:, c, cols].unsqueeze(2).broadcast_to([P, 4, P]), ALU.add).then_inc(h_ready, 1)
                        dve.wait_ge(lg_full, n + 1)
                        dve.tensor_copy(logits[:, bass.ds(n, 1), :], lg[:, 0:NE].unsqueeze(1)).then_inc(lg_kept, 1)

                pairs(dve, pair, ch, 2)
                dve.wait_ge(lg_kept, NT)
                ch.link(dve.tensor_reduce(top[:], logits[:], AX.X, ALU.max))
                dve.tensor_tensor(logits[:], logits[:], top[:].unsqueeze(2).broadcast_to([P, NT, NE]), ALU.subtract).then_inc(shifted, 1)
                dve.wait_ge(raised, 1)
                ch.link(dve.tensor_reduce(den[:], logits[:], AX.X, ALU.add))
                ch.link(dve.reciprocal(den[:], den[:]))
                dve.tensor_tensor(logits[:], logits[:], den[:].unsqueeze(2).broadcast_to([P, NT, NE]), ALU.mult).then_inc(aff_ready, 1)
                for m, lo in enumerate(range(0, TOK, BANK)):
                    hi = min(lo + BANK, TOK)
                    dve.wait_ge(wide_full, m + 1)
                    dve.tensor_copy(aff[:, lo:hi], wide[0:NE, 0:hi - lo]).then_inc(wide_kept, 1)
                dve.wait_ge(wide_kept, m + 1)
                if mod:
                    mod.prepare(dve)
                for c, lo, hi, cap in ((0, 0, SEQ, CAP_P), (1, SEQ, TOK, CAP_S)):
                    src = aff[:, lo:hi]
                    for r in range(cap // 8):
                        eight = slice(8 * r, 8 * r + 8)
                        ch.link(dve.max(best[c][:, eight], src))
                        ch.add(dve.max_index(at[c][:, eight], best[c][:, eight], src))
                        ch.add(dve.match_replace(left[:, 0:hi - lo], best[c][:, eight], src, -1.0))
                        ch.settle()
                        src = left[:, 0:hi - lo]
                    dve.tensor_copy(at_f[c][:], at[c][:]).then_inc(best_ready, 1)
                dve.wait_ge(cols_full, 1)
                dve.tensor_copy(per.at_s[:], tp[0][:, 0:NE])
                dve.tensor_copy(per.g_s[:], tp[0][:, NE:2 * NE])
                dve.tensor_copy(per.at_p[:], tp[0][0:CAP_P, 2 * NE:3 * NE])
                dve.tensor_copy(per.g_p[:], tp[0][0:CAP_P, 3 * NE:4 * NE])
                if mod:
                    mod.vector(dve)


class Weights:

    def __init__(self, s, t, layer):
        self.gate, self.up = ([s.sb(f"{m}{u}", [P, KD, FF]) for u in range(2)] for m in ("w_gate", "w_up"))
        self.down = [s.sb(f"w_down{u}", [P, KF, D]) for u in range(2)]
        self.gate_up_in, self.down_in = s.sems("gate_up_in", 2), s.sems("down_in", 2)
        self.gate_d, self.up_d = (t[f"{m}_l{layer}"].rearrange("e (k p) f -> p (e k) f", p=P) for m in ("w_gate", "w_up"))
        self.down_d = t[f"w_down_l{layer}"].rearrange("e (k p) d -> p (e k) d", p=P)

    def load_gate_up(self, eng, e, u):
        for w, src in ((self.gate, self.gate_d), (self.up, self.up_d)):
            eng.dma_start(w[u][:], src[:, bass.ts(e, KD), :]).then_inc(self.gate_up_in[u], 16)

    def load_down(self, eng, e, u):
        eng.dma_start(self.down[u][:], self.down_d[:, bass.ts(e, KF), :]).then_inc(self.down_in[u], 16)

    def load(self, eng, e, u):
        self.load_gate_up(eng, e, u)
        self.load_down(eng, e, u)


def experts(nc, t, per, layer, weights):
    groups = [(0, 3), (3, 6), (6, 8)]
    wg, wu, wd, wgu_in, wd_in = weights.gate, weights.up, weights.down, weights.gate_up_in, weights.down_in
    with Stage(nc, f"experts{layer}") as s:
        scale, shift, gate = (s.sb(m, [P, KD, SLOTS]) for m in ("scale", "shift", "gate"))
        g_s = [s.sb(f"g_s{u}", [P, 1]) for u in range(2)]
        g_p = [s.sb(f"g_p{u}", [CAP_P, 1]) for u in range(2)]
        xs = [s.sb(f"xs{u}", [P, D]) for u in range(2)]
        xp = [s.sb(f"xp{u}", [CAP_P, D]) for u in range(2)]
        h_t = [s.sb(f"h_t{u}", [P, KD, SLOTS]) for u in range(2)]
        act_sb = [s.sb(f"act{b}", [P, SLOTS]) for b in range(2)]
        hid = s.sb("hid", [P, KF, SLOTS])
        y_t = s.sb("y_t", [P, KD, SLOTS])
        ys = [s.sb(f"ys{u}", [P, D]) for u in range(2)]
        yp = [s.sb(f"yp{u}", [CAP_P, D]) for u in range(2)]
        tp = [s.ps(f"tp{b}") for b in range(2)]
        gu = [s.ps(f"gu{b}") for b in range(2)]
        dn = [s.ps(f"dn{b}") for b in range(2)]
        to = [s.ps(f"to{b}") for b in range(2)]
        spread, g_ready, x_in = s.sem("spread"), s.sem("g_ready"), s.sems("x_in", 2)
        tp_full, tp_kept, h_ready = s.sem("tp_full"), s.sem("tp_kept"), s.sem("h_ready")
        gu_full, silu_ready, hid_ready = s.sem("gu_full"), s.sem("silu_ready"), s.sem("hid_ready")
        dn_full, dn_kept, to_full, to_kept, y_out = s.sem("dn_full"), s.sem("dn_kept"), s.sem("to_full"), s.sem("to_kept"), s.sem("y_out")

        def middle(eng, body):
            body(1, 0, 1)
            body(2, 1, 0)
            with eng.Fori(1, NE // 2 - 1) as i:
                body(2 * i + 1, i, 1)
                body(2 * i + 2, i + 1, 0)

        def turn_bank(u, g):
            return tp[(g + u) % 2]

        def down_bank(u, g):
            return dn[(g + u) % 2]

        with nc.Block() as block:

            @block.sync
            def _(sp):
                with sp.Fori(1, NE // 2) as i:
                    for u in range(2):
                        e = 2 * i + u
                        sp.wait_ge(gu_full, KF * (e - 1))
                        weights.load_gate_up(sp, e, u)
                        sp.wait_ge(dn_full, 3 * (e - 1))
                        weights.load_down(sp, e, u)

            @block.gpsimd
            def _(pool):
                def fetch(e):
                    if e >= 2:
                        pool.wait_ge(tp_full, 3 * (e - 1))
                    for dst, src, at in ((xs, 1, per.at_s), (xp, 0, per.at_p)):
                        pool.indirect_dma_start(dst[e % 2][:], None, t["xh"][src], bass.IndirectOffsetOnAxis(at[:, e:e + 1], 0)).then_inc(x_in[e % 2], 16)

                def affinities(e):
                    if e >= 2:
                        pool.wait_ge(to_kept, 4 * (e - 1))
                    for dst, src in ((g_s, per.g_s), (g_p, per.g_p)):
                        pool.tensor_copy(dst[e % 2][:], src[:, e:e + 1]).then_inc(g_ready, 1)

                def scatter(e):
                    pool.wait_ge(to_kept, 4 * e + 4)
                    if e:
                        pool.wait_ge(y_out, 32 * e)
                    for dst, src, at in ((1, ys, per.at_s), (0, yp, per.at_p)):
                        pool.indirect_dma_start(t["x1"][dst], bass.IndirectOffsetOnAxis(at[:, e:e + 1], 0), src[e % 2][:], None,
                                                compute_op=ALU.add).then_inc(y_out, 16)

                fetch(0)
                fetch(1)
                affinities(0)
                for e in range(NE):
                    if e + 2 < NE:
                        fetch(e + 2)
                    if e + 1 < NE:
                        affinities(e + 1)
                    scatter(e)
                pool.wait_ge(y_out, 32 * NE)

            @block.tensor
            def _(pe):
                def turn_in(e, i, u, g):
                    lo, hi = groups[g]
                    if g == 0:
                        pe.wait_ge(x_in[u], 32 * (i + 1))
                    wait(pe, tp_kept, 3 * e + g - 1)
                    bank = turn_bank(u, g)
                    for k in range(lo, hi):
                        o = (k - lo) * SLOTS
                        pe.transpose(bank[:, o:o + CAP_S], xs[u][:, k * P:(k + 1) * P], per.ident[:])
                        last = pe.transpose(bank[:, o + CAP_S:o + SLOTS], xp[u][:, k * P:(k + 1) * P], per.ident[0:CAP_P, 0:CAP_P])
                    last.then_inc(tp_full, 1)

                def up_part(e, i, u, between):
                    pe.wait_ge(wgu_in[u], 32 * (i + 1))
                    pe.wait_ge(h_ready, 3 * e + 3)
                    for j in range(KF):
                        wait(pe, hid_ready, KF * e + j - 1)
                        for m, w in enumerate((wg, wu)):
                            for k in range(KD):
                                last = pe.matmul(gu[j % 2][:, m * SLOTS:(m + 1) * SLOTS], w[u][:, k, j * P:(j + 1) * P],
                                                 h_t[u][:, k, :], start=(k == 0), stop=(k == KD - 1))
                        last.then_inc(gu_full, 1)
                        between(j)

                def down_part(e, i, u):
                    pe.wait_ge(wd_in[u], 16 * (i + 1))
                    pe.wait_ge(hid_ready, KF * e + KF)
                    for g, (lo, hi) in enumerate(groups):
                        wait(pe, dn_kept, 3 * e + g - 1)
                        for d in range(lo, hi):
                            for k in range(KF):
                                last = pe.matmul(down_bank(u, g)[:, (d - lo) * SLOTS:(d - lo + 1) * SLOTS], wd[u][:, k, d * P:(d + 1) * P],
                                                 hid[:, k, :], start=(k == 0), stop=(k == KF - 1))
                        last.then_inc(dn_full, 1)

                def turn_out(e, u, piece):
                    m, half = divmod(piece, 2)
                    rows, lo = ((CAP_S, 0), (CAP_P, CAP_S))[m]
                    if piece == 0:
                        pe.wait_ge(dn_kept, 3 * e + 3)
                    wait(pe, to_kept, 4 * e + piece - 1)
                    for j in range(4):
                        last = pe.transpose(to[half][0:rows, j * P:(j + 1) * P], y_t[:, 4 * half + j, lo:lo + rows], per.ident[:])
                    last.then_inc(to_full, 1)

                def expert(e, i, u):
                    def between(j):
                        if not (isinstance(e, int) and e == 0):
                            turn_out(e - 1, 1 - u, j)
                        if j and not (isinstance(e, int) and e == NE - 1):
                            turn_in(e + 1, i + u, 1 - u, j - 1)

                    up_part(e, i, u, between)
                    down_part(e, i, u)

                for g in range(3):
                    turn_in(0, 0, 0, g)
                expert(0, 0, 0)
                middle(pe, expert)
                expert(NE - 1, NE // 2 - 1, 1)
                for piece in range(4):
                    turn_out(NE - 1, 1, piece)

            @block.scalar
            def _(act):
                def silu(e, j):
                    act.wait_ge(gu_full, KF * e + j + 1)
                    wait(act, hid_ready, KF * e + j - 1)
                    act.activation(act_sb[j % 2][:], gu[j % 2][:, 0:SLOTS], ACT.Silu).then_inc(silu_ready, 1)

                def rows_out(e, u, piece):
                    m, half = divmod(piece, 2)
                    rows, dst, g = ((CAP_S, ys, g_s), (CAP_P, yp, g_p))[m]
                    if piece == 0:
                        wait(act, y_out, 32 * (e - 1))
                        act.wait_ge(g_ready, 2 * e + 2)
                    act.wait_ge(to_full, 4 * e + piece + 1)
                    act.activation(dst[u][:, half * BANK:(half + 1) * BANK], to[half][0:rows, :], ACT.Copy, scale=g[u][:]).then_inc(to_kept, 1)

                def expert(e, i, u):
                    for j in range(KF):
                        silu(e, j)
                        if not (isinstance(e, int) and e == 0):
                            rows_out(e - 1, 1 - u, j)

                expert(0, 0, 0)
                middle(act, expert)
                expert(NE - 1, NE // 2 - 1, 1)
                for piece in range(4):
                    rows_out(NE - 1, 1, piece)

            @block.vector
            def _(dve):
                for dst, src in ((scale, per.scale2[layer]), (shift, per.shift2[layer]), (gate, per.gate2[layer])):
                    for c, lo, hi in ((1, 0, CAP_S), (0, CAP_S, SLOTS)):
                        dve.tensor_copy(dst[:, :, lo:hi], src[:, c, :].unsqueeze(2).broadcast_to([P, KD, hi - lo])).then_inc(spread, 1)
                dve.wait_ge(spread, 6)

                def hidden(e, j):
                    dve.wait_ge(silu_ready, KF * e + j + 1)
                    dve.tensor_tensor(hid[:, j, :], act_sb[j % 2][:], gu[j % 2][:, SLOTS:2 * SLOTS], ALU.mult).then_inc(hid_ready, 1)

                def modulate(e, u, g):
                    lo, hi = groups[g]
                    dve.wait_ge(tp_full, 3 * e + g + 1)
                    dve.tensor_tensor(h_t[u][:, lo:hi, :], turn_bank(u, g)[:, 0:(hi - lo) * SLOTS].rearrange("p (k c) -> p k c", c=SLOTS),
                                      scale[:, lo:hi, :], ALU.mult).then_inc(tp_kept, 1)
                    dve.wait_ge(tp_kept, 3 * e + g + 1)
                    dve.tensor_tensor(h_t[u][:, lo:hi, :], h_t[u][:, lo:hi, :], shift[:, lo:hi, :], ALU.add).then_inc(h_ready, 1)

                def gated(e, u, g):
                    lo, hi = groups[g]
                    dve.wait_ge(dn_full, 3 * e + g + 1)
                    dve.tensor_tensor(y_t[:, lo:hi, :], down_bank(u, g)[:, 0:(hi - lo) * SLOTS].rearrange("p (k c) -> p k c", c=SLOTS),
                                      gate[:, lo:hi, :], ALU.mult).then_inc(dn_kept, 1)

                def expert(e, i, u):
                    for j in range(KF):
                        hidden(e, j)
                        if j and not (isinstance(e, int) and e == NE - 1):
                            modulate(e + 1, 1 - u, j - 1)
                    for g in range(3):
                        gated(e, u, g)

                for g in range(3):
                    modulate(0, 0, g)
                expert(0, 0, 0)
                middle(dve, expert)
                expert(NE - 1, NE // 2 - 1, 1)


def fourier(nc, t, per):
    PAIRS = 1 + ST // 2
    HP, HS = SEQ // 2, DEC // 2
    KP, KS = HP + 1, HS + 1
    CE = GROUPS * HG
    with Stage(nc, "fourier") as s:
        x_a, x_b = s.sb("x_a", [P, PAIRS, D]), s.sb("x_b", [P, PAIRS, D])
        w = s.sb("w", [P, GROUPS, 2, D])
        fold = s.sb("fold", [P, 2 * GROUPS * D])
        w_even = fold[:, 0:GROUPS * D].rearrange("p (g e) -> p g e", g=GROUPS)
        w_odd = fold[:, GROUPS * D:2 * GROUPS * D].rearrange("p (g e) -> p g e", g=GROUPS)
        p_t = fold[:, 0:GROUPS * (KP + KS)].rearrange("p (g k) -> p g k", g=GROUPS)
        q_t = fold[:, GROUPS * D:GROUPS * (D + HP + HS)].rearrange("p (g k) -> p g k", g=GROUPS)
        p_mid = s.sb("p_mid", [GROUPS, KP + KS])
        w_mid = s.sb("w_mid", [GROUPS, D])
        h_even, h_odd = s.sb("h_even", [P, PAIRS, CE + GROUPS]), s.sb("h_odd", [P, PAIRS, CE])
        edge = s.sb("edge", [2, 2, CE + GROUPS])
        scale, gate = s.sb("scale", [P, 2, D]), s.sb("gate", [P, 2, D])
        x_mid, gate_mid = s.sb("x_mid", [2, D]), s.sb("gate_mid", [2, D])
        work = s.sb("work", [P, 4, D])
        norm_g, shift_rows = work[:, 1, :], work[0:2, 2:4, :]
        ms, rt, eps = s.sb("ms", [P, PAIRS, 2]), s.sb("rt", [P, PAIRS, 2]), s.sb("eps", [P, 1])
        cos_s, sin_s = s.sb("cos_s", [P, ST // 2, KS]), s.sb("sin_s", [P, ST // 2, HS])
        cos_p, sin_p = s.sb("cos_p", [P, KP]), s.sb("sin_p", [P, HP])
        cos_c, sin_c = s.sb("cos_c", [P, HG]), s.sb("sin_c", [P, HG])
        alt_c, odd_c = s.sb("alt_c", [P, GROUPS, GROUPS]), s.sb("odd_c", [1, HG])
        edge_n = s.sb("edge_n", [2, KP + KS])
        partner = s.sb("partner", [P, PAIRS], U32)
        banks = s.ps("banks", 8)

        w_in, tables_in, x_in, scale_in = s.sem("w_in"), s.sem("tables_in"), s.sems("x_in", PAIRS), s.sem("scale_in")
        shift_in, late_in, mid_in = s.sem("shift_in"), s.sem("late_in"), s.sem("mid_in")
        w_folded, ms_ready, h_ready = s.sem("w_folded"), s.sem("ms_ready"), s.sem("h_ready")
        full, kept = s.sem("full"), s.sem("kept")
        tile_full, odd_kept, tile_used = s.sem("tile_full"), s.sem("odd_kept"), s.sem("tile_used")
        partner_in, far_in = s.sem("partner_in"), s.sems("far_in", PAIRS)
        first_out, far_out = s.sem("first_out"), s.sem("far_out")
        y_ready, y_out, a_chain, chain = s.sem("y_ready"), s.sem("y_out"), s.sem("a_chain"), s.sem("chain")

        def bank(n):
            return banks[:, (n % 8) * BANK:(n % 8 + 1) * BANK]

        def near(x, q):
            return x[0][0:P, :] if q == 0 else x[1][(q - 1) * P:q * P, :]

        def products():
            for half in range(2):
                e = slice(half * BANK, (half + 1) * BANK)
                for g in range(GROUPS):
                    yield [(w[:, g, 0, e], slice(0, BANK), [(cos_c[:], w_even[:, g, e]), (odd_c[:], w_odd[0:1, g, e])])]
                    yield [(w[:, g, 1, e], slice(0, BANK), [(sin_c[:], w_odd[:, g, e])])]
                yield [(w_mid[:, e], slice(0, BANK), [(alt_c[:, g, :], w_even[:, g, e]) for g in range(GROUPS)])]
            for g in range(GROUPS + 1):
                c = slice(g * HG, (g + 1) * HG if g < GROUPS else CE + GROUPS)
                done = [(p_t[:, g, 0:KP] if g < GROUPS else p_mid[:, 0:KP], slice(0, KP),
                         [(h_even[:, 0, c], cos_p[:]), (edge[:, 0, c], edge_n[:, 0:KP])])]
                if g < GROUPS:
                    done.append((q_t[:, g, 0:HP], slice(256, 256 + HP), [(h_odd[:, 0, c], sin_p[:])]))
                yield done
            for g in range(GROUPS + 1):
                c = slice(g * HG, (g + 1) * HG if g < GROUPS else CE + GROUPS)
                for lo, hi in ((0, KS // 2 + 1), (KS // 2 + 1, KS)):
                    yield [(p_t[:, g, KP + lo:KP + hi] if g < GROUPS else p_mid[:, KP + lo:KP + hi], slice(0, hi - lo),
                            [(h_even[:, 1 + j, c], cos_s[:, j, lo:hi]) for j in range(ST // 2)] + [(edge[:, 1, c], edge_n[:, KP + lo:KP + hi])])]
                if g < GROUPS:
                    yield [(q_t[:, g, HP:HP + HS], slice(0, HS), [(h_odd[:, 1 + j, c], sin_s[:, j, :]) for j in range(ST // 2)])]

        N_W, N_PROMPT = 2 * (2 * GROUPS + 1), GROUPS + 1
        N_PRODUCTS = N_W + N_PROMPT + 3 * GROUPS + 2
        OUT = [(0, slice(0, HP), slice(0, HP)), (1, slice(KP, KP + P), slice(HP, HP + P)), (None, slice(HP, KP + KS, KS), None)]
        OUT += [(1 + j, slice(KP + j * P, KP + (j + 1) * P), slice(HP + j * P, HP + (j + 1) * P)) for j in range(1, ST // 2)]

        with nc.Block() as block:

            @block.sync
            def _(sp):
                for g in range(GROUPS):
                    sp.dma_start(w[:, g, :, :], t["w_f_pairs"][g].rearrange("a p e -> p a e")).then_inc(w_in, 16)
                for dst, name in ((cos_c[:], "chan_cos"), (sin_c[:], "chan_sin"), (odd_c[:], "chan_odd"),
                                  (alt_c[:].rearrange("p g a -> p (g a)"), "chan_alt")):
                    sp.dma_start(dst, t[name]).then_inc(w_in, 16)
                for q in range(PAIRS):
                    sp.dma_start(x_a[:, q, :], near(t["x2"], q)).then_inc(x_in[q], 16)
                for dst, name in ((cos_p[:], "pos_cos_p"), (sin_p[:], "pos_sin_p"), (edge_n[:], "pos_edge")):
                    sp.dma_start(dst, t[name]).then_inc(tables_in, 16)
                sp.dma_start(cos_s[:], t["pos_cos_s"].rearrange("(j p) k -> p j k", p=P)).then_inc(tables_in, 16)
                sp.dma_start(sin_s[:], t["pos_sin_s"].rearrange("(j p) k -> p j k", p=P)).then_inc(tables_in, 16)
                for c in range(2):
                    sp.dma_start(gate[:, c, :], t["mod_rows"][c, 2 * D:3 * D].partition_broadcast(P)).then_inc(late_in, 16)
                sp.dma_start(gate_mid[:], t["mod_rows"][:, 2 * D:3 * D]).then_inc(mid_in, 16)
                sp.dma_start(x_mid[0:1, :], t["x2"][0][SEQ // 2:SEQ // 2 + 1, :]).then_inc(mid_in, 16)
                sp.dma_start(x_mid[1:2, :], t["x2"][1][DEC // 2:DEC // 2 + 1, :]).then_inc(mid_in, 16)

                for n, (q, _, _) in enumerate(OUT):
                    sp.wait_ge(y_ready, n + 1)
                    if q is None:
                        sp.wait_ge(first_out, 32)
                        for c, mid in ((0, SEQ // 2), (1, DEC // 2)):
                            sp.dma_start(t["y"][c][mid:mid + 1, :], x_mid[c:c + 1, :]).then_inc(y_out, 16)
                    else:
                        sp.dma_start(near(t["y"], q), x_a[:, q, :]).then_inc(y_out, 16)
                sp.wait_ge(y_out, 16 * (PAIRS + 2))

            @block.gpsimd
            def _(pool):
                pool.dma_start(partner[:], t["partner"]).then_inc(partner_in, 16)
                pool.wait_ge(partner_in, 16)
                for q in range(PAIRS):
                    pool.indirect_dma_start(x_b[:, q, :], None, t["x2"][min(q, 1)], bass.IndirectOffsetOnAxis(partner[:, q:q + 1], 0)).then_inc(far_in[q], 16)
                pool.dma_start(norm_g, t["norm1_l1"].partition_broadcast(P)).then_inc(scale_in, 16)
                for c in range(2):
                    pool.dma_start(scale[:, c, :], t["mod_rows"][c, D:2 * D].partition_broadcast(P)).then_inc(scale_in, 16)
                    pool.dma_start(shift_rows[:, c, :], t["mod_rows"][c, 0:D].partition_broadcast(2)).then_inc(shift_in, 16)
                for n, (q, _, _) in enumerate(OUT):
                    if q is not None:
                        pool.wait_ge(y_ready, n + 1)
                        pool.indirect_dma_start(t["y"][min(q, 1)], bass.IndirectOffsetOnAxis(partner[:, q:q + 1], 0),
                                                x_b[:, q, :], None).then_inc(first_out if q < 2 else far_out, 16)
                pool.wait_ge(far_out, 16 * (PAIRS - 2))

            @block.tensor
            def _(pe):
                pe.wait_ge(w_folded, 2 * GROUPS)
                for n, results in enumerate(products()):
                    if n == N_W:
                        pe.wait_ge(tables_in, 80)
                        pe.wait_ge(h_ready, 1)
                    if n == N_W + N_PROMPT:
                        pe.wait_ge(h_ready, PAIRS)
                    if n >= 8:
                        pe.wait_ge(kept, n - 7)
                    for dst, cols, terms in results:
                        for m, (stationary, moving) in enumerate(terms):
                            last = pe.matmul(bank(n)[0:dst.shape[0], cols], stationary, moving, start=(m == 0), stop=(m == len(terms) - 1))
                    last.then_inc(full, 1)
                pe.wait_ge(kept, N_PRODUCTS)
                for n, (q, ks, qs) in enumerate(OUT):
                    if n >= 2:
                        pe.wait_ge(tile_used, n - 1)
                    m = 2 if q is None else P
                    for half in range(2):
                        e = slice(half * BANK, (half + 1) * BANK)
                        even = bank(4 * n + half)[0:m, :]
                        for g in range(GROUPS):
                            pe.matmul(even, p_t[:, g, ks], w[:, g, 0, e], start=(g == 0), stop=False)
                        last = pe.matmul(even, p_mid[:, ks], w_mid[:, e], start=False, stop=True)
                        if q is not None:
                            for g in range(GROUPS):
                                last = pe.matmul(bank(4 * n + 2 + half), q_t[:, g, qs], w[:, g, 1, e], start=(g == 0), stop=(g == GROUPS - 1))
                    last.then_inc(tile_full, 1)

            @block.scalar
            def _(act):
                ch = Chain(act, a_chain)
                act.wait_ge(chain, 1)

                def move(n, results):
                    act.wait_ge(full, n + 1)
                    for m, (dst, cols, _) in enumerate(results):
                        done = act.activation(dst, bank(n)[0:dst.shape[0], cols], ACT.Copy)
                        if m < len(results) - 1:
                            ch.link(done)
                    done.then_inc(kept, 1)

                results = enumerate(products())
                for q in range(PAIRS):
                    act.wait_ge(x_in[q], 16)
                    act.wait_ge(far_in[q], 16)
                    for side, x in enumerate((x_a, x_b)):
                        ch.link(act.activation(work[:, 0, :], x[:, q, :], ACT.Square, accum_out=ms[:, q, side:side + 1]))
                    act.activation(rt[:, q, :], ms[:, q, :], ACT.Sqrt, bias=eps[:], scale=1.0 / D).then_inc(ms_ready, 1)
                    for _ in range(3):
                        move(*next(results))
                for n, result in results:
                    move(n, result)
                for n, (q, _, _) in enumerate(OUT):
                    if q is not None:
                        act.wait_ge(tile_full, n + 1)
                        if n >= 2:
                            act.wait_ge(tile_used, n - 1)
                        act.activation(work[:, 2 + n % 2, :], banks[:, (4 * n % 8 + 2) * BANK:(4 * n % 8 + 4) * BANK], ACT.Copy).then_inc(odd_kept, 1)

            @block.vector
            def _(dve):
                ch = Chain(dve, chain)

                def columns(x):
                    x = x.rearrange("p (g c) -> p g c", g=GROUPS)
                    return x[:, :, 1:HG], x[:, :, GW - 1:HG:-1], x[:, :, 0:1], x[:, :, HG:HG + 1]

                def fold_even(dst, src):
                    near, far, zero, mid = columns(src)
                    main = dst[:, 0:CE].rearrange("p (g c) -> p g c", g=GROUPS)
                    ch.add(dve.tensor_tensor(main[:, :, 1:HG], near, far, ALU.add))
                    ch.add(dve.tensor_copy(main[:, :, 0:1], zero))
                    ch.add(dve.tensor_copy(dst[:, CE:CE + GROUPS].unsqueeze(2), mid))

                ch.link(dve.memset(eps[:], EPS))
                ch.add(dve.memset(h_odd[:].rearrange("p q (g c) -> p q g c", g=GROUPS)[:, :, :, 0:1], 0.0))
                dve.wait_ge(w_in, 16 * (GROUPS + 4))
                for g in range(GROUPS):
                    dve.tensor_tensor(w_even[:, g, :], w[:, g, 0, :], w[:, g, 1, :], ALU.add).then_inc(w_folded, 1)
                    dve.tensor_tensor(w_odd[:, g, :], w[:, g, 0, :], w[:, g, 1, :], ALU.subtract).then_inc(w_folded, 1)
                dve.wait_ge(scale_in, 48)
                for c in range(2):
                    ch.add(dve.scalar_tensor_tensor(out=scale[:, c, :], in0=scale[:, c, :], scalar=1.0, in1=norm_g, op0=ALU.add, op1=ALU.mult))
                dve.wait_ge(shift_in, 32)
                for c in range(2):
                    fold_even(edge[:, c, :], shift_rows[:, c, :])
                ch.settle()
                for q in range(PAIRS):
                    c = min(q, 1)
                    total, diff, far = work[:, 1, :], work[:, 2, :], work[:, 3, :]
                    dve.wait_ge(ms_ready, q + 1)
                    ch.link(dve.reciprocal(rt[:, q, :], rt[:, q, :]))
                    ch.link(dve.tensor_scalar(far, x_b[:, q, :], rt[:, q, 1:2], None, ALU.mult))
                    for dst, op in ((total, ALU.add), (diff, ALU.subtract)):
                        ch.add(dve.scalar_tensor_tensor(out=dst, in0=x_a[:, q, :], scalar=rt[:, q, 0:1], in1=far, op0=ALU.mult, op1=op))
                    ch.settle()
                    for dst in (total, diff):
                        ch.add(dve.tensor_tensor(dst, dst, scale[:, c, :], ALU.mult))
                    ch.settle()
                    fold_even(h_even[:, q, :], total)
                    if q < 2:
                        fold_even(edge[0:1, c, :], diff[0:1, :])
                    ch.settle()
                    near, back, _, _ = columns(diff)
                    dve.tensor_tensor(h_odd[:, q, :].rearrange("p (g c) -> p g c", g=GROUPS)[:, :, 1:HG], near, back, ALU.subtract).then_inc(h_ready, 1)
                    dve.wait_ge(h_ready, q + 1)

                dve.wait_ge(late_in, 32)
                dve.wait_ge(mid_in, 48)
                for n, (q, _, _) in enumerate(OUT):
                    dve.wait_ge(tile_full, n + 1)
                    if n:
                        dve.wait_ge(y_ready, n)
                    even = banks[:, (4 * n % 8) * BANK:(4 * n % 8 + 2) * BANK]
                    odd = work[:, 2 + n % 2, :]
                    if q is None:
                        dve.tensor_tensor(work[0:2, 0, :], even[0:2, :], gate_mid[:], ALU.mult).then_inc(tile_used, 1)
                        dve.wait_ge(tile_used, n + 1)
                        dve.tensor_tensor(x_mid[:], x_mid[:], work[0:2, 0, :], ALU.add).then_inc(y_ready, 1)
                        continue
                    dve.wait_ge(odd_kept, n + 1 if n < 2 else n)
                    ch.link(dve.tensor_tensor(work[:, 0, :], even, odd, ALU.subtract))
                    dve.tensor_tensor(work[:, 1, :], even, odd, ALU.add).then_inc(tile_used, 1)
                    dve.wait_ge(tile_used, n + 1)
                    for m in range(2):
                        ch.add(dve.tensor_tensor(work[:, m, :], work[:, m, :], gate[:, min(q, 1), :], ALU.mult))
                    ch.settle()
                    ch.link(dve.tensor_tensor(x_a[:, q, :], x_a[:, q, :], work[:, 0, :], ALU.add))
                    dve.tensor_tensor(x_b[:, q, :], x_b[:, q, :], work[:, 1, :], ALU.add).then_inc(y_ready, 1)


def _trunk(nc, t):
    with Stage(nc, "all") as s:
        per = Lasting(s)
        ident_in = s.sem("ident_in")
        with nc.Block() as block:

            @block.sync
            def _(sp):
                sp.dma_start(per.ident[:], t["ident"]).then_inc(ident_in, 16)
                sp.wait_ge(ident_in, 16)

        layer_0 = dict(t, mod_rows=t["mod_rows_l0"], x1=(t["x_prompt_1"], t["x_sample_1"]))
        layer_1 = dict(t, mod_rows=t["mod_rows_l1"], x2=layer_0["x1"], x1=t["y"])
        first_modulation(nc, layer_0, per)
        projections(nc, layer_0, per)
        attention(nc, layer_0, per, "attn_p", 0, PT, 0, PT, rest_of_modulation=True)
        attention(nc, layer_0, per, "attn_s", PT, ST, PT, ST + CT)
        mixer_out(nc, layer_0, per)
        channel_mixer(nc, dict(layer_0, mod_rows=t["mod_rows_l1"]), per, 0)
        fourier(nc, layer_1, per)
        channel_mixer(nc, layer_1, per, 1)


def channel_mixer(nc, t, per, layer):
    with Stage(nc, f"weights{layer}") as s:
        weights = Weights(s, t, layer)
        route(nc, t, per, layer, weights)
        experts(nc, t, per, layer, weights)


def _tables():
    inv = (np.float32(THETA) ** (-np.arange(0, ROPE // 2, 2, dtype=np.float32) / np.float32(ROPE // 2))).astype(np.float32)
    token = np.arange(DEC)
    angle = np.concatenate([(token // GRID_W).astype(np.float32)[:, None] * inv,
                            (token % GRID_W).astype(np.float32)[:, None] * inv], axis=1)
    rope = np.zeros((KEYT * P, ROPE), np.float32)
    rope[:, 0:ROPE // 2] = 1.0
    rope[SEQ:TOK, 0:ROPE // 2] = np.cos(angle)
    rope[SEQ:TOK, ROPE // 2:] = np.sin(angle)

    def dft(n, wave, rows, cols):
        return wave(2 * np.pi * (np.outer(np.arange(rows), np.arange(cols)) % n) / n) / np.sqrt(n)

    def cos_table(n, cols):
        table = dft(n, np.cos, n // 2, cols)
        table[0, 1::2] = 0.0
        return table

    def edge_table(n):
        table = np.zeros((2, n // 2 + 1))
        table[0, 1::2] = n ** -0.5
        table[1, 0] = n ** 0.5
        return table

    alt = np.zeros((HG, GROUPS, GROUPS))
    for g in range(GROUPS):
        alt[:, g, g] = (-1.0) ** np.arange(HG) / np.sqrt(GW)
    pick = np.zeros((P, 2))
    for c in range(2):
        pick[c::P // 4, c] = 1.0
    tables = dict(ident=np.eye(P), rope=rope, pick=pick,
                  pos_cos_p=cos_table(SEQ, SEQ // 2 + 1), pos_sin_p=dft(SEQ, np.sin, SEQ // 2, SEQ // 2),
                  pos_cos_s=cos_table(DEC, DEC // 2 + 1), pos_sin_s=dft(DEC, np.sin, DEC // 2, DEC // 2),
                  pos_edge=np.concatenate([edge_table(SEQ), edge_table(DEC)], axis=1),
                  chan_cos=cos_table(GW, HG), chan_sin=dft(GW, np.sin, HG, HG),
                  chan_odd=edge_table(GW)[0:1, 0:HG], chan_alt=alt.reshape(HG, GROUPS * GROUPS))
    tables = {name: np.ascontiguousarray(a, dtype=np.float32) for name, a in tables.items()}
    slot = np.arange(P)[:, None]
    partner = np.concatenate([SEQ - slot] + [DEC - j * P - slot for j in range(ST // 2)], axis=1)
    partner[0, 0:2] = SEQ // 2, DEC // 2
    tables["partner"] = partner.astype(np.uint32)
    return tables


_PLAIN = ["norm1_l0", "norm2_l0", "w_mod_l0", "b_mod_l0", "w_in_l0", "q_a_norm_l0", "w_q_up_l0", "q_norm_l0",
          "kv_a_norm_l0", "w_kv_up_l0", "k_norm_l0", "conv_w_l0", "w_o_l0", "w_router_l0", "w_gate_l0", "w_up_l0",
          "w_down_l0", "norm1_l1", "norm2_l1", "w_mod_l1", "b_mod_l1", "w_router_l1", "w_gate_l1", "w_up_l1", "w_down_l1"]
_SCRATCH = dict(mod_rows_l0=[2, 3 * D], mod_rows_l1=[2, 3 * D], state=[TOK, KVL + ROPE], qt=[NT * QK, HEADS * P], kt=[KEYT * QK, HEADS * P],
                v=[KEYT * P, HEADS * VH], conv=[CJ, P, TOK], attn=[TOK, HEADS * VH],
                x_prompt_1=[SEQ, D], x_sample_1=[DEC, D], xh_prompt=[SEQ, D], xh_sample=[DEC, D])
_OUTPUTS = dict(y_prompt=[SEQ, D], y_sample=[DEC, D], new_c_kv=[SEQ, KVL], new_k_rope=[SEQ, ROPE])


def _layout(inputs):
    w_f = inputs["w_f_l1"].reshape(GROUPS, GW, D)
    partner = np.concatenate([[HG], np.arange(GW - 1, HG, -1)])
    arrays = {name: inputs[name] for name in _PLAIN}
    arrays["x"] = np.concatenate([inputs["x_prompt"][0], inputs["x_sample"][0]])
    arrays["cond"] = np.concatenate([inputs["c_ctx"].reshape(KD, P), inputs["c"].reshape(KD, P)])
    arrays["cache_c_kv_l0"] = inputs["cache_c_kv_l0"][0]
    arrays["cache_k_rope_l0"] = inputs["cache_k_rope_l0"][0]
    arrays["w_f_pairs"] = np.stack([w_f[:, 0:HG], w_f[:, partner]], axis=1)
    return arrays


def kernel(**inputs):
    import concourse.bacc as bacc
    from concourse.bass_utils import run_bass_kernel_spmd

    inputs = {name: np.asarray(a) for name, a in inputs.items()}
    arrays = {name: np.ascontiguousarray(a) for name, a in {**_layout(inputs), **_tables()}.items()}
    nc = bacc.Bacc("TRN2", target_bir_lowering=False, num_devices=1)
    t = {name: nc.dram_tensor(name, list(a.shape), mybir.dt.from_np(a.dtype), kind="ExternalInput").ap() for name, a in arrays.items()}
    t.update({name: nc.dram_tensor(name, shape, F32, kind="Internal").ap() for name, shape in _SCRATCH.items()})
    t.update({name: nc.dram_tensor(name, shape, F32, kind="ExternalOutput").ap() for name, shape in _OUTPUTS.items()})
    t["xh"] = (t["xh_prompt"], t["xh_sample"])
    t["y"] = (t["y_prompt"], t["y_sample"])
    _trunk(nc, t)
    out = run_bass_kernel_spmd(nc, [arrays], core_ids=[0]).results[0]
    return (out["y_prompt"][None], out["y_sample"][None], out["new_c_kv"][None], out["new_k_rope"][None])
```

```python
from contextlib import ExitStack, contextmanager

import numpy as np

import concourse.bass as bass
from concourse import mybir

F32 = mybir.dt.float32
F32R = mybir.dt.float32r
U32 = mybir.dt.uint32
ALU = mybir.AluOpType
ACT = mybir.ActivationFunctionType
AX = mybir.AxisListType

P = 128
D = 1024
KD = D // P
SEQ, DEC, PAST = 256, 1024, 256
TOK = SEQ + DEC
NT = TOK // P
PT, ST, CT = SEQ // P, DEC // P, PAST // P
KEYT = NT + CT
HEADS, NOPE, ROPE, VH = 8, 64, 32, 64
QK = NOPE + ROPE
QL, KVL = 384, 256
LAT = QL + KVL + ROPE
CONV = 512
CJ = CONV // P
IN0 = LAT + 3 * CONV
NE, FF = 16, 512
KF = FF // P
CAP_S, CAP_P = 2 * DEC // NE, 2 * SEQ // NE
SLOTS = CAP_S + CAP_P
GROUPS = 4
GW = D // GROUPS
HG = GW // 2
EPS = 1e-6
GRID_W = 64
THETA = 10000.0
MOD = 6 * D
BANK = 512


class Chain:

    def __init__(self, eng, sem):
        self.eng, self.sem, self.base, self.n = eng, sem, 0, 0

    def add(self, instruction):
        instruction.then_inc(self.sem, 1)
        self.n += 1

    def settle(self):
        self.eng.wait_ge(self.sem, self.base + self.n)

    def link(self, instruction):
        self.add(instruction)
        self.settle()

    @contextmanager
    def over(self, count, per):
        start = self.base + self.n
        with self.eng.Fori(0, count) as i:
            self.base, self.n = start + i * per, 0
            yield i
            assert self.n == per, f"{self.n} links in the loop, {per} said"
        self.base, self.n = start + count * per, 0


class Lasting:

    def __init__(self, s):
        self.ident = s.sb("ident", [P, P])
        self.scale1, self.shift1 = s.sb("scale1", [P, NT // 2, KD]), s.sb("shift1", [P, NT // 2, KD])
        self.scale2, self.shift2, self.gate2 = ([s.sb(f"{name}_l{layer}", [P, 2, KD]) for layer in range(2)]
                                                for name in ("scale2", "shift2", "gate2"))
        self.at_s, self.at_p = s.sb("at_s", [P, NE], U32), s.sb("at_p", [CAP_P, NE], U32)
        self.g_s, self.g_p = s.sb("g_s", [P, NE]), s.sb("g_p", [CAP_P, NE])


def wait(eng, sem, value):
    if not isinstance(value, int) or value > 0:
        eng.wait_ge(sem, value)


def turns(eng, count, body, ch=None, per=0):
    body(0)
    if count > 1:
        with (ch.over(count - 1, per) if ch else eng.Fori(0, count - 1)) as i:
            body(i + 1)


class Stage:

    def __init__(self, nc, name):
        self.nc, self.name, self.stack, self.own = nc, name, ExitStack(), []

    def __enter__(self):
        self.stack.__enter__()
        return self

    def __exit__(self, *a):
        self.nc.clear_and_free_semaphores(self.own)
        self.nc.all_engine_barrier()
        return self.stack.__exit__(*a)

    def sb(self, name, shape, dt=F32):
        return self.stack.enter_context(self.nc.sbuf_tensor(f"{self.name}_{name}", shape, dt))

    def ps(self, name, banks=1):
        return self.stack.enter_context(self.nc.psum_tensor(f"{self.name}_{name}", [P, banks * BANK], F32))

    def sem(self, name):
        self.own.append(self.nc.alloc_semaphore(f"{self.name}_{name}"))
        return self.own[-1]

    def sems(self, name, n):
        return [self.sem(f"{name}{k}") for k in range(n)]


def four_banks(ps):
    return [ps[:, b * BANK:(b + 1) * BANK] for b in range(4)]


class Modulation:
    CH, NA, Q = 512, 2, 4

    def __init__(self, s, t, per, layer, first, end, banks, room=None):
        self.NB = len(room) if room else end - first
        self.t, self.per, self.layer, self.first, self.end = t, per, layer, first, end
        self.w_mod = t[f"w_mod_l{layer}"].rearrange("(k p) f -> p k f", p=P)
        self.rows = s.sb("mod_in", [2 * KD, 2, P])
        self.cond, self.gains, self.pick = s.sb("cond", [P, KD, 2]), s.sb("gains", [P, 2, KD]), s.sb("pick", [P, 2])
        self.mrow = s.sb("mrow", [2, (end - first) * self.CH])
        self.mcol = s.sb("mcol", [P, (end - first) * self.CH // P, 2])
        self.w = room or [s.sb(f"w_mod{b}", [P, KD, self.CH]) for b in range(self.NB)]
        self.parts = [s.sb(f"parts{b}", [P, self.CH]) for b in range(self.NA)]
        self.sums = [s.sb(f"sums{b}", [2, self.CH]) for b in range(self.NA)]
        self.tp, self.acc, self.total = banks[0], banks[1:1 + self.NA], banks[1 + self.NA]
        self.rows_in, self.w_in = s.sem("rows_in"), s.sems("w_mod_in", self.NB)
        self.turned, self.zeroed, self.gains_kept, self.silu_done = s.sem("turned"), s.sem("zeroed"), s.sem("gains_kept"), s.sem("silu_done")
        self.summed, self.moved, self.added, self.fetched = s.sems("summed", self.NB), s.sem("moved"), s.sem("added"), s.sem("fetched")
        self.biased, self.columns, self.rows_out = s.sem("biased"), s.sem("columns"), s.sem("rows_out")

    def start_loads(self, sp):
        t, lo = self.t, self.first * self.CH
        sp.dma_start(self.rows[:, 0, :], t["cond"]).then_inc(self.rows_in, 16)
        sp.dma_start(self.rows[0:KD, 1, :], t[f"norm1_l{self.layer}"].rearrange("(k p) -> k p", p=P)).then_inc(self.rows_in, 16)
        sp.dma_start(self.rows[KD:2 * KD, 1, :], t[f"norm2_l{self.layer}"].rearrange("(k p) -> k p", p=P)).then_inc(self.rows_in, 16)
        sp.dma_start(self.pick[:], t["pick"]).then_inc(self.rows_in, 16)
        sp.dma_start(self.mrow[:], t[f"b_mod_l{self.layer}"][lo:self.end * self.CH].partition_broadcast(2)).then_inc(self.rows_in, 16)
        self.load(sp, 0)

    def load(self, sp, i):
        for b in range(self.NB):
            wait(sp, self.summed[b], i)
            sp.dma_start(self.w[b][:], self.w_mod[:, :, bass.ts(self.first + i * self.NB + b, self.CH)]).then_inc(self.w_in[b], 16)

    def loads(self, sp):
        if self.end - self.first > self.NB:
            with sp.Fori(1, (self.end - self.first) // self.NB) as i:
                self.load(sp, i)

    def wait_for_products(self, eng):
        for b in range(self.NB):
            eng.wait_ge(self.summed[b], (self.end - self.first) // self.NB)

    def store(self, sp):
        lo, hi = self.first * self.CH, min(self.end * self.CH, 3 * D)
        sp.wait_ge(self.biased, self.end - self.first)
        sp.dma_start(self.t["mod_rows"][:, lo:hi], self.mrow[:, 0:hi - lo]).then_inc(self.rows_out, 16)
        sp.wait_ge(self.rows_out, 16)

    def tensor_start(self, pe):
        tp, rows = self.tp, self.rows
        pe.wait_ge(self.rows_in, 80)
        pe.transpose(tp[:, 0:2 * KD], rows[:, 0, :], self.per.ident[0:2 * KD, 0:2 * KD])
        pe.transpose(tp[:, 16:16 + 2 * KD], rows[:, 1, :], self.per.ident[0:2 * KD, 0:2 * KD]).then_inc(self.turned, 1)
        pe.wait_ge(self.silu_done, 1)
        pe.wait_ge(self.zeroed, self.NA)

    def add_parts(self, pe, n, b):
        if not isinstance(n, int) or n >= 0:
            pe.wait_ge(self.moved, n + 1)
            wait(pe, self.fetched, n)
            pe.matmul(self.total[0:2, :], self.pick[:], self.parts[b % self.NA][:], start=True, stop=True).then_inc(self.added, 1)

    def tensor_chunk(self, pe, i, b):
        n = i * self.NB + b
        pe.wait_ge(self.w_in[b], (i + 1) * 16)
        wait(pe, self.moved, n - 1)
        for k in range(KD):
            q = k % self.Q
            last = pe.matmul(self.acc[b % self.NA][32 * q:32 * q + 2, :], self.cond[:, k, :], self.w[b][:, k, :],
                             start=(k < self.Q), stop=(k >= KD - self.Q), skip_group_check=True)
        last.then_inc(self.summed[b], 1)
        self.add_parts(pe, n - 1, b - 1)

    def tensor_end(self, pe):
        chunks = self.end - self.first
        self.add_parts(pe, chunks - 1, self.NB - 1)
        pe.wait_ge(self.biased, chunks)
        pe.wait_ge(self.gains_kept, 1)
        for j in range(chunks * self.CH // P):
            last = pe.transpose(self.tp[:, 2 * j:2 * j + 2], self.mrow[:, j * P:(j + 1) * P], self.per.ident[0:2, 0:2])
        last.then_inc(self.turned, 1)

    def tensor(self, pe):
        def chunks(i):
            for b in range(self.NB):
                self.tensor_chunk(pe, i, b)

        self.tensor_start(pe)
        turns(pe, (self.end - self.first) // self.NB, chunks)
        self.tensor_end(pe)

    def scalar_start(self, act):
        act.wait_ge(self.turned, 1)
        act.activation(self.cond[:].rearrange("p k c -> p c k"), self.tp[:, 0:2 * KD].rearrange("p (c k) -> p c k", c=2),
                       ACT.Silu).then_inc(self.silu_done, 1)

    def fetch(self, act, n, b):
        if not isinstance(n, int) or n >= 0:
            act.wait_ge(self.added, n + 1)
            wait(act, self.biased, n - 1)
            act.activation(self.sums[b % self.NA][:], self.total[0:2, :], ACT.Copy).then_inc(self.fetched, 1)

    def scalar_chunk(self, act, i, b):
        n = i * self.NB + b
        act.wait_ge(self.summed[b], i + 1)
        wait(act, self.added, n - 1)
        act.activation(self.parts[b % self.NA][:], self.acc[b % self.NA][:], ACT.Copy).then_inc(self.moved, 1)
        self.fetch(act, n - 1, b - 1)

    def scalar_end(self, act):
        self.fetch(act, self.end - self.first - 1, self.NB - 1)

    def scalar(self, act):
        def chunks(i):
            for b in range(self.NB):
                self.scalar_chunk(act, i, b)

        self.scalar_start(act)
        turns(act, (self.end - self.first) // self.NB, chunks)
        self.scalar_end(act)

    def gpsimd(self, pool):
        pool.wait_ge(self.rows_in, 80)

        def bias(i):
            for b in range(self.NB):
                n = i * self.NB + b
                m = self.mrow[:, bass.ts(n, self.CH)]
                pool.wait_ge(self.fetched, n + 1)
                pool.tensor_tensor(m, self.sums[b % self.NA][:], m, ALU.add).then_inc(self.biased, 1)

        turns(pool, (self.end - self.first) // self.NB, bias)

    def prepare(self, dve):
        for b in range(self.NA):
            dve.memset(self.acc[b][:], 0.0).then_inc(self.zeroed, 1)
        dve.wait_ge(self.silu_done, 1)
        dve.tensor_copy(self.gains[:].rearrange("p c k -> p (c k)"), self.tp[:, 16:16 + 2 * KD]).then_inc(self.gains_kept, 1)

    def vector(self, dve):
        per, gains, layer = self.per, self.gains, self.layer
        dve.wait_ge(self.gains_kept, 1)
        dve.wait_ge(self.turned, 2)
        dve.tensor_copy(self.mcol[:].rearrange("p j c -> p (j c)"), self.tp[:, 0:self.mcol.shape[1] * 2]).then_inc(self.columns, 1)
        dve.wait_ge(self.columns, 1)

        def piece(c, n):
            lo = n * KD - self.first * self.CH // P
            return self.mcol[:, lo:lo + KD, c]

        if self.first == 0 and layer == 0:
            for tile in range(NT // 2):
                c = min(tile, 1)
                dve.scalar_tensor_tensor(out=per.scale1[:, tile, :], in0=piece(c, 1), scalar=1.0,
                                         in1=gains[:, 0, :], op0=ALU.add, op1=ALU.mult)
                dve.tensor_copy(per.shift1[:, tile, :], piece(c, 0))
        if self.end == MOD // self.CH:
            for c in range(2):
                dve.scalar_tensor_tensor(out=per.scale2[layer][:, c, :], in0=piece(c, 4), scalar=1.0,
                                         in1=gains[:, 1, :], op0=ALU.add, op1=ALU.mult)
                dve.tensor_copy(per.shift2[layer][:, c, :], piece(c, 3))
                dve.tensor_copy(per.gate2[layer][:, c, :], piece(c, 5))


def first_modulation(nc, t, per, w_in, w_lat_in, w_conv_in):
    with Stage(nc, "mod0") as s:
        mod = Modulation(s, t, per, 0, 0, 2 * D // Modulation.CH, four_banks(s.ps("mod", 4)))
        with nc.Block() as block:

            @block.sync
            def _(sp):
                mod.start_loads(sp)
                w_in_d = t["w_in_l0"].rearrange("(k p) f -> p k f", p=P)
                sp.dma_start(w_in[:, :, 0:LAT], w_in_d[:, :, 0:LAT]).then_inc(w_lat_in, 16)
                sp.dma_start(w_in[:, :, LAT:IN0], w_in_d[:, :, LAT:IN0]).then_inc(w_conv_in, 16)

            @block.tensor
            def _(pe):
                mod.tensor(pe)

            @block.scalar
            def _(act):
                mod.scalar(act)

            @block.gpsimd
            def _(pool):
                mod.gpsimd(pool)

            @block.vector
            def _(dve):
                mod.prepare(dve)
                mod.vector(dve)
def projections(nc, t, per, w_in, w_lat_in, w_conv_in):
    TP = 4
    HALF = NT // 2 - 1
    with Stage(nc, "proj") as s:
        w_q = s.sb("w_q", [P, QL // P, HEADS * QK])
        w_kv = s.sb("w_kv", [P, KVL // P, HEADS * 2 * VH])
        conv_w = s.sb("conv_w", [P, 3 * CJ])
        conv_rows = s.sb("conv_rows", [3 * CJ, P])
        lat_gain = s.sb("lat_gain", [P, QL + KVL])
        q_gain, k_gain = s.sb("q_gain", [P, QK]), s.sb("k_gain", [P, QK])
        eps = s.sb("eps", [P, 1])
        x_t = [s.sb(f"x{u}", [P, D]) for u in range(2)]
        rope_t = s.sb("rope", [P, 2, ROPE // 2])
        junk = s.sb("junk", [P, D])
        xh = s.sb("xh", [P, D])
        h_t = [s.sb(f"h_t{u}", [P, KD, P]) for u in range(2)]
        ms, rstd = s.sb("ms", [P, 1]), s.sb("rstd", [P, 1])
        lms, lrstd = s.sb("lms", [P, 2]), s.sb("lrstd", [P, 2])
        lat = [s.sb(f"lat{u}", [P, LAT]) for u in range(2)]
        lat_t = s.sb("lat_t", [P, (QL + KVL) // P, P])
        q_sq, k_sq = s.sb("q_sq", [P, HEADS, QK]), s.sb("k_sq", [P, HEADS, QK])
        q_n, k_n = s.sb("q_n", [P, HEADS, QK]), s.sb("k_n", [P, HEADS, QK])
        q_ms, k_ms = s.sb("q_ms", [P, 2, HEADS]), s.sb("k_ms", [P, 2, HEADS])
        turn = s.sb("turn", [P, 4, HEADS, ROPE // 2])
        gate_b = s.sb("gate_b", [P, CJ, TOK])
        taps = s.sb("taps", [P, TOK])
        q_out = s.sb("q_out", [QK, HEADS * P])
        k_out = s.sb("k_out", [QK, HEADS * P])
        v_out = s.sb("v_out", [P, HEADS * VH])
        u_sb = s.sb("u_sb", [P, CJ * P])
        gated = s.sb("gated", [P, CJ, TOK])

        tp = [s.ps(f"tp{b}") for b in range(2)]
        lp = s.ps("lp", 2)
        up = s.ps("up", 2)
        cv = [s.ps(f"cv{b}") for b in range(2)]

        w_up_in = s.sem("w_up_in")
        gains_in, conv_in = s.sem("gains_in"), s.sem("conv_in")
        x_in, rope_in = s.sems("x_in", 2), s.sem("rope_in")
        ms_ready, x_ready, h_ready = s.sem("ms_ready"), s.sem("x_ready"), s.sem("h_ready")
        tp_full, tp_free = s.sems("tp_full", 2), s.sems("tp_free", 2)
        lp_full, kv_kept = s.sem("lp_full"), s.sem("kv_kept")
        lms_ready, lat_ready, lat_in = s.sem("lms_ready"), s.sem("lat_ready"), s.sem("lat_in")
        up_full, up_free = s.sem("up_full"), s.sem("up_free")
        q_sq_ready, q_sum, q_ms_ready = s.sem("q_sq_ready"), s.sem("q_sum"), s.sem("q_ms_ready")
        k_sq_ready, k_sum, k_ms_ready = s.sem("k_sq_ready"), s.sem("k_sum"), s.sem("k_ms_ready")
        q_ready, k_ready = s.sem("q_ready"), s.sem("k_ready")
        q_stored, k_stored, v_stored = s.sem("q_stored"), s.sem("k_stored"), s.sem("v_stored")
        lat_stored = s.sems("lat_stored", 2)
        u_full, c_full, b_full = s.sem("u_full"), s.sem("c_full"), s.sem("b_full")
        u_kept, c_kept, b_kept = s.sem("u_kept"), s.sem("c_kept"), s.sem("b_kept")
        taps_full, taps_kept, mixed = s.sem("taps_full"), s.sem("taps_kept"), s.sem("mixed")
        late_out, a_chain, v_chain = s.sem("late_out"), s.sem("a_chain"), s.sem("v_chain")

        def tiles(eng, body, ch=None, per_turn=0):
            def pair(i):
                body(2 * i, i, 0, True)
                body(2 * i + 1, i, 1, True)

            turns(eng, HALF, pair, ch, per_turn)
            body(NT - 2, HALF, 0, True)
            body(NT - 1, HALF, 1, False)

        def x_use(n):
            return 0 if isinstance(n, int) and n == 0 else TP * n - 2

        def latent_use(n):
            return TP * n + 1

        def q_use(n, more):
            return TP * n + 3 if more else TP * n + 2

        def k_use(n, more):
            return q_use(n, more) + 1

        def has_previous(n):
            return not (isinstance(n, int) and n == 0)

        def has_second(n):
            return not (isinstance(n, int) and n + 2 >= NT)

        with nc.Block() as block:

            @block.sync
            def _(sp):
                sp.dma_start(lat_gain[:, 0:QL], t["q_a_norm_l0"].partition_broadcast(P)).then_inc(gains_in, 16)
                sp.dma_start(lat_gain[:, QL:QL + KVL], t["kv_a_norm_l0"].partition_broadcast(P)).then_inc(gains_in, 16)
                sp.dma_start(q_gain[:], t["q_norm_l0"].partition_broadcast(P)).then_inc(gains_in, 16)
                sp.dma_start(k_gain[:], t["k_norm_l0"].partition_broadcast(P)).then_inc(gains_in, 16)
                sp.dma_start(conv_rows[:], t["conv_w_l0"].rearrange("a (j p) -> (a j) p", p=P)).then_inc(conv_in, 16)
                sp.dma_start(w_q[:], t["w_q_up_l0"].rearrange("(k p) f -> p k f", p=P)).then_inc(w_up_in, 16)
                sp.dma_start(w_kv[:], t["w_kv_up_l0"].rearrange("(k p) f -> p k f", p=P)).then_inc(w_up_in, 16)

                def rope_load(n):
                    wait(sp, k_ready, 2 * n)
                    sp.dma_start(rope_t[:].rearrange("p a r -> p (a r)"), t["rope"][bass.ts(n, P), :]).then_inc(rope_in, 16)

                def values_store(n):
                    sp.wait_ge(kv_kept, 2 * n + 2)
                    sp.dma_start(t["v"][bass.ts(n, P), :], v_out[:]).then_inc(v_stored, 16)

                def queries_store(n, use):
                    for b in range(2):
                        sp.wait_ge(tp_free[b], use + 1)
                    sp.dma_start(t["qt"][bass.ts(n, QK), :], q_out[:]).then_inc(q_stored, 16)

                def keys_store(n, use):
                    for b in range(2):
                        sp.wait_ge(tp_free[b], use + 1)
                    sp.dma_start(t["kt"][bass.ts(n, QK), :], k_out[:]).then_inc(k_stored, 16)

                def tile(n, i, u, more):
                    rope_load(n)
                    sp.wait_ge(lat_ready, 3 * n + 3)
                    sp.dma_start(t["state"][bass.ts(n, P), :], lat[u][:, QL:LAT]).then_inc(lat_stored[u], 16)
                    if has_previous(n):
                        queries_store(n - 1, q_use(n - 1, True))
                        keys_store(n - 1, k_use(n - 1, True))
                    values_store(n)

                tiles(sp, tile)
                queries_store(NT - 1, q_use(NT - 1, False))
                keys_store(NT - 1, k_use(NT - 1, False))
                for c in range(CT):
                    n = NT + c
                    rope_load(n)
                    sp.wait_ge(lat_stored[c], 16 * NT // 2)
                    sp.dma_start(lat[c][:, QL:QL + KVL], t["cache_c_kv_l0"][c * P:(c + 1) * P, :]).then_inc(lat_in, 16)
                    sp.dma_start(lat[c][:, QL + KVL:LAT], t["cache_k_rope_l0"][c * P:(c + 1) * P, :]).then_inc(lat_in, 16)
                    for j in range(c * CJ // CT, (c + 1) * CJ // CT):
                        sp.wait_ge(mixed, j + 1)
                        sp.dma_start(t["conv"][j], gate_b[:, j, :]).then_inc(late_out, 16)
                    values_store(n)
                    keys_store(n, TP * NT + 2 * c + 1)
                sp.dma_start(t["new_c_kv"], t["state"][0:SEQ, 0:KVL]).then_inc(late_out, 16)
                sp.dma_start(t["new_k_rope"], t["state"][0:SEQ, KVL:KVL + ROPE]).then_inc(late_out, 16)
                for done, value in ((q_stored, 16 * NT), (k_stored, 16 * KEYT), (v_stored, 16 * KEYT), (late_out, 16 * (2 + CJ))):
                    sp.wait_ge(done, value)

            @block.gpsimd
            def _(pool):
                for u in range(2):
                    pool.dma_start(x_t[u][:], t["x"][u * P:(u + 1) * P, :]).then_inc(x_in[u], 16)
                with pool.Fori(1, NT // 2) as i:
                    for u in range(2):
                        pool.wait_ge(x_ready, 2 * i + u - 1)
                        pool.dma_start(x_t[u][:], t["x"][bass.ts(2 * i + u, P), :]).then_inc(x_in[u], 16)

            @block.tensor
            def _(pe):
                def latent_turns(use, first, u):
                    for b, lo, hi in ((0, first, 4), (1, 4, 5)):
                        pe.wait_ge(tp_free[b], use)
                        for j in range(lo, hi):
                            last = pe.transpose(tp[b][:, (j % 4) * P:(j % 4 + 1) * P], lat[u][:, j * P:(j + 1) * P], per.ident[:])
                        last.then_inc(tp_full[b], 1)

                def kv_up(use):
                    for b in range(2):
                        pe.wait_ge(tp_free[b], use)
                    for half in range(2):
                        for k in range(KVL // P):
                            last = pe.matmul(lp[:, half * BANK:(half + 1) * BANK], lat_t[:, QL // P + k, :],
                                             w_kv[:, k, half * BANK:(half + 1) * BANK], start=(k == 0), stop=(k == KVL // P - 1))
                    last.then_inc(lp_full, 1)

                def head_turns(src, ready, n, use):
                    pe.wait_ge(ready, 2 * n + 2)
                    for b in range(2):
                        pe.wait_ge(tp_free[b], use)
                        for j in range(4):
                            last = pe.transpose(tp[b][0:QK, j * P:(j + 1) * P], src[:, 4 * b + j, :], per.ident[:])
                        last.then_inc(tp_full[b], 1)

                def conv_part(base, bank, full, u):
                    for j in range(CJ):
                        for k in range(KD):
                            last = pe.matmul(cv[bank][:, j * P:(j + 1) * P], w_in[:, k, base + j * P:base + (j + 1) * P],
                                             h_t[u][:, k, :], start=(k == 0), stop=(k == KD - 1))
                    last.then_inc(full, 1)

                pe.wait_ge(conv_in, 16)
                pe.transpose(cv[0][:, 0:3 * CJ], conv_rows[:], per.ident[0:3 * CJ, 0:3 * CJ]).then_inc(taps_full, 1)
                pe.wait_ge(taps_kept, 1)

                def x_turns(n):
                    pe.wait_ge(x_ready, n + 1)
                    for b in range(2):
                        wait(pe, tp_free[b], x_use(n))
                        for j in range(4):
                            k = 4 * b + j
                            last = pe.transpose(tp[b][:, j * P:(j + 1) * P], xh[:, k * P:(k + 1) * P], per.ident[:])
                        last.then_inc(tp_full[b], 1)

                def tile(n, i, u, more):
                    pe.wait_ge(h_ready, 2 * n + 2)
                    if not has_previous(n):
                        pe.wait_ge(w_lat_in, 16)
                    wait(pe, kv_kept, 2 * n)
                    for base, lo, hi in ((0, 0, QL), (BANK, QL, LAT)):
                        for k in range(KD):
                            last = pe.matmul(lp[:, base:base + hi - lo], h_t[u][:, k, :], w_in[:, k, lo:hi],
                                             start=(k == 0), stop=(k == KD - 1))
                    last.then_inc(lp_full, 1)
                    wait(pe, b_kept, n)
                    if not has_previous(n):
                        pe.wait_ge(w_conv_in, 16)
                    conv_part(LAT + 2 * CONV, 0, u_full, u)
                    if has_previous(n):
                        head_turns(q_n, q_ready, n - 1, q_use(n - 1, True))
                        head_turns(k_n, k_ready, n - 1, k_use(n - 1, True))
                    pe.wait_ge(lat_ready, 3 * n + 3)
                    latent_turns(latent_use(n), 0, u)
                    wait(pe, c_kept, n)
                    conv_part(LAT + CONV, 1, c_full, u)
                    for b in range(2):
                        pe.wait_ge(tp_free[b], latent_use(n) + 1)
                    wait(pe, up_free, n)
                    if not has_previous(n):
                        pe.wait_ge(w_up_in, 32)
                    for lo, hi in ((0, BANK), (BANK, HEADS * QK)):
                        for k in range(QL // P):
                            last = pe.matmul(up[:, lo:hi], lat_t[:, k, :], w_q[:, k, lo:hi],
                                             start=(k == 0), stop=(k == QL // P - 1))
                    last.then_inc(up_full, 1)
                    kv_up(latent_use(n) + 1)
                    if more:
                        x_turns(n + 1)
                    pe.wait_ge(u_kept, n + 1)
                    conv_part(LAT, 0, b_full, u)

                x_turns(0)
                tiles(pe, tile)
                head_turns(q_n, q_ready, NT - 1, q_use(NT - 1, False))
                head_turns(k_n, k_ready, NT - 1, k_use(NT - 1, False))
                for c in range(CT):
                    pe.wait_ge(lat_in, 32 * (c + 1))
                    latent_turns(TP * NT + 2 * c, QL // P, c)
                    pe.wait_ge(kv_kept, 2 * (NT + c))
                    kv_up(TP * NT + 2 * c + 1)
                    head_turns(k_n, k_ready, NT + c, TP * NT + 2 * c + 1)

            @block.scalar
            def _(act):
                ch = Chain(act, a_chain)

                def x_square(n, i, u):
                    act.wait_ge(x_in[u], 16 * (i + 1))
                    wait(act, x_ready, n)
                    ch.link(act.activation(junk[:], x_t[u][:], ACT.Square, accum_out=ms[:]))
                    act.activation(rstd[:], ms[:], ACT.Sqrt, bias=eps[:], scale=1.0 / D).then_inc(ms_ready, 1)

                def latents_kept(use, first):
                    for b, lo, hi in ((0, first, 4), (1, 4, 5)):
                        act.wait_ge(tp_full[b], use)
                        act.activation(lat_t[:, lo:hi, :].rearrange("p j c -> p (j c)"),
                                       tp[b][:, (lo % 4) * P:(lo % 4 + hi - lo) * P], ACT.Copy).then_inc(tp_free[b], 1)

                def keys_values(n, lp_use, rope_cols):
                    act.wait_ge(lp_full, lp_use)
                    kv = lp[:].rearrange("p (h c) -> p h c", h=HEADS)
                    ch.add(act.activation(k_n[:, :, NOPE:QK], rope_cols.unsqueeze(1).broadcast_to([P, HEADS, ROPE]), ACT.Copy))
                    act.activation(k_n[:, :, 0:NOPE], kv[:, :, 0:NOPE], ACT.Copy).then_inc(kv_kept, 1)
                    wait(act, v_stored, 16 * n)
                    act.activation(v_out[:].rearrange("p (h c) -> p h c", h=HEADS), kv[:, :, NOPE:NOPE + VH], ACT.Copy).then_inc(kv_kept, 1)
                    ch.settle()
                    act.wait_ge(kv_kept, 2 * n + 1)
                    wait(act, k_sum, n)
                    act.activation(k_sq[:], k_n[:], ACT.Square).then_inc(k_sq_ready, 1)

                def root(n, sums, src, ready):
                    act.wait_ge(sums, n + 1)
                    act.activation(src[:, 1, :], src[:, 0, :], ACT.Sqrt, bias=eps[:], scale=1.0 / QK).then_inc(ready, 1)

                def queries_kept(n, use):
                    wait(act, q_stored, 16 * n)
                    for b in range(2):
                        act.wait_ge(tp_full[b], use + 1)
                        act.activation(q_out[:, b * BANK:(b + 1) * BANK], tp[b][0:QK, :], ACT.Copy).then_inc(tp_free[b], 1)

                def tile(n, i, u, more):
                    if has_second(n):
                        x_square(n + 2, i + 1, u)
                    act.wait_ge(lp_full, 2 * n + 1)
                    ch.add(act.activation(junk[:, 0:QL], lp[:, 0:QL], ACT.Square, accum_out=lms[:, 0:1]))
                    ch.settle()
                    ch.link(act.activation(junk[:, 0:KVL], lp[:, BANK:BANK + KVL], ACT.Square, accum_out=lms[:, 1:2]))
                    act.activation(lrstd[:, 0:1], lms[:, 0:1], ACT.Sqrt, bias=eps[:], scale=1.0 / QL).then_inc(lms_ready, 1)
                    act.activation(lrstd[:, 1:2], lms[:, 1:2], ACT.Sqrt, bias=eps[:], scale=1.0 / KVL).then_inc(lms_ready, 1)
                    if has_previous(n):
                        queries_kept(n - 1, q_use(n - 1, True))
                    act.wait_ge(u_full, n + 1)
                    wait(act, c_kept, n)
                    act.activation(u_sb[:], cv[0][:], ACT.Copy).then_inc(u_kept, 1)
                    latents_kept(latent_use(n) + 1, 0)
                    act.wait_ge(up_full, n + 1)
                    act.activation(q_sq[:].rearrange("p h c -> p (h c)"), up[:, 0:HEADS * QK], ACT.Square).then_inc(q_sq_ready, 1)
                    keys_values(n, 2 * n + 2, lat[u][:, QL + KVL:LAT])
                    root(n, q_sum, q_ms, q_ms_ready)
                    root(n, k_sum, k_ms, k_ms_ready)
                    act.wait_ge(b_full, n + 1)
                    act.activation(gate_b[:, :, bass.ts(n, P)], cv[0][:].rearrange("p (j c) -> p j c", j=CJ), ACT.Copy).then_inc(b_kept, 1)

                act.wait_ge(v_chain, 1)
                x_square(0, 0, 0)
                x_square(1, 0, 1)
                tiles(act, tile, ch, 2 * 4)
                queries_kept(NT - 1, q_use(NT - 1, False))
                for c in range(CT):
                    n = NT + c
                    latents_kept(TP * NT + 2 * c + 1, QL // P)
                    keys_values(n, 2 * NT + c + 1, lat[c][:, QL + KVL:LAT])
                    root(n, k_sum, k_ms, k_ms_ready)

            @block.vector
            def _(dve):
                ch = Chain(dve, v_chain)

                def normalise_x(n, u):
                    dve.wait_ge(ms_ready, n + 1)
                    ch.link(dve.reciprocal(rstd[:], rstd[:]))
                    dve.tensor_scalar(xh[:], x_t[u][:], rstd[:], None, ALU.mult).then_inc(x_ready, 1)

                def normalise_heads(src, dst, ms_, ready_in, n, gain, freed, ready):
                    dve.wait_ge(ready_in, n + 1)
                    ch.link(dve.reciprocal(ms_[:, 1, :], ms_[:, 1, :]))
                    first = dve.tensor_tensor(dst[:], src, ms_[:, 1, :].unsqueeze(2).broadcast_to([P, HEADS, QK]), ALU.mult)
                    if freed is None:
                        ch.link(first)
                    else:
                        first.then_inc(freed, 1)
                        dve.wait_ge(freed, n + 1)
                    ch.link(dve.tensor_tensor(dst[:], dst[:], gain[:].unsqueeze(1).broadcast_to([P, HEADS, QK]), ALU.mult))
                    pair = dst[:, :, NOPE:QK].rearrange("p h (r two) -> p h r two", two=2)
                    cos = rope_t[:, 0, :].unsqueeze(1).broadcast_to([P, HEADS, ROPE // 2])
                    sin = rope_t[:, 1, :].unsqueeze(1).broadcast_to([P, HEADS, ROPE // 2])
                    dve.wait_ge(rope_in, 16 * (n + 1))
                    for m, (x, f) in enumerate(((0, cos), (1, sin), (0, sin), (1, cos))):
                        ch.add(dve.tensor_tensor(turn[:, m, :, :], pair[:, :, :, x], f, ALU.mult))
                    ch.settle()
                    dve.tensor_tensor(pair[:, :, :, 0], turn[:, 0, :, :], turn[:, 1, :, :], ALU.subtract).then_inc(ready, 1)
                    dve.tensor_tensor(pair[:, :, :, 1], turn[:, 2, :, :], turn[:, 3, :, :], ALU.add).then_inc(ready, 1)

                def sums(sq, ready_in, n, out, ready):
                    dve.wait_ge(ready_in, n + 1)
                    dve.tensor_reduce(out[:, 0, :], sq[:], AX.X, ALU.add).then_inc(ready, 1)

                def modulate(n, i, u):
                    for b in range(2):
                        dve.wait_ge(tp_full[b], x_use(n) + 1)
                        cols = slice(4 * b, 4 * b + 4)
                        dve.tensor_tensor(h_t[u][:, cols, :], tp[b][:].rearrange("p (k c) -> p k c", k=4),
                                          per.scale1[:, i, cols].unsqueeze(2).broadcast_to([P, 4, P]), ALU.mult).then_inc(tp_free[b], 1)
                        dve.wait_ge(tp_free[b], x_use(n) + 1)
                        dve.tensor_tensor(h_t[u][:, cols, :], h_t[u][:, cols, :],
                                          per.shift1[:, i, cols].unsqueeze(2).broadcast_to([P, 4, P]), ALU.add).then_inc(h_ready, 1)

                def keys_kept(n, use):
                    wait(dve, k_stored, 16 * n)
                    for b in range(2):
                        dve.wait_ge(tp_full[b], use + 1)
                        dve.tensor_copy(k_out[:, b * BANK:(b + 1) * BANK], tp[b][0:QK, :]).then_inc(tp_free[b], 1)

                def tile(n, i, u, more):
                    dve.wait_ge(lms_ready, 2 * n + 2)
                    ch.link(dve.reciprocal(lrstd[:], lrstd[:]))
                    wait(dve, lat_stored[u], 16 * i)
                    dve.scalar_tensor_tensor(out=lat[u][:, 0:QL], in0=lp[:, 0:QL], scalar=lrstd[:, 0:1], in1=lat_gain[:, 0:QL],
                                             op0=ALU.mult, op1=ALU.mult).then_inc(lat_ready, 1)
                    dve.scalar_tensor_tensor(out=lat[u][:, QL:QL + KVL], in0=lp[:, BANK:BANK + KVL], scalar=lrstd[:, 1:2],
                                             in1=lat_gain[:, QL:QL + KVL], op0=ALU.mult, op1=ALU.mult).then_inc(lat_ready, 1)
                    dve.tensor_copy(lat[u][:, QL + KVL:LAT], lp[:, BANK + KVL:BANK + LAT - QL]).then_inc(lat_ready, 1)
                    if has_previous(n):
                        keys_kept(n - 1, k_use(n - 1, True))
                    dve.wait_ge(c_full, n + 1)
                    dve.wait_ge(u_kept, n + 1)
                    dve.tensor_tensor(gated[:, :, bass.ts(n, P)], cv[1][:].rearrange("p (j c) -> p j c", j=CJ),
                                      u_sb[:].rearrange("p (j c) -> p j c", j=CJ), ALU.mult).then_inc(c_kept, 1)
                    sums(q_sq, q_sq_ready, n, q_ms, q_sum)
                    if more:
                        modulate(n + 1, i + u, 1 - u)
                    if has_second(n):
                        normalise_x(n + 2, u)
                    sums(k_sq, k_sq_ready, n, k_ms, k_sum)
                    normalise_heads(up[:, 0:HEADS * QK].rearrange("p (h c) -> p h c", h=HEADS), q_n, q_ms, q_ms_ready, n, q_gain,
                                    up_free, q_ready)
                    dve.wait_ge(q_ready, 2 * n + 2)
                    normalise_heads(k_n[:], k_n, k_ms, k_ms_ready, n, k_gain, None, k_ready)

                def convolve(j):
                    ch.link(dve.tensor_scalar(taps[:], gated[:, j, :], conv_w[:, CJ + j:CJ + j + 1], None, ALU.mult))
                    for a, shift in ((0, -1), (2, 1)):
                        for lo, hi in ((0, SEQ), (SEQ, TOK)):
                            o = slice(lo + max(0, -shift), hi - max(0, shift))
                            i_ = slice(lo + max(0, shift), hi - max(0, -shift))
                            ch.add(dve.scalar_tensor_tensor(out=taps[:, o], in0=gated[:, j, i_],
                                                            scalar=conv_w[:, a * CJ + j:a * CJ + j + 1], in1=taps[:, o],
                                                            op0=ALU.mult, op1=ALU.add))
                        ch.settle()
                    dve.tensor_tensor(gate_b[:, j, :], gate_b[:, j, :], taps[:], ALU.mult).then_inc(mixed, 1)
                    dve.wait_ge(mixed, j + 1)

                ch.link(dve.memset(eps[:], EPS))
                dve.wait_ge(taps_full, 1)
                dve.tensor_copy(conv_w[:], cv[0][:, 0:3 * CJ]).then_inc(taps_kept, 1)
                dve.wait_ge(gains_in, 64)
                normalise_x(0, 0)
                modulate(0, 0, 0)
                normalise_x(1, 1)
                tiles(dve, tile, ch, 2 * 15)
                keys_kept(NT - 1, k_use(NT - 1, False))
                dve.wait_ge(b_kept, NT)
                dve.wait_ge(c_kept, NT)
                for c in range(CT):
                    n = NT + c
                    for j in range(c * CJ // CT, (c + 1) * CJ // CT):
                        convolve(j)
                    sums(k_sq, k_sq_ready, n, k_ms, k_sum)
                    normalise_heads(k_n[:], k_n, k_ms, k_ms_ready, n, k_gain, None, k_ready)
                    keys_kept(n, TP * NT + 2 * c + 1)


def attention(nc, t, per, name, q_first, q_tiles, k_first, nk, rest_of_modulation=False):
    K = nk * P
    SCALE = float(QK) ** -0.5
    PAIRS = q_tiles // 2
    spans = [(lo, min(lo + BANK, K)) for lo in range(0, K, BANK)]
    with Stage(nc, name) as s:
        keys = s.sb("keys", [QK, HEADS, K])
        vals = s.sb("vals", [P, nk, HEADS * VH])
        q_t = [s.sb(f"q{u}", [QK, HEADS * P]) for u in range(2)]
        pr = [s.sb(f"pr{b}", [P, K]) for b in range(2)]
        pr_t = [s.sb(f"pr_t{b}", [P, K]) for b in range(2)]
        top, neg = s.sb("top", [P, 1]), [s.sb(f"neg{b}", [P, 1]) for b in range(2)]
        total, inv = [s.sb(f"total{b}", [P, 1]) for b in range(2)], s.sb("inv", [P, 1])
        o_sb = [s.sb(f"o_sb{u}", [P, HEADS // 2 * P]) for u in range(2)]
        sc = [s.ps(f"sc{b}", len(spans)) for b in range(2)]
        o_ps = [s.ps(f"o{u}") for u in range(2)]

        keys_in, vals_in, q_in, o_out = s.sem("keys_in"), s.sem("vals_in"), s.sems("q_in", 2), s.sems("o_out", 2)
        s_full, neg_ready, p_ready, p_scaled = s.sem("s_full"), s.sem("neg_ready"), s.sem("p_ready"), s.sem("p_scaled")
        t_full, v_kept, a_kept = s.sem("t_full"), s.sem("v_kept"), s.sem("a_kept")
        o_full, o_kept, chain = s.sem("o_full"), s.sem("o_kept"), s.sem("chain")

        def tiles(eng, body, ch=None, per_turn=0):
            if PAIRS > 1:
                body(0, 0, 0, True)
                body(1, 0, 1, True)
            if PAIRS > 2:
                with (ch.over(PAIRS - 2, per_turn) if ch else eng.Fori(0, PAIRS - 2)) as turn:
                    i = turn + 1
                    body(2 * i, i, 0, True)
                    body(2 * i + 1, i, 1, True)
            body(q_tiles - 2, PAIRS - 1, 0, True)
            body(q_tiles - 1, PAIRS - 1, 1, False)

        def count(n, h, less):
            return HEADS * n + h - less

        if rest_of_modulation:
            mod = Modulation(s, t, per, 0, 2 * D // Modulation.CH, MOD // Modulation.CH, four_banks(s.ps("mod", 4)))
        else:
            mod = None

        with nc.Block() as block:

            @block.sync
            def _(sp):
                for u in range(2):
                    sp.dma_start(q_t[u][:], t["qt"][(q_first + u) * QK:(q_first + u + 1) * QK, :]).then_inc(q_in[u], 16)
                for m in range(nk):
                    sp.dma_start(keys[:, :, m * P:(m + 1) * P],
                                 t["kt"][(k_first + m) * QK:(k_first + m + 1) * QK, :].rearrange("c (h k) -> c h k", h=HEADS)).then_inc(keys_in, 16)
                sp.dma_start(vals[:], t["v"][k_first * P:(k_first + nk) * P, :].rearrange("(m p) c -> p m c", p=P)).then_inc(vals_in, 16)
                if mod:
                    mod.start_loads(sp)

                if PAIRS > 1:
                    with sp.Fori(0, PAIRS - 1) as i:
                        for u in range(2):
                            n = 2 * i + u
                            sp.wait_ge(s_full, HEADS * (n + 1))
                            sp.dma_start(q_t[u][:], t["qt"][bass.ds((q_first + 2 + n) * QK, QK), :]).then_inc(q_in[u], 16)
                            sp.wait_ge(o_kept, n + 1)
                            sp.dma_start(t["attn"][bass.ds((q_first + n) * P, P), :], o_sb[u][:]).then_inc(o_out[u], 16)
                for u in range(2):
                    n = q_tiles - 2 + u
                    sp.wait_ge(o_kept, n + 1)
                    sp.dma_start(t["attn"][(q_first + n) * P:(q_first + n + 1) * P, :], o_sb[u][:]).then_inc(o_out[u], 16)
                if mod:
                    mod.store(sp)
                for u in range(2):
                    sp.wait_ge(o_out[u], 16 * (q_tiles // 2))

            @block.tensor
            def _(pe):
                def scores(n, h, i, u):
                    if h == 0:
                        pe.wait_ge(q_in[u], 16 * (i + 1))
                    b = h % 2
                    for kept in (v_kept, a_kept) if K > BANK else (v_kept,):
                        wait(pe, kept, count(n, h, 1))
                    for lo, hi in spans:
                        last = pe.matmul(sc[b][:, lo:hi], q_t[u][:, h * P:(h + 1) * P], keys[:, h, lo:hi], start=True, stop=True)
                    last.then_inc(s_full, 1)

                def turns(n, h):
                    pe.wait_ge(p_scaled, HEADS * n + h + 1)
                    for m in range(nk):
                        last = pe.transpose(sc[h % 2][:, m * P:(m + 1) * P], pr[h % 2][:, m * P:(m + 1) * P], per.ident[:])
                    last.then_inc(t_full, 1)

                def mix(n, h, u):
                    for kept in (v_kept, a_kept) if K > BANK else (v_kept,):
                        pe.wait_ge(kept, HEADS * n + h + 1)
                    if h == 0:
                        wait(pe, o_kept, n - 1)
                    lo = 64 * (h % 2)
                    out = o_ps[u][lo:lo + VH, (h // 2) * P:(h // 2 + 1) * P]
                    for m in range(nk):
                        last = pe.matmul(out, vals[:, m, h * VH:(h + 1) * VH], pr_t[h % 2][:, m * P:(m + 1) * P],
                                         start=(m == 0), stop=(m == nk - 1))
                    last.then_inc(o_full, 1)

                def tile(n, i, u, more):
                    for h in range(HEADS):
                        if h < HEADS - 1:
                            scores(n, h + 1, i, u)
                        elif more:
                            scores(n + 1, 0, i + u, 1 - u)
                        turns(n, h)
                        if h:
                            mix(n, h - 1, u)
                        if mod and h % 2:
                            mod.tensor_chunk(pe, 0, (HEADS * n + h) // 2)
                    mix(n, HEADS - 1, u)

                if mod:
                    mod.tensor_start(pe)
                pe.wait_ge(keys_in, 16 * nk)
                scores(0, 0, 0, 0)
                pe.wait_ge(vals_in, 16)
                tiles(pe, tile)
                if mod:
                    mod.tensor_end(pe)

            @block.scalar
            def _(act):
                def exp(n, h):
                    b = h % 2
                    act.wait_ge(neg_ready, HEADS * n + h + 1)
                    wait(act, t_full, count(n, h, 1))
                    act.activation(pr[b][:], sc[b][:, 0:K], ACT.Exp, bias=neg[b][:], scale=SCALE, accum_out=total[b][:]).then_inc(p_ready, 1)

                def tile(n, i, u, more):
                    for h in range(HEADS):
                        b = h % 2
                        if K > BANK:
                            act.wait_ge(t_full, HEADS * n + h + 1)
                            wait(act, o_full, count(n, h, 1))
                            act.activation(pr_t[b][:, BANK:K], sc[b][:, BANK:K], ACT.Copy).then_inc(a_kept, 1)
                        if h < HEADS - 1:
                            exp(n, h + 1)
                        elif more:
                            exp(n + 1, 0)
                        if mod and h % 2:
                            mod.scalar_chunk(act, 0, (HEADS * n + h) // 2)
                    act.wait_ge(o_full, HEADS * (n + 1))
                    wait(act, o_out[u], 16 * i)
                    act.activation(o_sb[u][:], o_ps[u][:], ACT.Copy).then_inc(o_kept, 1)

                if mod:
                    mod.scalar_start(act)
                exp(0, 0)
                tiles(act, tile)
                if mod:
                    mod.scalar_end(act)

            @block.gpsimd
            def _(pool):
                if mod:
                    mod.gpsimd(pool)

            @block.vector
            def _(dve):
                ch = Chain(dve, chain)

                def maximum(n, h):
                    b = h % 2
                    dve.wait_ge(s_full, HEADS * n + h + 1)
                    ch.link(dve.tensor_reduce(top[:], sc[b][:, 0:K], AX.X, ALU.max))
                    wait(dve, p_ready, count(n, h, 1))
                    dve.tensor_scalar(neg[b][:], top[:], -SCALE, None, ALU.mult).then_inc(neg_ready, 1)

                def tile(n, i, u, more):
                    for h in range(HEADS):
                        b = h % 2
                        dve.wait_ge(p_ready, HEADS * n + h + 1)
                        ch.link(dve.reciprocal(inv[:], total[b][:]))
                        dve.tensor_scalar(pr[b][:], pr[b][:], inv[:], None, ALU.mult).then_inc(p_scaled, 1)
                        if h < HEADS - 1:
                            maximum(n, h + 1)
                        elif more:
                            maximum(n + 1, 0)
                        dve.wait_ge(t_full, HEADS * n + h + 1)
                        wait(dve, o_full, count(n, h, 1))
                        dve.tensor_copy(pr_t[b][:, 0:min(K, BANK)], sc[b][:, 0:min(K, BANK)]).then_inc(v_kept, 1)

                if mod:
                    mod.prepare(dve)
                maximum(0, 0)
                tiles(dve, tile, ch, 2 * 2 * HEADS)
                if mod:
                    mod.vector(dve)


def route(nc, t, per, layer, weights):
    first = layer == 0
    with Stage(nc, f"route{layer}") as s:
        w_r = s.sb("w_r", [P, KD, NE])
        w_rs = s.sb("w_rs", [P, 2, KD, NE])
        bias = s.sb("bias", [NE, 2])
        eps = s.sb("eps", [P, 1])
        xh = [s.sb(f"xh{u}", [P, D]) for u in range(2)]
        xh_t = [s.sb(f"xh_t{u}", [P, KD, P]) for u in range(2)]
        if first:
            a_t = [s.sb(f"a{u}", [P, KD, P]) for u in range(2)]
            x_t = [s.sb(f"x{u}", [P, D]) for u in range(2)]
            y_t = [s.sb(f"y{u}", [P, D]) for u in range(2)]
            w_o, gate = (weights.gate[1], weights.up[1]), weights.down[1][:, 0:2, :]
        else:
            x_all = s.sb("x_all", [P, NT, D])
        junk = weights.down[1][:, 2, :]
        ms, rt = [s.sb(f"ms{u}", [P, 1]) for u in range(2)], [s.sb(f"rt{u}", [P, 1]) for u in range(2)]
        lg_t = s.sb("lg_t", [NE, TOK])
        logits = s.sb("logits", [P, NT, NE])
        top, den = s.sb("top", [P, NT]), s.sb("den", [P, NT])
        aff = s.sb("aff", [NE, TOK])
        left = s.sb("left", [NE, DEC])
        best = {c: s.sb(f"best{c}", [NE, cap]) for c, cap in ((0, CAP_P), (1, CAP_S))}
        at = {c: s.sb(f"at{c}", [NE, cap], U32) for c, cap in ((0, CAP_P), (1, CAP_S))}
        at_f = {c: s.sb(f"at_f{c}", [NE, cap]) for c, cap in ((0, CAP_P), (1, CAP_S))}
        tp = [s.ps(f"tp{b}") for b in range(2)]
        lg = s.ps("lg")
        wide = s.ps("wide")
        four = s.ps("four", 4)
        acc = [four[:, u * 2 * BANK:(u + 1) * 2 * BANK] for u in range(2)]
        mod = Modulation(s, t, per, 1, 0, MOD // Modulation.CH, four_banks(four), (weights.gate[1], weights.up[1])) if first else None

        w_r_in, w_o_in, gate_in, a_in, x_in = s.sem("w_r_in"), s.sem("w_o_in"), s.sem("gate_in"), s.sems("a_in", 2), s.sems("x_in", 2)
        scaled, bias_full, bias_kept = s.sem("scaled"), s.sem("bias_full"), s.sem("bias_kept")
        full, gated, y_ready, y_out = s.sem("full"), s.sem("gated"), s.sem("y_ready"), s.sems("y_out", 2)
        ms_ready, xh_ready, xh_out = s.sem("ms_ready"), s.sem("xh_ready"), s.sems("xh_out", 2)
        tp_full, v_kept, a_kept = s.sem("tp_full"), s.sem("v_kept"), s.sem("a_kept")
        lg_full, lg_kept, lg_turned, shifted, raised = s.sem("lg_full"), s.sem("lg_kept"), s.sem("lg_turned"), s.sem("shifted"), s.sem("raised")
        logits_kept, aff_ready, wide_full, wide_kept = s.sem("logits_kept"), s.sem("aff_ready"), s.sem("wide_full"), s.sem("wide_kept")
        best_ready, cols_full, a_chain, chain = s.sem("best_ready"), s.sem("cols_full"), s.sem("a_chain"), s.sem("chain")

        def steps(eng, body, ch=None, per_turn=0):
            for n in range(4):
                body(n, n // 2, n % 2)
            with (ch.over(NT // 2 - 2, per_turn) if ch else eng.Fori(0, NT // 2 - 2)) as turn:
                for u in range(2):
                    body(2 * turn + 4 + u, turn + 2, u)

        def rows(x, n):
            return x[0][n * P:(n + 1) * P, :] if isinstance(n, int) and n < PT else x[1][bass.ts(n - PT, P), :]

        def stream(n, u):
            return y_t[u][:] if first else x_all[:, bass.ds(n, 1), :].rearrange("p a d -> p (a d)")

        def condition(n):
            return 0 if isinstance(n, int) and n < PT else 1

        def exists(n):
            return not isinstance(n, int) or 0 <= n < NT

        with nc.Block() as block:

            @block.sync
            def _(sp):
                sp.dma_start(w_r[:], t[f"w_router_l{layer}"].rearrange("(k p) e -> p k e", p=P)).then_inc(w_r_in, 16)
                if first:
                    w_o_d = t["w_o_l0"].rearrange("(k p) f -> p k f", p=P)
                    for half in range(2):
                        sp.dma_start(w_o[half][:], w_o_d[:, :, half * BANK:(half + 1) * BANK]).then_inc(w_o_in, 16)
                    for c in range(2):
                        sp.dma_start(gate[:, c, :], t["mod_rows_l0"][c, 2 * D:3 * D].partition_broadcast(P)).then_inc(gate_in, 16)

                else:
                    sp.dma_start(x_all[:, 0:PT, :], t["x1"][0].rearrange("(n p) d -> p n d", p=P)).then_inc(x_in[0], 16)
                    sp.dma_start(x_all[:, PT:NT, :], t["x1"][1].rearrange("(n p) d -> p n d", p=P)).then_inc(x_in[1], 16)

                def store(n, u):
                    if exists(n):
                        if first:
                            sp.wait_ge(y_ready, n + 1)
                            sp.dma_start(rows(t["x1"], n), y_t[u][:]).then_inc(y_out[u], 16)
                        sp.wait_ge(xh_ready, n + 1)
                        sp.dma_start(rows(t["xh"], n), xh[u][:]).then_inc(xh_out[u], 16)

                def tile(n, i, u):
                    if first:
                        wait(sp, full, n - 1)
                        sp.dma_start(a_t[u][:, 0:KD // 2, :].rearrange("p k c -> p (k c)"), t["attn"][bass.ts(n, P), :]).then_inc(a_in[u], 16)
                        sp.dma_start(a_t[u][:, KD // 2:KD, :], t["conv"].rearrange("j p n -> p j n")[:, :, bass.ts(n, P)]).then_inc(a_in[u], 16)
                        wait(sp, y_ready, n - 1)
                        sp.dma_start(x_t[u][:], t["x"][bass.ts(n, P), :]).then_inc(x_in[u], 16)
                    store(n - 1, 1 - u)

                steps(sp, tile)
                store(NT - 1, 1)
                if mod:
                    sp.wait_ge(full, NT)
                    mod.start_loads(sp)
                weights.load(sp, 0, 0)
                if mod:
                    mod.loads(sp)
                    mod.wait_for_products(sp)
                    sp.wait_ge(y_ready, NT)
                sp.wait_ge(ms_ready, NT)
                weights.load(sp, 1, 1)
                if mod:
                    mod.store(sp)
                for u in range(2):
                    sp.wait_ge(xh_out[u], 16 * NT // 2)
                    if first:
                        sp.wait_ge(y_out[u], 16 * NT // 2)

            @block.gpsimd
            def _(pool):
                if mod:
                    mod.gpsimd(pool)

            @block.tensor
            def _(pe):
                def product(n, i, u, half):
                    if first and exists(n):
                        if half == 0:
                            pe.wait_ge(a_in[u], 32 * (i + 1))
                            wait(pe, gated, n - 1)
                        for k in range(KD):
                            last = pe.matmul(acc[u][:, half * BANK:(half + 1) * BANK], a_t[u][:, k, :],
                                             w_o[half][:, k, :], start=(k == 0), stop=(k == KD - 1))
                        if half == 1:
                            last.then_inc(full, 1)

                def turn(n, u):
                    if exists(n):
                        pe.wait_ge(xh_ready, n + 1)
                        for b, kept in ((0, v_kept), (1, a_kept)):
                            wait(pe, kept, n)
                            for j in range(4):
                                k = 4 * b + j
                                last = pe.transpose(tp[b][:, j * P:(j + 1) * P], xh[u][:, k * P:(k + 1) * P], per.ident[:])
                            last.then_inc(tp_full, 1)

                def router(n, u):
                    if exists(n):
                        pe.wait_ge(v_kept, n + 1)
                        pe.wait_ge(a_kept, n + 1)
                        wait(pe, lg_kept, n)
                        for k in range(KD):
                            last = pe.matmul(lg[0:NE, 0:P], w_rs[:, condition(n), k, :], xh_t[u][:, k, :], start=(k == 0), stop=(k == KD - 1))
                        last.then_inc(lg_full, 1)

                def step(n, i, u):
                    product(n, i, u, 0)
                    turn(n - 1, 1 - u)
                    product(n, i, u, 1)
                    router(n - 2, u)

                pe.wait_ge(w_r_in, 16)
                for c in range(2):
                    for k in range(KD):
                        last = pe.matmul(lg[0:NE, c:c + 1], w_r[:, k, :], per.shift2[layer][:, c, k:k + 1], start=(k == 0), stop=(k == KD - 1))
                last.then_inc(bias_full, 1)
                pe.wait_ge(bias_kept, 1)
                pe.wait_ge(scaled, 2)
                if first:
                    pe.wait_ge(w_o_in, 32)
                steps(pe, step)
                step(NT, NT // 2, 0)
                step(NT + 1, NT // 2, 1)
                pe.wait_ge(lg_kept, NT)
                for n in range(NT):
                    last = pe.transpose(wide[:, n * NE:(n + 1) * NE], lg_t[:, n * P:(n + 1) * P], per.ident[0:NE, 0:NE])
                last.then_inc(lg_turned, 1)
                pe.wait_ge(logits_kept, 1)
                pe.wait_ge(aff_ready, 1)
                for m, lo in enumerate(range(0, NT, 4)):
                    wait(pe, wide_kept, m)
                    for n in range(lo, min(lo + 4, NT)):
                        last = pe.transpose(wide[0:NE, (n - lo) * P:(n - lo + 1) * P], logits[:, n, :], per.ident[:])
                    last.then_inc(wide_full, 1)
                if mod:
                    pe.wait_ge(gated, NT)
                    mod.tensor(pe)
                pe.wait_ge(best_ready, 2)
                for m, src in enumerate((at_f[1], best[1], at_f[0], best[0])):
                    cap = src.shape[1]
                    last = pe.transpose(tp[0][0:cap, m * NE:(m + 1) * NE], src[:], per.ident[0:NE, 0:NE])
                last.then_inc(cols_full, 1)

            @block.scalar
            def _(act):
                ch = Chain(act, a_chain)
                act.wait_ge(chain, 1)
                act.wait_ge(bias_full, 1)
                act.activation(bias[:], lg[0:NE, 0:2], ACT.Copy).then_inc(bias_kept, 1)
                act.wait_ge(bias_kept, 1)

                def turned_kept(n, u):
                    if exists(n):
                        act.wait_ge(tp_full, 2 * n + 2)
                        wait(act, lg_full, n - 1)
                        act.activation(xh_t[u][:, KD // 2:KD, :].rearrange("p k c -> p (k c)"), tp[1][:], ACT.Copy).then_inc(a_kept, 1)

                def logits_out(n):
                    if exists(n):
                        c = condition(n)
                        act.wait_ge(lg_full, n + 1)
                        act.activation(lg_t[:, bass.ts(n, P)], lg[0:NE, 0:P], ACT.Identity, bias=bias[:, c:c + 1]).then_inc(lg_kept, 1)

                def step(n, i, u):
                    if exists(n):
                        if first:
                            act.wait_ge(y_ready, n + 1)
                        elif isinstance(n, int) and n in (0, PT):
                            act.wait_ge(x_in[condition(n)], 16)
                        wait(act, xh_ready, n - 1)
                        ch.link(act.activation(junk, stream(n, u), ACT.Square, accum_out=ms[u][:]))
                        act.activation(rt[u][:], ms[u][:], ACT.Sqrt, bias=eps[:], scale=1.0 / D).then_inc(ms_ready, 1)
                    turned_kept(n - 1, 1 - u)
                    logits_out(n - 2)

                steps(act, step, ch, 2)
                step(NT, NT // 2, 0)
                step(NT + 1, NT // 2, 1)
                act.wait_ge(shifted, 1)
                flat = logits[:].rearrange("p n e -> p (n e)")
                act.activation(flat, flat, ACT.Exp).then_inc(raised, 1)
                if mod:
                    mod.scalar(act)

            @block.vector
            def _(dve):
                ch = Chain(dve, chain)
                ch.link(dve.memset(eps[:], EPS))
                dve.wait_ge(w_r_in, 16)
                for c in range(2):
                    dve.tensor_tensor(w_rs[:, c, :, :], w_r[:], per.scale2[layer][:, c, :].unsqueeze(2).broadcast_to([P, KD, NE]),
                                      ALU.mult).then_inc(scaled, 1)
                if first:
                    dve.wait_ge(gate_in, 32)

                def step(n, i, u):
                    if exists(n):
                        if first:
                            dve.wait_ge(full, n + 1)
                            wait(dve, y_out[u], 16 * i)
                            wait(dve, ms_ready, n - 1)
                            dve.tensor_tensor(y_t[u][:], acc[u], gate[:, condition(n), :], ALU.mult).then_inc(gated, 1)
                            dve.wait_ge(gated, n + 1)
                            dve.wait_ge(x_in[u], 16 * (i + 1))
                            dve.tensor_tensor(y_t[u][:], y_t[u][:], x_t[u][:], ALU.add).then_inc(y_ready, 1)
                        dve.wait_ge(ms_ready, n + 1)
                        ch.link(dve.reciprocal(rt[u][:], rt[u][:]))
                        wait(dve, xh_out[u], 16 * i)
                        wait(dve, tp_full, 2 * n - 2)
                        dve.tensor_scalar(xh[u][:], stream(n, u), rt[u][:], None, ALU.mult).then_inc(xh_ready, 1)
                    if exists(n - 1):
                        dve.wait_ge(tp_full, 2 * (n - 1) + 1)
                        wait(dve, lg_full, n - 2)
                        dve.tensor_copy(xh_t[1 - u][:, 0:KD // 2, :].rearrange("p k c -> p (k c)"), tp[0][:]).then_inc(v_kept, 1)

                steps(dve, step, ch, 2)
                step(NT, NT // 2, 0)
                dve.wait_ge(lg_turned, 1)
                dve.tensor_copy(logits[:].rearrange("p n e -> p (n e)"), wide[:, 0:NT * NE]).then_inc(logits_kept, 1)
                dve.wait_ge(logits_kept, 1)
                ch.link(dve.tensor_reduce(top[:], logits[:], AX.X, ALU.max))
                dve.tensor_tensor(logits[:], logits[:], top[:].unsqueeze(2).broadcast_to([P, NT, NE]), ALU.subtract).then_inc(shifted, 1)
                dve.wait_ge(raised, 1)
                ch.link(dve.tensor_reduce(den[:], logits[:], AX.X, ALU.add))
                ch.link(dve.reciprocal(den[:], den[:]))
                dve.tensor_tensor(logits[:], logits[:], den[:].unsqueeze(2).broadcast_to([P, NT, NE]), ALU.mult).then_inc(aff_ready, 1)
                for m, lo in enumerate(range(0, TOK, BANK)):
                    hi = min(lo + BANK, TOK)
                    dve.wait_ge(wide_full, m + 1)
                    dve.tensor_copy(aff[:, lo:hi], wide[0:NE, 0:hi - lo]).then_inc(wide_kept, 1)
                dve.wait_ge(wide_kept, m + 1)
                if mod:
                    mod.prepare(dve)
                for c, lo, hi, cap in ((0, 0, SEQ, CAP_P), (1, SEQ, TOK, CAP_S)):
                    src = aff[:, lo:hi]
                    for r in range(cap // 8):
                        eight = slice(8 * r, 8 * r + 8)
                        ch.link(dve.max(best[c][:, eight], src))
                        ch.add(dve.max_index(at[c][:, eight], best[c][:, eight], src))
                        ch.add(dve.match_replace(left[:, 0:hi - lo], best[c][:, eight], src, -1.0))
                        ch.settle()
                        src = left[:, 0:hi - lo]
                    dve.tensor_copy(at_f[c][:], at[c][:]).then_inc(best_ready, 1)
                dve.wait_ge(cols_full, 1)
                dve.tensor_copy(per.at_s[:], tp[0][:, 0:NE])
                dve.tensor_copy(per.g_s[:], tp[0][:, NE:2 * NE])
                dve.tensor_copy(per.at_p[:], tp[0][0:CAP_P, 2 * NE:3 * NE])
                dve.tensor_copy(per.g_p[:], tp[0][0:CAP_P, 3 * NE:4 * NE])
                if mod:
                    mod.vector(dve)


class Weights:

    def __init__(self, s, t, layer):
        self.gate, self.up = ([s.sb(f"{m}{u}", [P, KD, FF]) for u in range(2)] for m in ("w_gate", "w_up"))
        self.down = [s.sb(f"w_down{u}", [P, KF, D]) for u in range(2)]
        self.gate_up_in, self.down_in = s.sems("gate_up_in", 2), s.sems("down_in", 2)
        self.gate_d, self.up_d = (t[f"{m}_l{layer}"].rearrange("e (k p) f -> p (e k) f", p=P) for m in ("w_gate", "w_up"))
        self.down_d = t[f"w_down_l{layer}"].rearrange("e (k p) d -> p (e k) d", p=P)

    def load_gate_up(self, eng, e, u):
        for w, src in ((self.gate, self.gate_d), (self.up, self.up_d)):
            eng.dma_start(w[u][:], src[:, bass.ts(e, KD), :]).then_inc(self.gate_up_in[u], 16)

    def load_down(self, eng, e, u):
        eng.dma_start(self.down[u][:], self.down_d[:, bass.ts(e, KF), :]).then_inc(self.down_in[u], 16)

    def load(self, eng, e, u):
        self.load_gate_up(eng, e, u)
        self.load_down(eng, e, u)


def experts(nc, t, per, layer, weights):
    groups = [(0, 3), (3, 6), (6, 8)]
    wg, wu, wd, wgu_in, wd_in = weights.gate, weights.up, weights.down, weights.gate_up_in, weights.down_in
    with Stage(nc, f"experts{layer}") as s:
        scale, shift, gate = (s.sb(m, [P, KD, SLOTS]) for m in ("scale", "shift", "gate"))
        g_s = [s.sb(f"g_s{u}", [P, 1]) for u in range(2)]
        g_p = [s.sb(f"g_p{u}", [CAP_P, 1]) for u in range(2)]
        xs = [s.sb(f"xs{u}", [P, D]) for u in range(2)]
        xp = [s.sb(f"xp{u}", [CAP_P, D]) for u in range(2)]
        h_t = [s.sb(f"h_t{u}", [P, KD, SLOTS]) for u in range(2)]
        act_sb = [s.sb(f"act{b}", [P, SLOTS]) for b in range(2)]
        hid = s.sb("hid", [P, KF, SLOTS])
        y_t = s.sb("y_t", [P, KD, SLOTS])
        ys = [s.sb(f"ys{u}", [P, D]) for u in range(2)]
        yp = [s.sb(f"yp{u}", [CAP_P, D]) for u in range(2)]
        tp = [s.ps(f"tp{b}") for b in range(2)]
        gu = [s.ps(f"gu{b}") for b in range(2)]
        dn = [s.ps(f"dn{b}") for b in range(2)]
        to = [s.ps(f"to{b}") for b in range(2)]
        spread, g_ready, x_in = s.sem("spread"), s.sem("g_ready"), s.sems("x_in", 2)
        tp_full, tp_kept, h_ready = s.sem("tp_full"), s.sem("tp_kept"), s.sem("h_ready")
        gu_full, silu_ready, hid_ready = s.sem("gu_full"), s.sem("silu_ready"), s.sem("hid_ready")
        dn_full, dn_kept, to_full, to_kept, y_out = s.sem("dn_full"), s.sem("dn_kept"), s.sem("to_full"), s.sem("to_kept"), s.sem("y_out")

        def middle(eng, body):
            body(1, 0, 1)
            body(2, 1, 0)
            with eng.Fori(1, NE // 2 - 1) as i:
                body(2 * i + 1, i, 1)
                body(2 * i + 2, i + 1, 0)

        def turn_bank(u, g):
            return tp[(g + u) % 2]

        def down_bank(u, g):
            return dn[(g + u) % 2]

        with nc.Block() as block:

            @block.sync
            def _(sp):
                with sp.Fori(1, NE // 2) as i:
                    for u in range(2):
                        e = 2 * i + u
                        sp.wait_ge(gu_full, KF * (e - 1))
                        weights.load_gate_up(sp, e, u)
                        sp.wait_ge(dn_full, 3 * (e - 1))
                        weights.load_down(sp, e, u)

            @block.gpsimd
            def _(pool):
                def fetch(e):
                    if e >= 2:
                        pool.wait_ge(tp_full, 3 * (e - 1))
                    for dst, src, at in ((xs, 1, per.at_s), (xp, 0, per.at_p)):
                        pool.indirect_dma_start(dst[e % 2][:], None, t["xh"][src], bass.IndirectOffsetOnAxis(at[:, e:e + 1], 0)).then_inc(x_in[e % 2], 16)

                def affinities(e):
                    if e >= 2:
                        pool.wait_ge(to_kept, 4 * (e - 1))
                    for dst, src in ((g_s, per.g_s), (g_p, per.g_p)):
                        pool.tensor_copy(dst[e % 2][:], src[:, e:e + 1]).then_inc(g_ready, 1)

                def scatter(e):
                    pool.wait_ge(to_kept, 4 * e + 4)
                    if e:
                        pool.wait_ge(y_out, 32 * e)
                    for dst, src, at in ((1, ys, per.at_s), (0, yp, per.at_p)):
                        pool.indirect_dma_start(t["x1"][dst], bass.IndirectOffsetOnAxis(at[:, e:e + 1], 0), src[e % 2][:], None,
                                                compute_op=ALU.add).then_inc(y_out, 16)

                fetch(0)
                fetch(1)
                affinities(0)
                for e in range(NE):
                    if e + 2 < NE:
                        fetch(e + 2)
                    if e + 1 < NE:
                        affinities(e + 1)
                    scatter(e)
                pool.wait_ge(y_out, 32 * NE)

            @block.tensor
            def _(pe):
                def turn_in(e, i, u, g):
                    lo, hi = groups[g]
                    if g == 0:
                        pe.wait_ge(x_in[u], 32 * (i + 1))
                    wait(pe, tp_kept, 3 * e + g - 1)
                    bank = turn_bank(u, g)
                    for k in range(lo, hi):
                        o = (k - lo) * SLOTS
                        pe.transpose(bank[:, o:o + CAP_S], xs[u][:, k * P:(k + 1) * P], per.ident[:])
                        last = pe.transpose(bank[:, o + CAP_S:o + SLOTS], xp[u][:, k * P:(k + 1) * P], per.ident[0:CAP_P, 0:CAP_P])
                    last.then_inc(tp_full, 1)

                def up_part(e, i, u, between):
                    pe.wait_ge(wgu_in[u], 32 * (i + 1))
                    pe.wait_ge(h_ready, 3 * e + 3)
                    for j in range(KF):
                        wait(pe, hid_ready, KF * e + j - 1)
                        for m, w in enumerate((wg, wu)):
                            for k in range(KD):
                                last = pe.matmul(gu[j % 2][:, m * SLOTS:(m + 1) * SLOTS], w[u][:, k, j * P:(j + 1) * P],
                                                 h_t[u][:, k, :], start=(k == 0), stop=(k == KD - 1))
                        last.then_inc(gu_full, 1)
                        between(j)

                def down_part(e, i, u):
                    pe.wait_ge(wd_in[u], 16 * (i + 1))
                    pe.wait_ge(hid_ready, KF * e + KF)
                    for g, (lo, hi) in enumerate(groups):
                        wait(pe, dn_kept, 3 * e + g - 1)
                        for d in range(lo, hi):
                            for k in range(KF):
                                last = pe.matmul(down_bank(u, g)[:, (d - lo) * SLOTS:(d - lo + 1) * SLOTS], wd[u][:, k, d * P:(d + 1) * P],
                                                 hid[:, k, :], start=(k == 0), stop=(k == KF - 1))
                        last.then_inc(dn_full, 1)

                def turn_out(e, u, piece):
                    m, half = divmod(piece, 2)
                    rows, lo = ((CAP_S, 0), (CAP_P, CAP_S))[m]
                    if piece == 0:
                        pe.wait_ge(dn_kept, 3 * e + 3)
                    wait(pe, to_kept, 4 * e + piece - 1)
                    for j in range(4):
                        last = pe.transpose(to[half][0:rows, j * P:(j + 1) * P], y_t[:, 4 * half + j, lo:lo + rows], per.ident[:])
                    last.then_inc(to_full, 1)

                def expert(e, i, u):
                    def between(j):
                        if not (isinstance(e, int) and e == 0):
                            turn_out(e - 1, 1 - u, j)
                        if j and not (isinstance(e, int) and e == NE - 1):
                            turn_in(e + 1, i + u, 1 - u, j - 1)

                    up_part(e, i, u, between)
                    down_part(e, i, u)

                for g in range(3):
                    turn_in(0, 0, 0, g)
                expert(0, 0, 0)
                middle(pe, expert)
                expert(NE - 1, NE // 2 - 1, 1)
                for piece in range(4):
                    turn_out(NE - 1, 1, piece)

            @block.scalar
            def _(act):
                def silu(e, j):
                    act.wait_ge(gu_full, KF * e + j + 1)
                    wait(act, hid_ready, KF * e + j - 1)
                    act.activation(act_sb[j % 2][:], gu[j % 2][:, 0:SLOTS], ACT.Silu).then_inc(silu_ready, 1)

                def rows_out(e, u, piece):
                    m, half = divmod(piece, 2)
                    rows, dst, g = ((CAP_S, ys, g_s), (CAP_P, yp, g_p))[m]
                    if piece == 0:
                        wait(act, y_out, 32 * (e - 1))
                        act.wait_ge(g_ready, 2 * e + 2)
                    act.wait_ge(to_full, 4 * e + piece + 1)
                    act.activation(dst[u][:, half * BANK:(half + 1) * BANK], to[half][0:rows, :], ACT.Copy, scale=g[u][:]).then_inc(to_kept, 1)

                def expert(e, i, u):
                    for j in range(KF):
                        silu(e, j)
                        if not (isinstance(e, int) and e == 0):
                            rows_out(e - 1, 1 - u, j)

                expert(0, 0, 0)
                middle(act, expert)
                expert(NE - 1, NE // 2 - 1, 1)
                for piece in range(4):
                    rows_out(NE - 1, 1, piece)

            @block.vector
            def _(dve):
                for dst, src in ((scale, per.scale2[layer]), (shift, per.shift2[layer]), (gate, per.gate2[layer])):
                    for c, lo, hi in ((1, 0, CAP_S), (0, CAP_S, SLOTS)):
                        dve.tensor_copy(dst[:, :, lo:hi], src[:, c, :].unsqueeze(2).broadcast_to([P, KD, hi - lo])).then_inc(spread, 1)
                dve.wait_ge(spread, 6)

                def hidden(e, j):
                    dve.wait_ge(silu_ready, KF * e + j + 1)
                    dve.tensor_tensor(hid[:, j, :], act_sb[j % 2][:], gu[j % 2][:, SLOTS:2 * SLOTS], ALU.mult).then_inc(hid_ready, 1)

                def modulate(e, u, g):
                    lo, hi = groups[g]
                    dve.wait_ge(tp_full, 3 * e + g + 1)
                    dve.tensor_tensor(h_t[u][:, lo:hi, :], turn_bank(u, g)[:, 0:(hi - lo) * SLOTS].rearrange("p (k c) -> p k c", c=SLOTS),
                                      scale[:, lo:hi, :], ALU.mult).then_inc(tp_kept, 1)
                    dve.wait_ge(tp_kept, 3 * e + g + 1)
                    dve.tensor_tensor(h_t[u][:, lo:hi, :], h_t[u][:, lo:hi, :], shift[:, lo:hi, :], ALU.add).then_inc(h_ready, 1)

                def gated(e, u, g):
                    lo, hi = groups[g]
                    dve.wait_ge(dn_full, 3 * e + g + 1)
                    dve.tensor_tensor(y_t[:, lo:hi, :], down_bank(u, g)[:, 0:(hi - lo) * SLOTS].rearrange("p (k c) -> p k c", c=SLOTS),
                                      gate[:, lo:hi, :], ALU.mult).then_inc(dn_kept, 1)

                def expert(e, i, u):
                    for j in range(KF):
                        hidden(e, j)
                        if j and not (isinstance(e, int) and e == NE - 1):
                            modulate(e + 1, 1 - u, j - 1)
                    for g in range(3):
                        gated(e, u, g)

                for g in range(3):
                    modulate(0, 0, g)
                expert(0, 0, 0)
                middle(dve, expert)
                expert(NE - 1, NE // 2 - 1, 1)


def fourier(nc, t, per):
    PAIRS = 1 + ST // 2
    HP, HS = SEQ // 2, DEC // 2
    KP, KS = HP + 1, HS + 1
    CE = GROUPS * HG
    with Stage(nc, "fourier") as s:
        x_a, x_b = s.sb("x_a", [P, PAIRS, D]), s.sb("x_b", [P, PAIRS, D])
        w = s.sb("w", [P, GROUPS, 2, D])
        fold = s.sb("fold", [P, 2 * GROUPS * D])
        w_even = fold[:, 0:GROUPS * D].rearrange("p (g e) -> p g e", g=GROUPS)
        w_odd = fold[:, GROUPS * D:2 * GROUPS * D].rearrange("p (g e) -> p g e", g=GROUPS)
        p_t = fold[:, 0:GROUPS * (KP + KS)].rearrange("p (g k) -> p g k", g=GROUPS)
        q_t = fold[:, GROUPS * D:GROUPS * (D + HP + HS)].rearrange("p (g k) -> p g k", g=GROUPS)
        p_mid = s.sb("p_mid", [GROUPS, KP + KS])
        w_mid = s.sb("w_mid", [GROUPS, D])
        h_even, h_odd = s.sb("h_even", [P, PAIRS, CE + GROUPS]), s.sb("h_odd", [P, PAIRS, CE])
        edge = s.sb("edge", [2, 2, CE + GROUPS])
        scale, gate = s.sb("scale", [P, 2, D]), s.sb("gate", [P, 2, D])
        x_mid, gate_mid = s.sb("x_mid", [2, D]), s.sb("gate_mid", [2, D])
        work = s.sb("work", [P, 4, D])
        halves = s.sb("halves", [P, 2, D])
        total, diffs = halves[:, 0, :], (halves[:, 1, :], work[:, 1, :])
        norm_g, shift_rows = halves[:, 0, :], gate[0:2, :, :]
        ms, rt, eps = s.sb("ms", [P, PAIRS, 2]), s.sb("rt", [P, PAIRS, 2]), s.sb("eps", [P, 1])
        cos_s, sin_s = s.sb("cos_s", [P, ST // 2, KS]), s.sb("sin_s", [P, ST // 2, HS])
        cos_p, sin_p = s.sb("cos_p", [P, KP]), s.sb("sin_p", [P, HP])
        cos_c, sin_c = s.sb("cos_c", [P, HG]), s.sb("sin_c", [P, HG])
        alt_c, odd_c = s.sb("alt_c", [P, GROUPS, GROUPS]), s.sb("odd_c", [1, HG])
        edge_n = s.sb("edge_n", [2, KP + KS])
        partner = s.sb("partner", [P, PAIRS], U32)
        banks = s.ps("banks", 8)

        w_in, chan_in, tables_in, x_in, scale_in = s.sems("w_in", GROUPS), s.sem("chan_in"), s.sem("tables_in"), s.sems("x_in", PAIRS), s.sem("scale_in")
        shift_in, late_in, mid_in = s.sem("shift_in"), s.sem("late_in"), s.sem("mid_in")
        w_folded, ms_ready, roots_ready, far_ready = s.sem("w_folded"), s.sem("ms_ready"), s.sem("roots_ready"), s.sem("far_ready")
        scale_ready, even_ready, odd_ready = s.sem("scale_ready"), s.sem("even_ready"), s.sem("odd_ready")
        diff_ready, p_chain = s.sem("diff_ready"), s.sem("p_chain")
        full, kept = s.sem("full"), s.sem("kept")
        tile_full, odd_kept, tile_used = s.sem("tile_full"), s.sem("odd_kept"), s.sem("tile_used")
        partner_in, far_in = s.sem("partner_in"), s.sems("far_in", PAIRS)
        first_out, far_out = s.sem("first_out"), s.sem("far_out")
        y_ready, y_out, a_chain, chain = s.sem("y_ready"), s.sem("y_out"), s.sem("a_chain"), s.sem("chain")

        def bank(n):
            return banks[:, (n % 8) * BANK:(n % 8 + 1) * BANK]

        def near(x, q):
            return x[0][0:P, :] if q == 0 else x[1][(q - 1) * P:q * P, :]

        def columns(x):
            x = x.rearrange("p (g c) -> p g c", g=GROUPS)
            return x[:, :, 1:HG], x[:, :, GW - 1:HG:-1], x[:, :, 0:1], x[:, :, HG:HG + 1]

        def fold_even(eng, ch, dst, src):
            first, second, zero, mid = columns(src)
            main = dst[:, 0:CE].rearrange("p (g c) -> p g c", g=GROUPS)
            ch.add(eng.tensor_tensor(main[:, :, 1:HG], first, second, ALU.add))
            ch.add(eng.tensor_copy(main[:, :, 0:1], zero))
            ch.add(eng.tensor_copy(dst[:, CE:CE + GROUPS].unsqueeze(2), mid))

        def products():
            for half in range(2):
                e = slice(half * BANK, (half + 1) * BANK)
                for g in range(GROUPS):
                    yield [(w[:, g, 0, e], slice(0, BANK), [(cos_c[:], w_even[:, g, e]), (odd_c[:], w_odd[0:1, g, e])])]
                    yield [(w[:, g, 1, e], slice(0, BANK), [(sin_c[:], w_odd[:, g, e])])]
                yield [(w_mid[:, e], slice(0, BANK), [(alt_c[:, g, :], w_even[:, g, e]) for g in range(GROUPS)])]
            for g in range(GROUPS + 1):
                c = slice(g * HG, (g + 1) * HG if g < GROUPS else CE + GROUPS)
                done = [(p_t[:, g, 0:KP] if g < GROUPS else p_mid[:, 0:KP], slice(0, KP),
                         [(h_even[:, 0, c], cos_p[:]), (edge[:, 0, c], edge_n[:, 0:KP])])]
                if g < GROUPS:
                    done.append((q_t[:, g, 0:HP], slice(256, 256 + HP), [(h_odd[:, 0, c], sin_p[:])]))
                yield done
            for g in range(GROUPS + 1):
                c = slice(g * HG, (g + 1) * HG if g < GROUPS else CE + GROUPS)
                for lo, hi in ((0, KS // 2 + 1), (KS // 2 + 1, KS)):
                    yield [(p_t[:, g, KP + lo:KP + hi] if g < GROUPS else p_mid[:, KP + lo:KP + hi], slice(0, hi - lo),
                            [(h_even[:, 1 + j, c], cos_s[:, j, lo:hi]) for j in range(ST // 2)] + [(edge[:, 1, c], edge_n[:, KP + lo:KP + hi])])]
                if g < GROUPS:
                    yield [(q_t[:, g, HP:HP + HS], slice(0, HS), [(h_odd[:, 1 + j, c], sin_s[:, j, :]) for j in range(ST // 2)])]

        N_W, N_PROMPT = 2 * (2 * GROUPS + 1), GROUPS + 1
        N_PRODUCTS = N_W + N_PROMPT + 3 * GROUPS + 2
        OUT = [(0, slice(0, HP), slice(0, HP)), (1, slice(KP, KP + P), slice(HP, HP + P)), (None, slice(HP, KP + KS, KS), None)]
        OUT += [(1 + j, slice(KP + j * P, KP + (j + 1) * P), slice(HP + j * P, HP + (j + 1) * P)) for j in range(1, ST // 2)]

        with nc.Block() as block:

            @block.sync
            def _(sp):
                for g in range(GROUPS):
                    sp.dma_start(w[:, g, :, :], t["w_f_pairs"][g].rearrange("a p e -> p a e")).then_inc(w_in[g], 16)
                for dst, name in ((cos_c[:], "chan_cos"), (sin_c[:], "chan_sin"), (odd_c[:], "chan_odd"),
                                  (alt_c[:].rearrange("p g a -> p (g a)"), "chan_alt")):
                    sp.dma_start(dst, t[name]).then_inc(chan_in, 16)
                for q in range(PAIRS):
                    sp.dma_start(x_a[:, q, :], near(t["x2"], q)).then_inc(x_in[q], 16)
                for dst, name in ((cos_p[:], "pos_cos_p"), (sin_p[:], "pos_sin_p"), (edge_n[:], "pos_edge")):
                    sp.dma_start(dst, t[name]).then_inc(tables_in, 16)
                sp.dma_start(cos_s[:], t["pos_cos_s"].rearrange("(j p) k -> p j k", p=P)).then_inc(tables_in, 16)
                sp.dma_start(sin_s[:], t["pos_sin_s"].rearrange("(j p) k -> p j k", p=P)).then_inc(tables_in, 16)
                sp.wait_ge(scale_ready, 2)
                for c in range(2):
                    sp.dma_start(gate[:, c, :], t["mod_rows"][c, 2 * D:3 * D].partition_broadcast(P)).then_inc(late_in, 16)
                sp.dma_start(gate_mid[:], t["mod_rows"][:, 2 * D:3 * D]).then_inc(mid_in, 16)
                sp.dma_start(x_mid[0:1, :], t["x2"][0][SEQ // 2:SEQ // 2 + 1, :]).then_inc(mid_in, 16)
                sp.dma_start(x_mid[1:2, :], t["x2"][1][DEC // 2:DEC // 2 + 1, :]).then_inc(mid_in, 16)

                for n, (q, _, _) in enumerate(OUT):
                    sp.wait_ge(y_ready, n + 1)
                    if q is None:
                        sp.wait_ge(first_out, 32)
                        for c, mid in ((0, SEQ // 2), (1, DEC // 2)):
                            sp.dma_start(t["y"][c][mid:mid + 1, :], x_mid[c:c + 1, :]).then_inc(y_out, 16)
                    else:
                        sp.dma_start(near(t["y"], q), x_a[:, q, :]).then_inc(y_out, 16)
                sp.wait_ge(y_out, 16 * (PAIRS + 2))

            @block.gpsimd
            def _(pool):
                pool.dma_start(partner[:], t["partner"]).then_inc(partner_in, 16)
                pool.wait_ge(partner_in, 16)
                for q in range(PAIRS):
                    pool.indirect_dma_start(x_b[:, q, :], None, t["x2"][min(q, 1)], bass.IndirectOffsetOnAxis(partner[:, q:q + 1], 0)).then_inc(far_in[q], 16)
                pool.dma_start(norm_g, t["norm1_l1"].partition_broadcast(P)).then_inc(scale_in, 16)
                for c in range(2):
                    pool.dma_start(scale[:, c, :], t["mod_rows"][c, D:2 * D].partition_broadcast(P)).then_inc(scale_in, 16)
                    pool.dma_start(shift_rows[:, c, :], t["mod_rows"][c, 0:D].partition_broadcast(2)).then_inc(shift_in, 16)
                ch = Chain(pool, p_chain)
                pool.wait_ge(scale_ready, 2)
                for q in range(PAIRS):
                    c, diff = min(q, 1), diffs[q % 2]
                    pool.wait_ge(diff_ready, q + 1)
                    ch.link(pool.tensor_tensor(diff, diff, scale[:, c, :], ALU.mult))
                    if q < 2:
                        fold_even(pool, ch, edge[0:1, c, :], diff[0:1, :])
                        ch.settle()
                    first, second, _, _ = columns(diff)
                    pool.tensor_tensor(h_odd[:, q, :].rearrange("p (g c) -> p g c", g=GROUPS)[:, :, 1:HG], first, second, ALU.subtract).then_inc(odd_ready, 1)
                    pool.wait_ge(odd_ready, q + 1)

                for n, (q, _, _) in enumerate(OUT):
                    if q is not None:
                        pool.wait_ge(y_ready, n + 1)
                        pool.indirect_dma_start(t["y"][min(q, 1)], bass.IndirectOffsetOnAxis(partner[:, q:q + 1], 0),
                                                x_b[:, q, :], None).then_inc(first_out if q < 2 else far_out, 16)
                pool.wait_ge(far_out, 16 * (PAIRS - 2))

            @block.tensor
            def _(pe):
                pe.wait_ge(chan_in, 64)
                for n, results in enumerate(products()):
                    if n < 2 * GROUPS and n % 2 == 0:
                        pe.wait_ge(w_folded, n + 2)
                    if n == N_W:
                        pe.wait_ge(tables_in, 80)
                        pe.wait_ge(even_ready, 1)
                        pe.wait_ge(odd_ready, 1)
                    if n == N_W + N_PROMPT:
                        pe.wait_ge(even_ready, PAIRS)
                        pe.wait_ge(odd_ready, PAIRS)
                    if n >= 8:
                        pe.wait_ge(kept, n - 7)
                    for dst, cols, terms in results:
                        for m, (stationary, moving) in enumerate(terms):
                            last = pe.matmul(bank(n)[0:dst.shape[0], cols], stationary, moving, start=(m == 0), stop=(m == len(terms) - 1))
                    last.then_inc(full, 1)
                pe.wait_ge(kept, N_PRODUCTS)
                for n, (q, ks, qs) in enumerate(OUT):
                    if n >= 2:
                        pe.wait_ge(tile_used, n - 1)
                    m = 2 if q is None else P
                    for half in range(2):
                        e = slice(half * BANK, (half + 1) * BANK)
                        even = bank(4 * n + half)[0:m, :]
                        for g in range(GROUPS):
                            pe.matmul(even, p_t[:, g, ks], w[:, g, 0, e], start=(g == 0), stop=False)
                        last = pe.matmul(even, p_mid[:, ks], w_mid[:, e], start=False, stop=True)
                        if q is not None:
                            for g in range(GROUPS):
                                last = pe.matmul(bank(4 * n + 2 + half), q_t[:, g, qs], w[:, g, 1, e], start=(g == 0), stop=(g == GROUPS - 1))
                    last.then_inc(tile_full, 1)

            @block.scalar
            def _(act):
                ch = Chain(act, a_chain)
                act.wait_ge(chain, 1)

                def move(n, results):
                    act.wait_ge(full, n + 1)
                    for m, (dst, cols, _) in enumerate(results):
                        done = act.activation(dst, bank(n)[0:dst.shape[0], cols], ACT.Copy)
                        if m < len(results) - 1:
                            ch.link(done)
                    done.then_inc(kept, 1)

                results = enumerate(products())

                def squares(q):
                    act.wait_ge(x_in[q], 16)
                    act.wait_ge(far_in[q], 16)
                    for side, x in enumerate((x_a, x_b)):
                        ch.link(act.activation(work[:, 0, :], x[:, q, :], ACT.Square, accum_out=ms[:, q, side:side + 1]))
                    act.activation(rt[:, q, :], ms[:, q, :], ACT.Sqrt, bias=eps[:], scale=1.0 / D).then_inc(ms_ready, 1)

                for _ in range(6):
                    move(*next(results))
                squares(0)
                for q in range(PAIRS):
                    if q + 1 < PAIRS:
                        squares(q + 1)
                    act.wait_ge(roots_ready, q + 1)
                    if q >= 2:
                        act.wait_ge(even_ready, q - 1)
                    act.activation(work[:, 2 + q % 2, :], x_b[:, q, :], ACT.Copy, scale=rt[:, q, 1:2]).then_inc(far_ready, 1)
                    for _ in range(2):
                        move(*next(results))
                for n, result in results:
                    move(n, result)
                for n, (q, _, _) in enumerate(OUT):
                    if q is not None:
                        act.wait_ge(tile_full, n + 1)
                        if n >= 2:
                            act.wait_ge(tile_used, n - 1)
                        act.activation(work[:, 2 + n % 2, :], banks[:, (4 * n % 8 + 2) * BANK:(4 * n % 8 + 4) * BANK], ACT.Copy).then_inc(odd_kept, 1)

            @block.vector
            def _(dve):
                ch = Chain(dve, chain)

                def invert(q):
                    dve.wait_ge(ms_ready, q + 1)
                    dve.reciprocal(rt[:, q, :], rt[:, q, :]).then_inc(roots_ready, 1)
                    dve.wait_ge(roots_ready, q + 1)

                ch.link(dve.memset(eps[:], EPS))
                ch.add(dve.memset(h_odd[:].rearrange("p q (g c) -> p q g c", g=GROUPS)[:, :, :, 0:1], 0.0))
                for g in range(GROUPS):
                    dve.wait_ge(w_in[g], 16)
                    dve.tensor_tensor(w_even[:, g, :], w[:, g, 0, :], w[:, g, 1, :], ALU.add).then_inc(w_folded, 1)
                    dve.tensor_tensor(w_odd[:, g, :], w[:, g, 0, :], w[:, g, 1, :], ALU.subtract).then_inc(w_folded, 1)
                dve.wait_ge(shift_in, 32)
                for c in range(2):
                    fold_even(dve, ch, edge[:, c, :], shift_rows[:, c, :])
                ch.settle()
                dve.wait_ge(scale_in, 48)
                for c in range(2):
                    dve.scalar_tensor_tensor(out=scale[:, c, :], in0=scale[:, c, :], scalar=1.0, in1=norm_g,
                                             op0=ALU.add, op1=ALU.mult).then_inc(scale_ready, 1)
                dve.wait_ge(scale_ready, 2)

                for q in range(PAIRS):
                    if q == 0:
                        invert(0)
                    dve.wait_ge(far_ready, q + 1)
                    if q + 1 < PAIRS:
                        invert(q + 1)
                    ch.link(dve.scalar_tensor_tensor(out=total, in0=x_a[:, q, :], scalar=rt[:, q, 0:1], in1=work[:, 2 + q % 2, :],
                                                     op0=ALU.mult, op1=ALU.add))
                    if q >= 2:
                        dve.wait_ge(odd_ready, q - 1)
                    dve.scalar_tensor_tensor(out=diffs[q % 2], in0=x_a[:, q, :], scalar=rt[:, q, 0:1], in1=work[:, 2 + q % 2, :],
                                             op0=ALU.mult, op1=ALU.subtract).then_inc(diff_ready, 1)
                    ch.link(dve.tensor_tensor(total, total, scale[:, min(q, 1), :], ALU.mult))
                    first, second, zero, mid = columns(total)
                    main = h_even[:, q, 0:CE].rearrange("p (g c) -> p g c", g=GROUPS)
                    ch.add(dve.tensor_copy(main[:, :, 0:1], zero))
                    ch.add(dve.tensor_copy(h_even[:, q, CE:CE + GROUPS].unsqueeze(2), mid))
                    ch.settle()
                    dve.tensor_tensor(main[:, :, 1:HG], first, second, ALU.add).then_inc(even_ready, 1)
                    dve.wait_ge(even_ready, q + 1)
                    dve.wait_ge(diff_ready, q + 1)

                dve.wait_ge(late_in, 32)
                dve.wait_ge(mid_in, 48)
                for n, (q, _, _) in enumerate(OUT):
                    dve.wait_ge(tile_full, n + 1)
                    if n:
                        dve.wait_ge(y_ready, n)
                    even = banks[:, (4 * n % 8) * BANK:(4 * n % 8 + 2) * BANK]
                    odd = work[:, 2 + n % 2, :]
                    if q is None:
                        dve.tensor_tensor(work[0:2, 0, :], even[0:2, :], gate_mid[:], ALU.mult).then_inc(tile_used, 1)
                        dve.wait_ge(tile_used, n + 1)
                        dve.tensor_tensor(x_mid[:], x_mid[:], work[0:2, 0, :], ALU.add).then_inc(y_ready, 1)
                        continue
                    dve.wait_ge(odd_kept, n + 1 if n < 2 else n)
                    ch.link(dve.tensor_tensor(work[:, 0, :], even, odd, ALU.subtract))
                    dve.tensor_tensor(work[:, 1, :], even, odd, ALU.add).then_inc(tile_used, 1)
                    dve.wait_ge(tile_used, n + 1)
                    for m in range(2):
                        ch.add(dve.tensor_tensor(work[:, m, :], work[:, m, :], gate[:, min(q, 1), :], ALU.mult))
                    ch.settle()
                    ch.link(dve.tensor_tensor(x_a[:, q, :], x_a[:, q, :], work[:, 0, :], ALU.add))
                    dve.tensor_tensor(x_b[:, q, :], x_b[:, q, :], work[:, 1, :], ALU.add).then_inc(y_ready, 1)


def _trunk(nc, t):
    with Stage(nc, "all") as s:
        per = Lasting(s)
        ident_in = s.sem("ident_in")
        with nc.Block() as block:

            @block.sync
            def _(sp):
                sp.dma_start(per.ident[:], t["ident"]).then_inc(ident_in, 16)
                sp.wait_ge(ident_in, 16)

        layer_0 = dict(t, mod_rows=t["mod_rows_l0"], x1=(t["x_prompt_1"], t["x_sample_1"]))
        layer_1 = dict(t, mod_rows=t["mod_rows_l1"], x2=layer_0["x1"], x1=t["y"])
        with Stage(nc, "w_in") as w:
            w_in = w.sb("w_in", [P, KD, IN0]), w.sem("w_lat_in"), w.sem("w_conv_in")
            first_modulation(nc, layer_0, per, *w_in)
            projections(nc, layer_0, per, *w_in)
        attention(nc, layer_0, per, "attn_p", 0, PT, 0, PT, rest_of_modulation=True)
        attention(nc, layer_0, per, "attn_s", PT, ST, PT, ST + CT)
        channel_mixer(nc, dict(layer_0, mod_rows=t["mod_rows_l1"]), per, 0)
        fourier(nc, layer_1, per)
        channel_mixer(nc, layer_1, per, 1)


def channel_mixer(nc, t, per, layer):
    with Stage(nc, f"weights{layer}") as s:
        weights = Weights(s, t, layer)
        route(nc, t, per, layer, weights)
        experts(nc, t, per, layer, weights)


def _tables():
    inv = (np.float32(THETA) ** (-np.arange(0, ROPE // 2, 2, dtype=np.float32) / np.float32(ROPE // 2))).astype(np.float32)
    token = np.arange(DEC)
    angle = np.concatenate([(token // GRID_W).astype(np.float32)[:, None] * inv,
                            (token % GRID_W).astype(np.float32)[:, None] * inv], axis=1)
    rope = np.zeros((KEYT * P, ROPE), np.float32)
    rope[:, 0:ROPE // 2] = 1.0
    rope[SEQ:TOK, 0:ROPE // 2] = np.cos(angle)
    rope[SEQ:TOK, ROPE // 2:] = np.sin(angle)

    def dft(n, wave, rows, cols):
        return wave(2 * np.pi * (np.outer(np.arange(rows), np.arange(cols)) % n) / n) / np.sqrt(n)

    def cos_table(n, cols):
        table = dft(n, np.cos, n // 2, cols)
        table[0, 1::2] = 0.0
        return table

    def edge_table(n):
        table = np.zeros((2, n // 2 + 1))
        table[0, 1::2] = n ** -0.5
        table[1, 0] = n ** 0.5
        return table

    alt = np.zeros((HG, GROUPS, GROUPS))
    for g in range(GROUPS):
        alt[:, g, g] = (-1.0) ** np.arange(HG) / np.sqrt(GW)
    pick = np.zeros((P, 2))
    for c in range(2):
        pick[c::P // 4, c] = 1.0
    tables = dict(ident=np.eye(P), rope=rope, pick=pick,
                  pos_cos_p=cos_table(SEQ, SEQ // 2 + 1), pos_sin_p=dft(SEQ, np.sin, SEQ // 2, SEQ // 2),
                  pos_cos_s=cos_table(DEC, DEC // 2 + 1), pos_sin_s=dft(DEC, np.sin, DEC // 2, DEC // 2),
                  pos_edge=np.concatenate([edge_table(SEQ), edge_table(DEC)], axis=1),
                  chan_cos=cos_table(GW, HG), chan_sin=dft(GW, np.sin, HG, HG),
                  chan_odd=edge_table(GW)[0:1, 0:HG], chan_alt=alt.reshape(HG, GROUPS * GROUPS))
    tables = {name: np.ascontiguousarray(a, dtype=np.float32) for name, a in tables.items()}
    slot = np.arange(P)[:, None]
    partner = np.concatenate([SEQ - slot] + [DEC - j * P - slot for j in range(ST // 2)], axis=1)
    partner[0, 0:2] = SEQ // 2, DEC // 2
    tables["partner"] = partner.astype(np.uint32)
    return tables


_PLAIN = ["norm1_l0", "norm2_l0", "w_mod_l0", "b_mod_l0", "w_in_l0", "q_a_norm_l0", "w_q_up_l0", "q_norm_l0",
          "kv_a_norm_l0", "w_kv_up_l0", "k_norm_l0", "conv_w_l0", "w_o_l0", "w_router_l0", "w_gate_l0", "w_up_l0",
          "w_down_l0", "norm1_l1", "norm2_l1", "w_mod_l1", "b_mod_l1", "w_router_l1", "w_gate_l1", "w_up_l1", "w_down_l1"]
_SCRATCH = dict(mod_rows_l0=[2, 3 * D], mod_rows_l1=[2, 3 * D], state=[TOK, KVL + ROPE], qt=[NT * QK, HEADS * P], kt=[KEYT * QK, HEADS * P],
                v=[KEYT * P, HEADS * VH], conv=[CJ, P, TOK], attn=[TOK, HEADS * VH],
                x_prompt_1=[SEQ, D], x_sample_1=[DEC, D], xh_prompt=[SEQ, D], xh_sample=[DEC, D])
_OUTPUTS = dict(y_prompt=[SEQ, D], y_sample=[DEC, D], new_c_kv=[SEQ, KVL], new_k_rope=[SEQ, ROPE])


def _layout(inputs):
    w_f = inputs["w_f_l1"].reshape(GROUPS, GW, D)
    partner = np.concatenate([[HG], np.arange(GW - 1, HG, -1)])
    arrays = {name: inputs[name] for name in _PLAIN}
    arrays["x"] = np.concatenate([inputs["x_prompt"][0], inputs["x_sample"][0]])
    arrays["cond"] = np.concatenate([inputs["c_ctx"].reshape(KD, P), inputs["c"].reshape(KD, P)])
    arrays["cache_c_kv_l0"] = inputs["cache_c_kv_l0"][0]
    arrays["cache_k_rope_l0"] = inputs["cache_k_rope_l0"][0]
    arrays["w_f_pairs"] = np.stack([w_f[:, 0:HG], w_f[:, partner]], axis=1)
    return arrays


def kernel(**inputs):
    import concourse.bacc as bacc
    from concourse.bass_utils import run_bass_kernel_spmd

    inputs = {name: np.asarray(a) for name, a in inputs.items()}
    arrays = {name: np.ascontiguousarray(a) for name, a in {**_layout(inputs), **_tables()}.items()}
    nc = bacc.Bacc("TRN2", target_bir_lowering=False, num_devices=1)
    t = {name: nc.dram_tensor(name, list(a.shape), mybir.dt.from_np(a.dtype), kind="ExternalInput").ap() for name, a in arrays.items()}
    t.update({name: nc.dram_tensor(name, shape, F32, kind="Internal").ap() for name, shape in _SCRATCH.items()})
    t.update({name: nc.dram_tensor(name, shape, F32, kind="ExternalOutput").ap() for name, shape in _OUTPUTS.items()})
    t["xh"] = (t["xh_prompt"], t["xh_sample"])
    t["y"] = (t["y_prompt"], t["y_sample"])
    _trunk(nc, t)
    out = run_bass_kernel_spmd(nc, [arrays], core_ids=[0]).results[0]
    return (out["y_prompt"][None], out["y_sample"][None], out["new_c_kv"][None], out["new_k_rope"][None])
```
